# Optimizing a Trainium2 kernel written in Bass

```python
import math
import jax
import jax.numpy as jnp
from jax import lax
import numpy as np

D_MODEL = 1024
BATCH = 1
SEQ = 128
DEPTH = 2
DEC_BATCH = 1
DEC_SEQ = 512
PAST_LEN = 128

GRID_W = 64
EPS = 1e-6
ROPE_BASE = 10000.0
Q_BLOCK = 128
N_BRANCH = 4
BRANCH_W = D_MODEL // 4
NA_HEADS = 4
NA_HEAD_DIM = 64
NA_KH = 8
NA_KW = 16
MLA_HEADS = 4
MLA_NOPE = 64
MLA_ROPE = 32
MLA_V = 64
MLA_Q_RANK = 384
MLA_KV_RANK = 256
DF_HEADS = 4
DF_HD = 32
DF_V = 64
SSM_HEADS = 4
SSM_P = 64
SSM_GROUPS = 2
SSM_N = 64
SSM_CONV = 3
SSM_CHUNK = 128
SSM_CONV_DIM = SSM_HEADS * SSM_P + 2 * SSM_GROUPS * SSM_N
N_EXPERTS = 16
EXPERT_FF = 1024
CAP_FACTOR = 2
IN_WIDTHS = (NA_HEADS * NA_HEAD_DIM, NA_HEADS * NA_HEAD_DIM, NA_HEADS * NA_HEAD_DIM,
             MLA_Q_RANK, MLA_KV_RANK, MLA_ROPE,
             DF_HEADS * 2 * DF_HD, DF_HEADS * 2 * DF_HD, DF_HEADS * DF_V,
             SSM_HEADS * SSM_P, SSM_HEADS * SSM_P, SSM_GROUPS * SSM_N, SSM_GROUPS * SSM_N, 2 * SSM_HEADS,
             N_BRANCH * D_MODEL)
IN_WIDTH = sum(IN_WIDTHS)

kernel_name = 'hybrid_diffusion_prefix_trunk_step'

def rmsnorm(x, g):
    xf = x.astype(jnp.float32)
    y = xf * lax.rsqrt(jnp.mean(xf * xf, axis=-1, keepdims=True) + EPS)
    return (y * g.astype(jnp.float32)).astype(x.dtype)

def axial_rope(x):
    L, d = x.shape[1], x.shape[-1]
    quarter = d // 4
    t = jnp.arange(L)
    inv = ROPE_BASE ** (-jnp.arange(quarter, dtype=jnp.float32) / quarter)
    rows = (t // GRID_W).astype(jnp.float32)[:, None]
    cols = (t % GRID_W).astype(jnp.float32)[:, None]
    ang = jnp.concatenate([rows * inv, cols * inv], axis=-1)
    ang = ang.reshape((1, L) + (1,) * (x.ndim - 3) + (d // 2,))
    cos = jnp.cos(ang).astype(x.dtype)
    sin = jnp.sin(ang).astype(x.dtype)
    xr, xi = x[..., 0::2], x[..., 1::2]
    return jnp.stack([xr * cos - xi * sin, xr * sin + xi * cos], axis=-1).reshape(x.shape)

def sweep_query_blocks(fn, *qs):
    b, L = qs[0].shape[:2]
    nb = L // Q_BLOCK
    blocks = tuple(q.reshape((b, nb, Q_BLOCK) + q.shape[2:]).swapaxes(0, 1) for q in qs)
    out = lax.map(lambda blk: fn(*blk), blocks).swapaxes(0, 1)
    return out.reshape((b, L) + out.shape[3:])

def softmax_attention(q, k, v):
    scale = q.shape[-1] ** -0.5

    def block(qb):
        s = jnp.einsum('bqhd,bkhd->bhqk', qb, k).astype(jnp.float32) * scale
        p = jax.nn.softmax(s, axis=-1).astype(v.dtype)
        return jnp.einsum('bhqk,bkhd->bqhd', p, v)

    return sweep_query_blocks(block, q)

def mla_attention(q_nope, q_rope, k_nope, k_rope, v):
    scale = (MLA_NOPE + MLA_ROPE) ** -0.5

    def block(qn, qr):
        s = jnp.einsum('bqhd,bkhd->bhqk', qn, k_nope) + jnp.einsum('bqhr,bkr->bhqk', qr, k_rope)
        p = jax.nn.softmax(s.astype(jnp.float32) * scale, axis=-1).astype(v.dtype)
        return jnp.einsum('bhqk,bkhd->bqhd', p, v)

    return sweep_query_blocks(block, q_nope, q_rope)

def diff_attention(q, k, v, lam):
    scale = DF_HD ** -0.5

    def block(qb):
        s = jnp.einsum('bqhcd,bkhcd->bchqk', qb, k).astype(jnp.float32) * scale
        p = jax.nn.softmax(s, axis=-1)
        w = (p[:, 0] - lam * p[:, 1]).astype(v.dtype)
        return jnp.einsum('bhqk,bkhd->bqhd', w, v)

    return sweep_query_blocks(block, q)

def neighborhood_attention(q, k, v, k_ctx, v_ctx, rel_bias):
    b, L, H, Dh = q.shape
    rows = L // GRID_W
    kh = min(NA_KH, rows)
    ncb = GRID_W // NA_KW
    band_w = 2 * NA_KW
    r = np.arange(rows)
    row_start = np.clip(r - kh // 2, 0, rows - kh)
    key_rows = row_start[:, None] + np.arange(kh)
    band_start = np.clip(np.arange(ncb) * NA_KW - NA_KW // 2, 0, GRID_W - band_w)
    key_cols = band_start[:, None] + np.arange(band_w)
    nk = kh * band_w
    key_idx = (key_rows[:, None, :, None] * GRID_W + key_cols[None, :, None, :]).reshape(rows, ncb, nk)
    q_cols = np.arange(ncb)[:, None] * NA_KW + np.arange(NA_KW)
    col_start = np.clip(q_cols - NA_KW // 2, 0, GRID_W - NA_KW)
    kc = key_cols[:, None, :]
    in_win = (kc >= col_start[..., None]) & (kc < col_start[..., None] + NA_KW)
    row_rel = (key_rows - r[:, None] + NA_KH - 1)[:, None, None, :, None]
    col_rel = np.clip(kc - q_cols[:, :, None] + NA_KW - 1, 0, 2 * NA_KW - 2)[None, :, :, None, :]
    bias = rel_bias[:, row_rel, col_rel].astype(jnp.float32)
    bias = jnp.where(in_win[None, None, :, :, None, :], bias, -1e30)
    bias = bias.reshape(H, rows, ncb, NA_KW, nk).transpose(1, 2, 0, 3, 4)
    qb = q.reshape(b, rows, ncb, NA_KW, H, Dh)
    kb = k[:, key_idx]
    vb = v[:, key_idx]
    scale = Dh ** -0.5
    s_loc = jnp.einsum('brjqhd,brjkhd->brjhqk', qb, kb).astype(jnp.float32) * scale + bias
    s_ctx = jnp.einsum('brjqhd,bkhd->brjhqk', qb, k_ctx).astype(jnp.float32) * scale
    p = jax.nn.softmax(jnp.concatenate([s_loc, s_ctx], axis=-1), axis=-1).astype(v.dtype)
    o = (jnp.einsum('brjhqk,brjkhd->brjqhd', p[..., :nk], vb)
         + jnp.einsum('brjhqk,bkhd->brjqhd', p[..., nk:], v_ctx))
    return o.reshape(b, L, H * Dh)

def depthwise_conv(x, w, bias):
    pad = SSM_CONV // 2
    y = lax.conv_general_dilated(x, w[:, None, :], window_strides=(1,), padding=[(pad, pad)],
                                 dimension_numbers=('NWC', 'WIO', 'NWC'), feature_group_count=x.shape[-1])
    return y + bias

def ssd_chunked(x, dt, A, B, C, h0):
    b, L, H, P = x.shape
    G, N = B.shape[2], B.shape[3]
    nc = L // SSM_CHUNK
    f32 = jnp.float32
    xc = x.astype(f32).reshape(b, nc, SSM_CHUNK, H, P)
    Bc = jnp.repeat(B.astype(f32), H // G, axis=2).reshape(b, nc, SSM_CHUNK, H, N)
    Cc = jnp.repeat(C.astype(f32), H // G, axis=2).reshape(b, nc, SSM_CHUNK, H, N)
    dtc = dt.reshape(b, nc, SSM_CHUNK, H)
    xdt = xc * dtc[..., None]
    a_cum = jnp.cumsum(jnp.moveaxis(dtc * A, 3, 1), axis=-1)
    causal = np.tril(np.ones((SSM_CHUNK, SSM_CHUNK), dtype=bool))
    seg = a_cum[..., :, None] - a_cum[..., None, :]
    decay = jnp.where(causal, jnp.exp(jnp.where(causal, seg, 0.0)), 0.0)
    scores = jnp.einsum('bclhn,bcshn->bhcls', Cc, Bc) * decay
    y_diag = jnp.einsum('bhcls,bcshp->bclhp', scores, xdt)
    decay_to_end = jnp.exp(a_cum[..., -1:] - a_cum)
    chunk_states = jnp.einsum('bclhn,bhcl,bclhp->bchpn', Bc, decay_to_end, xdt)
    chunk_decay = jnp.exp(a_cum[..., -1])

    def carry_state(h, inp):
        s, d = inp
        return h * d[..., None, None] + s, h

    h_final, h_start = lax.scan(carry_state, h0.astype(f32),
                                (jnp.moveaxis(chunk_states, 1, 0), jnp.moveaxis(chunk_decay, 2, 0)))
    h_start = jnp.moveaxis(h_start, 0, 1)
    y_off = jnp.einsum('bclhn,bchpn,bhcl->bclhp', Cc, h_start, jnp.exp(a_cum))
    y = (y_diag + y_off).reshape(b, L, H, P).astype(x.dtype)
    return y, h_final.astype(x.dtype)

def ssd_mixer(s_x, s_z, s_b, s_c, s_dt, h0, lp):
    b, L, _ = s_x.shape
    xbc = jax.nn.silu(depthwise_conv(jnp.concatenate([s_x, s_b, s_c], axis=-1), lp['ssm_conv_w'], lp['ssm_conv_b']))
    xs, bm, cm = jnp.split(xbc, [SSM_HEADS * SSM_P, SSM_HEADS * SSM_P + SSM_GROUPS * SSM_N], axis=-1)
    x4 = xs.reshape(b, L, SSM_HEADS, SSM_P)
    b4 = bm.reshape(b, L, SSM_GROUPS, SSM_N)
    c4 = cm.reshape(b, L, SSM_GROUPS, SSM_N)
    dt = jax.nn.softplus(s_dt.astype(jnp.float32).reshape(b, L, 2, SSM_HEADS) + lp['ssm_dt_bias'].astype(jnp.float32))
    A = -jnp.exp(lp['ssm_a_log'].astype(jnp.float32))

    def rev(a):
        return jnp.flip(a, axis=1)

    y_f, h_f = ssd_chunked(x4, dt[:, :, 0], A[0], b4, c4, h0[:, 0])
    y_b, h_b = ssd_chunked(rev(x4), rev(dt[:, :, 1]), A[1], rev(b4), rev(c4), h0[:, 1])
    y = y_f + rev(y_b) + lp['ssm_d'][:, None] * x4
    y = rmsnorm(y.reshape(b, L, SSM_HEADS * SSM_P) * jax.nn.silu(s_z), lp['ssm_norm'])
    return y, jnp.stack([h_f, h_b], axis=1)

def mixer_sublayer(h, lp, layer_idx, ctx):
    b, L, _ = h.shape
    latent = ctx is not None
    offsets = np.cumsum(IN_WIDTHS)[:-1].tolist()
    (na_q, na_k, na_v, mla_cq, mla_ckv, mla_kr, df_q, df_k, df_v,
     s_x, s_z, s_b, s_c, s_dt, gate_logits) = jnp.split(h @ lp['w_in'], offsets, axis=-1)

    na_q = na_q.reshape(b, L, NA_HEADS, NA_HEAD_DIM)
    na_k = na_k.reshape(b, L, NA_HEADS, NA_HEAD_DIM)
    na_v = na_v.reshape(b, L, NA_HEADS, NA_HEAD_DIM)
    if latent:
        na_out = neighborhood_attention(na_q, na_k, na_v, ctx['na_k'], ctx['na_v'], lp['na_rel_bias'])
    else:
        na_out = softmax_attention(na_q, na_k, na_v).reshape(b, L, NA_HEADS * NA_HEAD_DIM)

    q = (rmsnorm(mla_cq, lp['mla_q_norm']) @ lp['mla_w_uq']).reshape(b, L, MLA_HEADS, MLA_NOPE + MLA_ROPE)
    q_nope, q_rope = q[..., :MLA_NOPE], q[..., MLA_NOPE:]
    c_kv = rmsnorm(mla_ckv, lp['mla_kv_norm'])
    k_rope = mla_kr
    if latent:
        q_rope = axial_rope(q_rope)
        ckv_all = jnp.concatenate([c_kv, ctx['mla_ckv']], axis=1)
        krope_all = jnp.concatenate([axial_rope(k_rope), ctx['mla_krope']], axis=1)
    else:
        ckv_all, krope_all = c_kv, k_rope
    kv = (ckv_all @ lp['mla_w_ukv']).reshape(b, ckv_all.shape[1], MLA_HEADS, MLA_NOPE + MLA_V)
    mla_out = mla_attention(q_nope, q_rope, kv[..., :MLA_NOPE], krope_all, kv[..., MLA_NOPE:])
    mla_out = mla_out.reshape(b, L, MLA_HEADS * MLA_V)

    dq = df_q.reshape(b, L, DF_HEADS, 2, DF_HD)
    dk = df_k.reshape(b, L, DF_HEADS, 2, DF_HD)
    dv = df_v.reshape(b, L, DF_HEADS, DF_V)
    if latent:
        dq = axial_rope(dq)
        dk_all = jnp.concatenate([axial_rope(dk), ctx['df_k']], axis=1)
        dv_all = jnp.concatenate([dv, ctx['df_v']], axis=1)
    else:
        dk_all, dv_all = dk, dv
    lam_init = 0.8 - 0.6 * math.exp(-0.3 * layer_idx)
    lv = lp['df_lambda'].astype(jnp.float32)
    lam = jnp.exp(jnp.sum(lv[0] * lv[1])) - jnp.exp(jnp.sum(lv[2] * lv[3])) + lam_init
    df_o = diff_attention(dq, dk_all, dv_all, lam)
    df_out = (rmsnorm(df_o, lp['df_subln']) * (1.0 - lam_init)).reshape(b, L, DF_HEADS * DF_V)

    h0 = ctx['ssm'] if latent else jnp.zeros((b, 2, SSM_HEADS, SSM_P, SSM_N), h.dtype)
    ssm_out, ssm_state = ssd_mixer(s_x, s_z, s_b, s_c, s_dt, h0, lp)

    gates = jax.nn.sigmoid(gate_logits.astype(jnp.float32)).astype(h.dtype).reshape(b, L, N_BRANCH, D_MODEL)
    br = jnp.stack([na_out, mla_out, df_out, ssm_out], axis=2)
    proj = jnp.einsum('blnw,nwd->blnd', br, lp['w_branch'])
    out = jnp.sum(gates * proj, axis=2) @ lp['w_out']
    new_ctx = None if latent else {'na_k': na_k, 'na_v': na_v, 'mla_ckv': c_kv, 'mla_krope': k_rope,
                                   'df_k': dk, 'df_v': dv, 'ssm': ssm_state}
    return out, new_ctx

def expert_choice_ffn(h, router_w, w_gate, w_up, w_down):
    b, L, d = h.shape
    n = b * L
    cap = (CAP_FACTOR * n) // N_EXPERTS
    tok = h.reshape(n, d)
    aff = jax.nn.softmax((tok @ router_w).astype(jnp.float32), axis=-1)
    top_aff, top_idx = lax.top_k(aff.T, cap)
    xe = tok[top_idx]
    hid = jax.nn.silu(jnp.einsum('ecd,edf->ecf', xe, w_gate)) * jnp.einsum('ecd,edf->ecf', xe, w_up)
    ye = jnp.einsum('ecf,efd->ecd', hid, w_down) * top_aff[..., None].astype(h.dtype)
    out = jnp.zeros_like(tok).at[top_idx.reshape(-1)].add(ye.reshape(-1, d))
    return out.reshape(b, L, d)

def trunk_layer(x, c_vec, lp, layer_idx, ctx):
    m = jax.nn.silu(c_vec) @ lp['mod_w'] + lp['mod_b']
    sh1, sc1, g1, sh2, sc2, g2 = [t[:, None, :] for t in jnp.split(m, 6, axis=-1)]
    h = rmsnorm(x, lp['norm1']) * (1 + sc1) + sh1
    mix, new_ctx = mixer_sublayer(h, lp, layer_idx, ctx)
    x = x + g1 * mix
    h = rmsnorm(x, lp['norm2']) * (1 + sc2) + sh2
    x = x + g2 * expert_choice_ffn(h, lp['router_w'], lp['exp_w_gate'], lp['exp_w_up'], lp['exp_w_down'])
    return x, new_ctx

def setup_inputs(seed: int = 0) -> dict:
    key = jax.random.key(seed)
    ks = jax.random.split(key, 40)
    cnt = [0]
    f32 = jnp.float32

    def nxt():
        cnt[0] += 1
        return ks[cnt[0] - 1]

    def nrm(shape, scale):
        return jax.random.normal(nxt(), shape, f32) * scale

    def gain(shape):
        return 1.0 + nrm(shape, 0.02)

    D = D_MODEL
    x_prompt = nrm((BATCH, SEQ, D), 1.0)
    x_sample = nrm((DEC_BATCH, DEC_SEQ, D), 1.0)
    cache_na_k = nrm((DEC_BATCH, DEPTH, PAST_LEN, NA_HEADS, NA_HEAD_DIM), 1.0)
    cache_na_v = nrm((DEC_BATCH, DEPTH, PAST_LEN, NA_HEADS, NA_HEAD_DIM), 1.0)
    cache_mla_ckv = nrm((DEC_BATCH, DEPTH, PAST_LEN, MLA_KV_RANK), 1.0)
    cache_mla_krope = nrm((DEC_BATCH, DEPTH, PAST_LEN, MLA_ROPE), 1.0)
    cache_df_k = nrm((DEC_BATCH, DEPTH, PAST_LEN, DF_HEADS, 2, DF_HD), 1.0)
    cache_df_v = nrm((DEC_BATCH, DEPTH, PAST_LEN, DF_HEADS, DF_V), 1.0)
    state_ssm = nrm((DEC_BATCH, DEPTH, 2, SSM_HEADS, SSM_P, SSM_N), 0.5)
    c = nrm((DEC_BATCH, D), 1.0)
    c_ctx = nrm((D,), 1.0)
    mod_w = nrm((DEPTH, D, 6 * D), 0.5 * D ** -0.5)
    mod_b = nrm((DEPTH, 6 * D), 0.02)
    norm1_g = gain((DEPTH, D))
    norm2_g = gain((DEPTH, D))
    w_in = nrm((DEPTH, D, IN_WIDTH), D ** -0.5)
    na_rel_bias = nrm((DEPTH, NA_HEADS, 2 * NA_KH - 1, 2 * NA_KW - 1), 0.1)
    mla_q_norm_g = gain((DEPTH, MLA_Q_RANK))
    mla_kv_norm_g = gain((DEPTH, MLA_KV_RANK))
    mla_w_uq = nrm((DEPTH, MLA_Q_RANK, MLA_HEADS * (MLA_NOPE + MLA_ROPE)), MLA_Q_RANK ** -0.5)
    mla_w_ukv = nrm((DEPTH, MLA_KV_RANK, MLA_HEADS * (MLA_NOPE + MLA_V)), MLA_KV_RANK ** -0.5)
    df_lambda = nrm((DEPTH, 4, DF_HD), 0.1)
    df_subln_g = gain((DEPTH, DF_V))
    ssm_conv_w = nrm((DEPTH, SSM_CONV, SSM_CONV_DIM), SSM_CONV ** -0.5)
    ssm_conv_b = nrm((DEPTH, SSM_CONV_DIM), 0.02)
    dt0 = jnp.exp(jax.random.uniform(nxt(), (DEPTH, 2, SSM_HEADS), f32, math.log(1e-3), math.log(1e-1)))
    ssm_dt_bias = dt0 + jnp.log(-jnp.expm1(-dt0))
    ssm_a_log = jnp.log(jax.random.uniform(nxt(), (DEPTH, 2, SSM_HEADS), f32, 1.0, 16.0))
    ssm_d = gain((DEPTH, SSM_HEADS))
    ssm_norm_g = gain((DEPTH, SSM_HEADS * SSM_P))
    w_branch = nrm((DEPTH, N_BRANCH, BRANCH_W, D), BRANCH_W ** -0.5)
    w_out = nrm((DEPTH, D, D), D ** -0.5)
    router_w = nrm((DEPTH, D, N_EXPERTS), D ** -0.5)
    exp_w_gate = nrm((DEPTH, N_EXPERTS, D, EXPERT_FF), D ** -0.5)
    exp_w_up = nrm((DEPTH, N_EXPERTS, D, EXPERT_FF), D ** -0.5)
    exp_w_down = nrm((DEPTH, N_EXPERTS, EXPERT_FF, D), EXPERT_FF ** -0.5)
    final_norm_g = gain((D,))
    return {'x_prompt': x_prompt, 'x_sample': x_sample,
            'cache_na_k': cache_na_k, 'cache_na_v': cache_na_v,
            'cache_mla_ckv': cache_mla_ckv, 'cache_mla_krope': cache_mla_krope,
            'cache_df_k': cache_df_k, 'cache_df_v': cache_df_v, 'state_ssm': state_ssm,
            'c': c, 'c_ctx': c_ctx, 'mod_w': mod_w, 'mod_b': mod_b, 'norm1_g': norm1_g, 'norm2_g': norm2_g,
            'w_in': w_in, 'na_rel_bias': na_rel_bias, 'mla_q_norm_g': mla_q_norm_g, 'mla_kv_norm_g': mla_kv_norm_g,
            'mla_w_uq': mla_w_uq, 'mla_w_ukv': mla_w_ukv, 'df_lambda': df_lambda, 'df_subln_g': df_subln_g,
            'ssm_conv_w': ssm_conv_w, 'ssm_conv_b': ssm_conv_b, 'ssm_dt_bias': ssm_dt_bias, 'ssm_a_log': ssm_a_log,
            'ssm_d': ssm_d, 'ssm_norm_g': ssm_norm_g, 'w_branch': w_branch, 'w_out': w_out, 'router_w': router_w,
            'exp_w_gate': exp_w_gate, 'exp_w_up': exp_w_up, 'exp_w_down': exp_w_down, 'final_norm_g': final_norm_g}

def reference(x_prompt, x_sample, cache_na_k, cache_na_v, cache_mla_ckv, cache_mla_krope, cache_df_k, cache_df_v,
              state_ssm, c, c_ctx, mod_w, mod_b, norm1_g, norm2_g, w_in, na_rel_bias, mla_q_norm_g, mla_kv_norm_g,
              mla_w_uq, mla_w_ukv, df_lambda, df_subln_g, ssm_conv_w, ssm_conv_b, ssm_dt_bias, ssm_a_log, ssm_d,
              ssm_norm_g, w_branch, w_out, router_w, exp_w_gate, exp_w_up, exp_w_down, final_norm_g):
    xp, xs = x_prompt, x_sample
    new_na_k, new_na_v, new_ckv, new_krope, new_df_k, new_df_v, new_ssm = [], [], [], [], [], [], []
    for l in range(DEPTH):
        lp = {'mod_w': mod_w[l], 'mod_b': mod_b[l], 'norm1': norm1_g[l], 'norm2': norm2_g[l], 'w_in': w_in[l],
              'na_rel_bias': na_rel_bias[l], 'mla_q_norm': mla_q_norm_g[l], 'mla_kv_norm': mla_kv_norm_g[l],
              'mla_w_uq': mla_w_uq[l], 'mla_w_ukv': mla_w_ukv[l], 'df_lambda': df_lambda[l], 'df_subln': df_subln_g[l],
              'ssm_conv_w': ssm_conv_w[l], 'ssm_conv_b': ssm_conv_b[l], 'ssm_dt_bias': ssm_dt_bias[l],
              'ssm_a_log': ssm_a_log[l], 'ssm_d': ssm_d[l], 'ssm_norm': ssm_norm_g[l], 'w_branch': w_branch[l],
              'w_out': w_out[l], 'router_w': router_w[l], 'exp_w_gate': exp_w_gate[l], 'exp_w_up': exp_w_up[l],
              'exp_w_down': exp_w_down[l]}
        xp, ctx_new = trunk_layer(xp, c_ctx[None, :], lp, l, None)
        new_na_k.append(ctx_new['na_k'])
        new_na_v.append(ctx_new['na_v'])
        new_ckv.append(ctx_new['mla_ckv'])
        new_krope.append(ctx_new['mla_krope'])
        new_df_k.append(ctx_new['df_k'])
        new_df_v.append(ctx_new['df_v'])
        new_ssm.append(ctx_new['ssm'])
        ctx_cached = {'na_k': cache_na_k[:, l], 'na_v': cache_na_v[:, l], 'mla_ckv': cache_mla_ckv[:, l],
                      'mla_krope': cache_mla_krope[:, l], 'df_k': cache_df_k[:, l], 'df_v': cache_df_v[:, l],
                      'ssm': state_ssm[:, l]}
        xs, _ = trunk_layer(xs, c, lp, l, ctx_cached)
    y_prompt = rmsnorm(xp, final_norm_g)
    y_sample = rmsnorm(xs, final_norm_g)
    return (y_prompt, y_sample, jnp.stack(new_na_k, axis=1), jnp.stack(new_na_v, axis=1),
            jnp.stack(new_ckv, axis=1), jnp.stack(new_krope, axis=1), jnp.stack(new_df_k, axis=1),
            jnp.stack(new_df_v, axis=1), jnp.stack(new_ssm, axis=1))


_drawn_inputs = setup_inputs


def setup_inputs(seed=0):
    import zlib

    import numpy as np

    out = dict(_drawn_inputs(seed))
    spreads = {}
    factors = {'cache_na_k': 3.629,
     'cache_na_v': 3.11,
     'cache_mla_ckv': 6.351,
     'cache_mla_krope': 8.0,
     'norm2_g': 6.888,
     'na_rel_bias': 64.0,
     'mla_q_norm_g': 8.0,
     'mla_kv_norm_g': 2.994,
     'df_lambda': 8.0,
     'df_subln_g': 8.0,
     'ssm_d': 8.0,
     'ssm_norm_g': 7.895,
     'final_norm_g': 8.518}
    for name, (base, spread) in spreads.items():
        noise = np.random.default_rng([zlib.crc32(name.encode()), seed]).standard_normal(out[name].shape)
        drawn = base * np.exp(spread * noise) if base else spread * noise
        out[name] = jnp.asarray(drawn.astype(out[name].dtype))
    for name, factor in factors.items():
        out[name] = (out[name] * factor).astype(out[name].dtype)
    return out
```

```python
import math
from contextlib import ExitStack, contextmanager

import numpy as np

import concourse.bass as bass
from concourse import mybir

F32 = mybir.dt.float32
ALU = mybir.AluOpType
ACT = mybir.ActivationFunctionType
AXX = mybir.AxisListType.X

P = 128
D = 1024
KD = D // P
SAMPLE, PROMPT, CTX = 512, 128, 128
T = SAMPLE + PROMPT
NT = T // P
KEYS = SAMPLE + CTX + PROMPT
OWN_P = SAMPLE + CTX
DEPTH = 2
GRID_W = 64
ROWS = SAMPLE // GRID_W
EPS = 1e-6
HEADS = 4
NE = 16
FF = 1024
CAP_S, CAP_P = 2 * SAMPLE // NE, 2 * PROMPT // NE
SLOTS = CAP_S + CAP_P
QR, KVR, ROPE = 384, 256, 32
NA_DY, NA_DX = 15, 31
BIAS_W = 128
BIAS_MID = GRID_W - 1
O_NAQ, O_NAK, O_NAV, O_CQ, O_CKV, O_KR = 0, 256, 512, 768, 1152, 1408
O_DFQ, O_DFK, O_DFV, O_SX, O_SZ, O_SB, O_SC, O_DT, O_GATE = 1440, 1696, 1952, 2208, 2464, 2720, 2848, 2976, 2984
IN_W = O_GATE + 4 * D
GROUPS = ((0, 0, SAMPLE), (1, SAMPLE, T))


class Count:

    def __init__(self, sem):
        self.sem, self.n = sem, 0

    def mark(self, ins):
        self.n += 1
        ins.then_inc(self.sem, 1)
        return self.n

    def link(self, eng, ins):
        self.mark(ins)
        eng.wait_ge(self.sem, self.n)


class Load:

    def __init__(self, sem):
        self.sem, self.n = sem, 0

    def start(self, eng, out, in_):
        self.n += 1
        eng.dma_start(out, in_).then_inc(self.sem, 16)

    @property
    def total(self):
        return 16 * self.n


@contextmanager
def stage(nc):
    with ExitStack() as own:
        sems = []

        def sem(name):
            s = own.enter_context(nc.semaphore(name))
            sems.append(s.num)
            return s

        def sb(name, shape, dt=F32):
            return own.enter_context(nc.sbuf_tensor(name, shape, dt))

        block = ExitStack()
        b = block.enter_context(nc.Block())
        yield b, sem, sb
        block.close()
        nc.all_engine_barrier(sems_to_clear=range(min(sems), max(sems) + 1))


def layer_row(ap, layer):
    names = " ".join(f"d{i}" for i in range(len(ap.shape) - 1))
    first, rest = ("d0", names.split(" ", 1)[1] if " " in names else "")
    return ap[bass.ds(layer, 1)].rearrange(f"l {names} -> (l {first}) {rest}".strip())


def chunk_columns(vec):
    return vec.rearrange("(c p) -> p c", p=P)


C_ID, C_LE, C_GE, C_ROT, C_BLK, C_ONE, C_SLOT, C_WIN = 0, 128, 256, 384, 512, 640, 768, 768 + SLOTS
C_COS = C_WIN + GRID_W
C_SIN = C_COS + SAMPLE
C_LAM = C_SIN + SAMPLE
C_END = C_LAM + 1
V_MODB, V_N1, V_N2, V_QG, V_KVG, V_SUB, V_CW, V_CB, V_DTB, V_ALOG, V_SD, V_SG, V_LAM = (
    0, 48, 56, 64, 67, 69, 70, 82, 86, 94, 102, 104, 106)
V_LI = V_LAM + 128
V_END = V_LI + 2
FEATURE_CHUNKS = 20
M_V = FEATURE_CHUNKS * P
M_DT = M_V + 512
M_END = M_DT + 8
K_NA, K_DF, K_CKV, K_KR, K_N = 0, 2, 4, 6, 7
SXW = T + 4
SX_S, SX_P = 1, SAMPLE + 3


def pcol(t):
    return t * P if t < NT - 1 else SAMPLE + 2


def build(nc, io):
    with ExitStack() as whole:
        def sb(name, shape, dt=F32):
            return whole.enter_context(nc.sbuf_tensor(name, shape, dt))

        g = {}
        g["ps"] = whole.enter_context(nc.psum_tensor("ps", [P, 8, 512], F32))
        g["cst"] = sb("cst", [P, C_END])
        g["x"] = sb("x", [P, KD, T])
        g["h"] = sb("h", [P, KD, T])
        g["vec"] = sb("vec", [P, V_END])
        g["cond"] = sb("cond", [P, KD, 2])
        g["mod"] = sb("mod", [P, 48, 2])
        g["gs1"] = sb("gs1", [P, KD, 2])
        g["gs2"] = sb("gs2", [P, KD, 2])
        g["fin"] = sb("fin", [P, KD])
        begin(nc, io, g)
        with nc.Fori(0, DEPTH) as layer:
            modulation(nc, io, g, layer)
            norm(nc, g, "n1", g["gs1"], g["mod"][:, 0:8, :])
            with ExitStack() as mix:
                def mb(name, shape, dt=F32):
                    g[name] = mix.enter_context(nc.sbuf_tensor(name, shape, dt))

                mb("br", [P, 4, 2, T])
                with ExitStack() as heads:
                    def hb(name, shape, dt=F32):
                        g[name] = heads.enter_context(nc.sbuf_tensor(name, shape, dt))

                    hb("kt", [P, K_N, KEYS])
                    hb("qt", [P, 4, T])
                    hb("v", [P, 6, 512])
                    hb("sx", [P, 4, SXW])
                    hb("sz", [P, 2, T])
                    hb("dtr", [P, NT, 8])
                    with ExitStack() as lat:
                        for name, shape in (("cq", [P, 3, T]), ("qn", [P, 2, T]), ("qr", [P, T]),
                                            ("kn", [P, 2, KEYS]), ("mv", [P, 6, 256])):
                            g[name] = lat.enter_context(nc.sbuf_tensor(name, shape, F32))
                        projections(nc, io, g, layer)
                        latent_heads(nc, io, g, layer)
                        attention(nc, io, g, layer)
                    ssm(nc, io, g, layer)
                merge(nc, io, g, layer)
            norm(nc, g, "n2", g["gs2"], g["mod"][:, 24:32, :])
            with ExitStack() as moe:
                for name, shape in (("htok", [P, NT, D]), ("pos", [P, NT, NE + 1]), ("aff", [P, NT, NE + 1])):
                    g[name] = moe.enter_context(nc.sbuf_tensor(name, shape, F32))
                router(nc, io, g, layer)
                experts(nc, io, g, layer)
        finish(nc, io, g)


def begin(nc, io, g):
    with stage(nc) as (block, sem, sb):
        start_loads = Load(sem("start_loads"))

        @block.sync
        def _(sp):
            start_loads.start(sp, g["cst"][:], io["cst"])
            start_loads.start(sp, g["x"][:], io["x"])
            start_loads.start(sp, g["cond"][:], io["cond"])
            start_loads.start(sp, g["fin"][:], io["fin"])
            sp.wait_ge(start_loads.sem, start_loads.total)


def modulation(nc, io, g, layer):
    ps, vec, mod, cst = g["ps"], g["vec"], g["mod"], g["cst"]
    NCH, RING = 12, 4
    with stage(nc) as (block, sem, sb):
        w = sb("mod_w", [P, RING, KD, 512])
        e = sb("mod_e", [P, KD, 2])
        e1 = sb("mod_e1", [P, KD, 2])
        e2 = sb("mod_e2", [P, KD, 2])
        sc = sb("mod_sc", [P, KD, 2])
        rows = sb("mod_rows", [2, NCH * 512])
        vec_loaded = sem("vec_loaded")
        w_loaded = [sem(f"mod_w_loaded{i}") for i in range(RING)]
        chunk_done, exp_done, rows_done, cols_done = (sem(n) for n in ("mod_chunk_done", "mod_exp_done", "mod_rows_done", "mod_cols_done"))
        silu = Count(sem("mod_silu"))
        src = layer_row(io["mod_w"], layer).rearrange("(k p) n -> p k n", p=P)

        @block.sync
        def _(sp):
            sp.dma_start(vec[:], layer_row(io["vec"], layer)).then_inc(vec_loaded, 16)
            for n in range(NCH):
                if n >= RING:
                    sp.wait_ge(chunk_done, n - RING + 1)
                sp.dma_start(w[:, n % RING], src[:, :, n * 512:(n + 1) * 512]).then_inc(w_loaded[n % RING], 16)

        @block.scalar
        def _(act):
            act.activation(e[:], g["cond"][:], ACT.Exp, scale=-1.0).then_inc(exp_done, 1)

        @block.tensor
        def _(pe):
            pe.wait_ge(silu.sem, 3)

            def columns(n):
                pe.wait_ge(rows_done, n + 1)
                for j in range(4 * n, 4 * n + 4):
                    last = pe.transpose(ps[:, 7, 2 * j:2 * j + 2], rows[:, j * P:(j + 1) * P], cst[0:2, C_ID:C_ID + 2])
                last.then_inc(cols_done, 1)

            for n in range(NCH):
                pe.wait_ge(w_loaded[n % RING], 16 * (n // RING + 1))
                if n >= 4:
                    pe.wait_ge(rows_done, n - 3)
                for k in range(KD):
                    last = pe.matmul(ps[0:2, n % 4, :], sc[:, k, :], w[:, n % RING, k, :],
                                     start=(k == 0), stop=(k == KD - 1))
                last.then_inc(chunk_done, 1)
                if n >= 1:
                    columns(n - 1)
            columns(NCH - 1)

        @block.vector
        def _(v):
            v.wait_ge(exp_done, 1)
            silu.link(v, v.tensor_scalar(e1[:], e[:], 1.0, None, ALU.add))
            silu.link(v, v.reciprocal(e2[:], e1[:]))
            silu.link(v, v.tensor_tensor(sc[:], e2[:], g["cond"][:], ALU.mult))
            for n in range(NCH):
                v.wait_ge(chunk_done, n + 1)
                v.tensor_copy(rows[:, n * 512:(n + 1) * 512], ps[0:2, n % 4, :]).then_inc(rows_done, 1)
            v.wait_ge(cols_done, NCH)
            v.wait_ge(vec_loaded, 16)
            silu.link(v, v.tensor_tensor(mod[:], ps[:, 7, 0:96].rearrange("p (a b) -> p a b", b=2),
                                         vec[:, V_MODB:V_MODB + 48].unsqueeze(2).broadcast_to([P, 48, 2]), ALU.add))
            for gs, first, gain in ((g["gs1"], 8, V_N1), (g["gs2"], 32, V_N2)):
                silu.mark(v.scalar_tensor_tensor(
                    out=gs[:], in0=mod[:, first:first + 8, :], scalar=1.0,
                    in1=vec[:, gain:gain + 8].unsqueeze(2).broadcast_to([P, KD, 2]), op0=ALU.add, op1=ALU.mult))


def norm(nc, g, name, gain, shift):
    ps, x, h, cst = g["ps"], g["x"], g["h"], g["cst"]
    with stage(nc) as (block, sem, sb):
        sq = sb(name + "_sq", [P, 2, T])
        ms = sb(name + "_ms", [P, T])
        root = sb(name + "_root", [P, T])
        rstd = sb(name + "_rstd", [P, T])
        xn = sb(name + "_xn", [P, 2, T])
        sq_ready, sq_used, ms_ready, root_ready, rstd_ready, xn_ready, h_ready = (
            sem(name + s) for s in ("_sq_ready", "_sq_used", "_ms_ready", "_root_ready", "_rstd_ready", "_xn_ready", "_h_ready"))

        @block.scalar
        def _(act):
            for k in range(KD):
                if k >= 2:
                    act.wait_ge(sq_used, k - 1)
                act.activation(sq[:, k % 2], x[:, k], ACT.Square).then_inc(sq_ready, 1)
            act.wait_ge(ms_ready, 1)
            act.activation(root[:], ms[:], ACT.Sqrt).then_inc(root_ready, 1)
            for k in range(KD):
                act.wait_ge(xn_ready, k + 1)
                for grp, a, b in GROUPS:
                    if shift is None:
                        last = act.activation(h[:, k, a:b], xn[:, k % 2, a:b], ACT.Copy)
                    else:
                        last = act.activation(h[:, k, a:b], xn[:, k % 2, a:b], ACT.Identity,
                                              bias=shift[:, k, grp:grp + 1], scale=gain[:, k, grp:grp + 1])
                last.then_inc(h_ready, 1)

        @block.tensor
        def _(pe):
            for k in range(KD):
                pe.wait_ge(sq_ready, k + 1)
                pe.matmul(ps[:, 0, :], cst[:, C_ONE:C_ONE + P], sq[:, k % 2, 0:SAMPLE], start=(k == 0), stop=(k == KD - 1))
                pe.matmul(ps[:, 1, 0:PROMPT], cst[:, C_ONE:C_ONE + P], sq[:, k % 2, SAMPLE:T],
                          start=(k == 0), stop=(k == KD - 1)).then_inc(sq_used, 1)

        @block.vector
        def _(v):
            v.wait_ge(sq_used, KD)
            v.tensor_scalar(ms[:], ps[:, 0:2].rearrange("p a b -> p (a b)")[:, 0:T], 1.0 / D, EPS, ALU.mult, ALU.add).then_inc(ms_ready, 1)
            v.wait_ge(root_ready, 1)
            v.reciprocal(rstd[:], root[:]).then_inc(rstd_ready, 1)
            v.wait_ge(rstd_ready, 1)
            for k in range(KD):
                if k >= 2:
                    v.wait_ge(h_ready, k - 1)
                if shift is None:
                    v.scalar_tensor_tensor(out=xn[:, k % 2], in0=x[:, k], scalar=gain[:, k:k + 1], in1=rstd[:],
                                           op0=ALU.mult, op1=ALU.mult).then_inc(xn_ready, 1)
                else:
                    v.tensor_tensor(xn[:, k % 2], x[:, k], rstd[:], ALU.mult).then_inc(xn_ready, 1)


def projections(nc, io, g, layer):
    ps, h = g["ps"], g["h"]
    kt, qt, v_sb, sx, sz = g["kt"], g["qt"], g["v"], g["sx"], g["sz"]
    RING, LOADS = 3, FEATURE_CHUNKS // 4 + 1

    def key(c):
        return [(kt[:, c, 0:SAMPLE], 0, SAMPLE), (kt[:, c, OWN_P:KEYS], SAMPLE, T)]

    def conv(c):
        return [(sx[:, c, SX_S:SX_S + SAMPLE], 0, SAMPLE), (sx[:, c, SX_P:SX_P + PROMPT], SAMPLE, T)]

    def plain(buf, c):
        return [(buf[:, c, :], 0, T)]

    places = ([plain(qt, 0), plain(qt, 1), key(K_NA), key(K_NA + 1)] + [plain(g["cq"], c) for c in range(3)]
              + [key(K_CKV), key(K_CKV + 1), key(K_KR), plain(qt, 2), plain(qt, 3), key(K_DF), key(K_DF + 1)]
              + [conv(c) for c in range(4)] + [plain(sz, 0), plain(sz, 1)])
    assert len(places) == FEATURE_CHUNKS
    with stage(nc) as (block, sem, sb):
        w = sb("in_w", [P, RING, KD, 512])
        wdt = sb("in_wdt", [P, KD, 8])
        w_loaded = [sem(f"in_w_loaded{i}") for i in range(RING)]
        dt_w_loaded, ctx_loaded, chunk_done, copied_v, copied_a, pads = (
            sem(n) for n in ("dt_w_loaded", "ctx_loaded", "in_chunk_done", "in_copied_vector", "in_copied_scalar", "in_pads"))
        src = layer_row(io["w_mix"], layer).rearrange("(k p) n -> p k n", p=P)
        ctx = Load(ctx_loaded)

        @block.sync
        def _(sp):
            for n in range(LOADS):
                if n >= RING:
                    sp.wait_ge(chunk_done, 4 * (n - RING + 1))
                sp.dma_start(w[:, n % RING], src[:, :, n * 512:(n + 1) * 512]).then_inc(w_loaded[n % RING], 16)
                if n == 0:
                    ctx.start(sp, kt[:, :, SAMPLE:OWN_P], layer_row(io["ctx_k"], layer))
                    ctx.start(sp, v_sb[:, 4, :], layer_row(io["ctx_v"], layer))
                    sp.dma_start(wdt[:], src[:, :, M_DT:M_END]).then_inc(dt_w_loaded, 16)
            sp.wait_ge(ctx_loaded, ctx.total)

        @block.tensor
        def _(pe):
            def free_pair(i):
                if i >= 4:
                    pe.wait_ge(copied_v if i % 2 == 0 else copied_a, (i - 4) // 2 + 1)

            for i in range(FEATURE_CHUNKS):
                n, b = i // 4, 2 * (i % 4)
                if i % 4 == 0:
                    pe.wait_ge(w_loaded[n % RING], 16 * (n // RING + 1))
                free_pair(i)
                for a, z, bank in ((0, SAMPLE, b), (SAMPLE, T, b + 1)):
                    for k in range(KD):
                        last = pe.matmul(ps[:, bank, 0:z - a], w[:, n % RING, k, (i % 4) * P:(i % 4 + 1) * P],
                                         h[:, k, a:z], start=(k == 0), stop=(k == KD - 1))
                last.then_inc(chunk_done, 1)
            pe.wait_ge(w_loaded[(LOADS - 1) % RING], 16 * ((LOADS - 1) // RING + 1))
            pe.wait_ge(dt_w_loaded, 16)
            for t in range(NT):
                i = FEATURE_CHUNKS + t
                b = 2 * (i % 4)
                free_pair(i)
                for k in range(KD):
                    pe.matmul(ps[:, b, :], h[:, k, t * P:(t + 1) * P], w[:, (LOADS - 1) % RING, k, :],
                              start=(k == 0), stop=(k == KD - 1))
                for k in range(KD):
                    last = pe.matmul(ps[:, b + 1, 0:8], h[:, k, t * P:(t + 1) * P], wdt[:, k, :],
                                     start=(k == 0), stop=(k == KD - 1))
                last.then_inc(chunk_done, 1)

        def copy_out(eng, odd, copy, done):
            for i in range(FEATURE_CHUNKS + NT):
                if i % 2 != odd:
                    continue
                eng.wait_ge(chunk_done, i + 1)
                b = 2 * (i % 4)
                if i < FEATURE_CHUNKS:
                    for dst, a, z in places[i]:
                        if a == 0 and z == T:
                            last = copy(dst, ps[:, b:b + 2].rearrange("p a b -> p (a b)")[:, 0:T])
                        else:
                            last = copy(dst, ps[:, b + (1 if a else 0), 0:z - a])
                else:
                    t = i - FEATURE_CHUNKS
                    copy(v_sb[:, t if t < NT - 1 else 5, :], ps[:, b, :])
                    last = copy(g["dtr"][:, t, :], ps[:, b + 1, 0:8])
                last.then_inc(done, 1)

        @block.vector
        def _(v):
            copy_out(v, 0, v.tensor_copy, copied_v)

        @block.scalar
        def _(act):
            copy_out(act, 1, lambda o, i: act.activation(o, i, ACT.Copy), copied_a)

        @block.gpsimd
        def _(pool):
            pool.memset(sx[:, :, 0:1], 0.0)
            pool.memset(sx[:, :, SX_S + SAMPLE:SX_P], 0.0)
            pool.memset(sx[:, :, SXW - 1:SXW], 0.0).then_inc(pads, 1)


def latent_heads(nc, io, g, layer):
    ps, cst, vec, kt, qt, cq = g["ps"], g["cst"], g["vec"], g["kt"], g["qt"], g["cq"]
    qn, qr, kn, mv = g["qn"], g["qr"], g["kn"], g["mv"]
    SPLIT = ((0, SAMPLE, 0), (SAMPLE, T, OWN_P))

    def pair(b, n=T):
        return ps[:, b:b + 2].rearrange("p a b -> p (a b)")[:, 0:n]

    with stage(nc) as (block, sem, sb):
        wuq = sb("wuq", [P, 3, 384])
        wukv = sb("wukv", [P, 2, 512])
        sq = sb("lat_sq", [P, 5, T])
        ms = sb("lat_ms", [P, 2, T])
        root = sb("lat_root", [P, 2, T])
        rstd = sb("lat_rstd", [P, 2, T])
        xc = sb("rot_cos", [P, 2, SAMPLE])
        xs = sb("rot_sin", [P, 2, SAMPLE])
        up = Load(sem("up_weights_loaded"))
        sq_ready, sums_done, ms_ready, root_ready, out_done = (
            sem(n) for n in ("lat_sq_ready", "lat_sums_done", "lat_ms_ready", "lat_root_ready", "prompt_out_done"))
        normed = Count(sem("lat_normed"))
        up_done, up_copied, turned, rotated = (
            sem(n) for n in ("up_done", "up_copied", "turned", "rotated"))
        units = []
        for c in range(3):
            dst = qn[:, c, :] if c < 2 else qr[:]
            units.append(([(dst, 0, T)], 3,
                          lambda k, c=c: wuq[:, k, c * P:(c + 1) * P], lambda k, a, z: cq[:, k, a:z], T))
        for c in range(2):
            units.append(([(kn[:, c, :], 0, KEYS)], 2,
                          lambda k, c=c: wukv[:, k, c * P:(c + 1) * P], lambda k, a, z: kt[:, K_CKV + k, a:z], KEYS))
        for t in range(6):
            units.append(([(mv[:, t, :], 0, 256)], 2,
                          lambda k, t=t: kt[:, K_CKV + k, t * P:(t + 1) * P], lambda k, a, z: wukv[:, k, 256 + a:256 + z], 256))
        NU = len(units)
        rots = [qr[:, 0:SAMPLE], kt[:, K_KR, 0:SAMPLE], qt[:, 2, 0:SAMPLE], qt[:, 3, 0:SAMPLE],
                kt[:, K_DF, 0:SAMPLE], kt[:, K_DF + 1, 0:SAMPLE]]

        @block.sync
        def _(sp):
            up.start(sp, wuq[:], layer_row(io["w_uq"], layer).rearrange("(k p) n -> p k n", p=P))
            up.start(sp, wukv[:], layer_row(io["w_ukv"], layer).rearrange("(k p) n -> p k n", p=P))
            sp.wait_ge(normed.sem, 1 + 3 + 4)
            sp.dma_start(layer_row(io["new_k"], layer), kt[:, :, OWN_P:KEYS]).then_inc(out_done, 16)
            sp.dma_start(layer_row(io["new_v"], layer), g["v"][:, 5, :]).then_inc(out_done, 16)
            sp.wait_ge(out_done, 32)

        @block.scalar
        def _(act):
            for c in range(3):
                act.activation(sq[:, c, :], cq[:, c, :], ACT.Square)
            for c in range(2):
                for a, z, ka in SPLIT:
                    last = act.activation(sq[:, 3 + c, a:z], kt[:, K_CKV + c, ka:ka + z - a], ACT.Square)
            last.then_inc(sq_ready, 1)
            act.wait_ge(ms_ready, 2)
            act.activation(root[:], ms[:], ACT.Sqrt).then_inc(root_ready, 1)
            for i in range(NU):
                act.wait_ge(up_done, i + 1)
                for dst, a, z in units[i][0]:
                    act.activation(dst, pair(2 * (i % 3), z), ACT.Copy).then_inc(up_copied, 1)

        @block.tensor
        def _(pe):
            pe.wait_ge(sq_ready, 1)
            for b, chunks in ((0, (0, 1, 2)), (2, (3, 4))):
                for a, z, bank in ((0, SAMPLE, b), (SAMPLE, T, b + 1)):
                    for c in chunks:
                        last = pe.matmul(ps[:, bank, 0:z - a], cst[:, C_ONE:C_ONE + P], sq[:, c, a:z],
                                         start=(c == chunks[0]), stop=(c == chunks[-1]))
            last.then_inc(sums_done, 1)
            pe.wait_ge(up.sem, 32)
            pe.wait_ge(normed.sem, 1 + 3 + 4)
            for i, (dsts, nk, lhs, rhs, n) in enumerate(units):
                b = 2 * (i % 3)
                if i >= 3:
                    pe.wait_ge(up_copied, i - 2)
                for a in range(0, n, 512):
                    z = min(n, a + 512)
                    for k in range(nk):
                        last = pe.matmul(ps[:, b + a // 512, 0:z - a], lhs(k), rhs(k, a, z), start=(k == 0), stop=(k == nk - 1))
                last.then_inc(up_done, 1)
            pe.wait_ge(up_copied, 3)
            for r, buf in enumerate(rots):
                if r >= 2:
                    pe.wait_ge(rotated, 3 * (r - 2) + 2)
                pe.matmul(ps[:, 6 + r % 2, :], cst[:, C_ROT:C_ROT + P], buf, start=True, stop=True).then_inc(turned, 1)

        @block.vector
        def _(v):
            v.wait_ge(sums_done, 1)
            v.tensor_scalar(ms[:, 0, :], pair(0), 1.0 / QR, EPS, ALU.mult, ALU.add).then_inc(ms_ready, 1)
            v.tensor_scalar(ms[:, 1, :], pair(2), 1.0 / KVR, EPS, ALU.mult, ALU.add).then_inc(ms_ready, 1)
            v.wait_ge(root_ready, 1)
            normed.link(v, v.reciprocal(rstd[:], root[:]))
            for c in range(3):
                normed.mark(v.scalar_tensor_tensor(out=cq[:, c, :], in0=cq[:, c, :], scalar=vec[:, V_QG + c:V_QG + c + 1],
                                                   in1=rstd[:, 0, :], op0=ALU.mult, op1=ALU.mult))
            for c in range(2):
                for a, z, ka in SPLIT:
                    dst = kt[:, K_CKV + c, ka:ka + z - a]
                    normed.mark(v.scalar_tensor_tensor(out=dst, in0=dst, scalar=vec[:, V_KVG + c:V_KVG + c + 1],
                                                       in1=rstd[:, 1, a:z], op0=ALU.mult, op1=ALU.mult))

            for r, buf in enumerate(rots):
                v.wait_ge(turned, r + 1)
                if r >= 2:
                    v.wait_ge(rotated, 3 * (r - 2) + 3)
                v.tensor_tensor(xc[:, r % 2], buf, cst[:, C_COS:C_COS + SAMPLE], ALU.mult).then_inc(rotated, 1)
                v.tensor_tensor(xs[:, r % 2], ps[:, 6 + r % 2, :], cst[:, C_SIN:C_SIN + SAMPLE], ALU.mult).then_inc(rotated, 1)
                v.wait_ge(rotated, 3 * r + 2)
                v.tensor_tensor(buf, xc[:, r % 2], xs[:, r % 2], ALU.add).then_inc(rotated, 1)



def attention(nc, io, g, layer):
    ps, cst, vec, kt, qt, br = g["ps"], g["cst"], g["vec"], g["kt"], g["qt"], g["br"]
    qn, qr, kn, mv, vv = g["qn"], g["qr"], g["kn"], g["mv"], g["v"]
    NA, MLA, DF = range(3)
    units = []
    for branch in (NA, MLA, DF):
        for hd in range(HEADS):
            lo, c = 64 * (hd % 2), hd // 2
            for t in range(NT):
                for comp in range(2 if branch == DF else 1):
                    if branch == NA:
                        parts = [(qt[lo:lo + 64, c, :], kt[lo:lo + 64, K_NA + c, :])]
                    elif branch == MLA:
                        parts = [(qn[lo:lo + 64, c, :], kn[lo:lo + 64, c, :]),
                                 (qr[32 * hd:32 * hd + 32, :], kt[32 * hd:32 * hd + 32, K_KR, :])]
                    else:
                        d0 = lo + 32 * comp
                        parts = [(qt[d0:d0 + 32, 2 + c, :], kt[d0:d0 + 32, K_DF + c, :])]
                    vals = mv[:, :, 64 * hd:64 * hd + 64] if branch == MLA else \
                        vv[:, :, (256 if branch == DF else 0) + 64 * hd:(256 if branch == DF else 0) + 64 * hd + 64]
                    units.append(dict(branch=branch, hd=hd, t=t, comp=comp, parts=parts, vals=vals,
                                      scale=(64 ** -0.5, 96 ** -0.5, 32 ** -0.5)[branch],
                                      biased=branch == NA and t < NT - 1,
                                      first=comp == 0, last=branch != DF or comp == 1,
                                      keys=(0, OWN_P) if t < NT - 1 else (OWN_P, KEYS)))
    NU = len(units)
    outs, n = [], 0
    for u in units:
        outs.append(n)
        n += u["last"]
    NO = n

    def scores(u, n):
        return ps[:, 2 * (u % 2):2 * (u % 2) + 2].rearrange("p a b -> p (a b)")[:, 0:n]

    def out_place(u):
        x = units[u]
        lo = 64 * (x["hd"] % 2)
        return (br[lo:lo + 64, x["branch"], x["hd"] // 2, x["t"] * P:(x["t"] + 1) * P],
                ps[lo:lo + 64, 6 + outs[u] % 2, 0:P])

    with stage(nc) as (block, sem, sb):
        bias = sb("na_bias", [P, HEADS, 16, GRID_W])
        biased = sb("biased_scores", [P, 2, OWN_P])
        prob = sb("prob", [P, 2, OWN_P])
        pt = sb("prob_turned", [P, 2, OWN_P])
        mx = sb("row_max", [P, 2])
        nm = sb("neg_max", [P, 2])
        rowsum = sb("row_sum", [P, 2])
        rec = sb("row_rec", [P, 2])
        lp = sb("lam_prod", [P, 2, 32])
        ls = sb("lam_sum", [P, 2])
        le = sb("lam_exp", [P, 2])
        ld = sb("lam_diff", [P, 1])
        neglam = sb("neg_lam", [P, 1])
        sub = sb("sub_gain", [P, 1])
        dsq = sb("df_sq", [P, 2, T])
        dms = sb("df_ms", [P, 2, T])
        droot = sb("df_root", [P, 2, T])
        drstd = sb("df_rstd", [P, 2, T])
        (bias_loaded, bias_ready, lam_sum_ready, lam_exp_ready, scores_done, neg_max_ready, exp_done, prob_ready,
         turned, turned_copied, out_done, out_copied, df_sq_ready, df_sums_done, df_ms_ready, df_root_ready) = (
            sem(n) for n in ("bias_loaded", "bias_ready", "lam_sum_ready", "lam_exp_ready", "scores_done",
                             "neg_max_ready", "exp_done", "prob_ready", "prob_turned_done", "turned_copied", "out_done",
                             "out_copied", "df_sq_ready", "df_sums_done", "df_ms_ready", "df_root_ready"))
        chain = Count(sem("attention_vector_chain"))

        @block.sync
        def _(sp):
            sp.dma_start(bias[:], layer_row(io["bias"], layer)).then_inc(bias_loaded, 16)

        @block.tensor
        def _(pe):
            def score(u):
                x = units[u]
                if u >= 2:
                    pe.wait_ge(exp_done, u - 1)
                k0, k1 = x["keys"]
                for a in range(k0, k1, 512):
                    z = min(a + 512, k1)
                    dst = scores(u, z - k0)[:, a - k0:z - k0]
                    for i, (q, k) in enumerate(x["parts"]):
                        last = pe.matmul(dst, q[:, x["t"] * P:(x["t"] + 1) * P], k[:, a:z],
                                         start=(i == 0), stop=(i == len(x["parts"]) - 1))
                last.then_inc(scores_done, 1)

            def turn(u):
                x = units[u]
                pe.wait_ge(prob_ready, u + 1)
                if u >= 1:
                    pe.wait_ge(turned_copied, u)
                for b in range((x["keys"][1] - x["keys"][0]) // P):
                    last = pe.transpose(ps[:, 4:6].rearrange("p a b -> p (a b)")[:, b * P:(b + 1) * P],
                                        prob[:, u % 2, b * P:(b + 1) * P], cst[:, C_ID:C_ID + P])
                last.then_inc(turned, 1)

            def values(u):
                x = units[u]
                pe.wait_ge(turned_copied, u + 1)
                if x["first"] and outs[u] >= 2:
                    pe.wait_ge(out_copied, outs[u] - 1)
                nb = (x["keys"][1] - x["keys"][0]) // P
                for b in range(nb):
                    last = pe.matmul(out_place(u)[1], x["vals"][:, b if nb > 1 else 5, :], pt[:, u % 2, b * P:(b + 1) * P],
                                     start=(b == 0 and x["first"]), stop=(b == nb - 1 and x["last"]))
                last.then_inc(out_done, 1)

            for i in range(NU + 2):
                if i < NU:
                    score(i)
                if 1 <= i <= NU:
                    turn(i - 1)
                if i >= 2:
                    values(i - 2)
            pe.wait_ge(df_sq_ready, 1)
            for c in range(2):
                pe.matmul(ps[:, 2 * c, :], cst[:, C_BLK:C_BLK + P], dsq[:, c, 0:SAMPLE], start=True, stop=True)
                last = pe.matmul(ps[:, 2 * c + 1, 0:PROMPT], cst[:, C_BLK:C_BLK + P], dsq[:, c, SAMPLE:T], start=True, stop=True)
            last.then_inc(df_sums_done, 1)

        @block.scalar
        def _(act):
            act.wait_ge(lam_sum_ready, 1)
            act.activation(le[:], ls[:], ACT.Exp).then_inc(lam_exp_ready, 1)
            for i in range(NU + 1):
                if i < NU:
                    x = units[i]
                    n = x["keys"][1] - x["keys"][0]
                    act.wait_ge(neg_max_ready, i + 1)
                    if i >= 2:
                        act.wait_ge(turned, i - 1)
                    src = biased[:, i % 2, 0:n] if x["biased"] else scores(i, n)
                    act.activation(prob[:, i % 2, 0:n], src, ACT.Exp, bias=nm[:, i % 2:i % 2 + 1],
                                   scale=1.0 if x["biased"] else x["scale"],
                                   accum_out=rowsum[:, i % 2:i % 2 + 1]).then_inc(exp_done, 1)
                if i >= 1:
                    u = i - 1
                    n = units[u]["keys"][1] - units[u]["keys"][0]
                    act.wait_ge(turned, u + 1)
                    if u >= 2:
                        act.wait_ge(out_done, u - 1)
                    act.activation(pt[:, u % 2, 0:n], ps[:, 4:6].rearrange("p a b -> p (a b)")[:, 0:n],
                                   ACT.Copy).then_inc(turned_copied, 1)
            act.wait_ge(out_copied, NO)
            act.activation(dsq[:], br[:, DF], ACT.Square).then_inc(df_sq_ready, 1)
            act.wait_ge(df_ms_ready, 1)
            act.activation(droot[:], dms[:], ACT.Sqrt).then_inc(df_root_ready, 1)

        @block.vector
        def _(v):
            lam = vec[:, V_LAM:V_LAM + 128].rearrange("p (a b d) -> p a b d", a=2, b=2)
            chain.link(v, v.tensor_tensor(lp[:], lam[:, :, 0, :], lam[:, :, 1, :], ALU.mult))
            v.tensor_reduce(ls[:], lp[:], AXX, ALU.add).then_inc(lam_sum_ready, 1)
            chain.mark(v.tensor_scalar(sub[:], vec[:, V_SUB:V_SUB + 1], vec[:, V_LI + 1:V_LI + 2], None, ALU.mult))
            v.wait_ge(lam_exp_ready, 1)
            chain.link(v, v.tensor_tensor(ld[:], le[:, 1:2], le[:, 0:1], ALU.subtract))
            chain.link(v, v.tensor_tensor(neglam[:], ld[:], vec[:, V_LI:V_LI + 1], ALU.subtract))
            v.wait_ge(bias_loaded, 16)
            flat = bias[:].rearrange("p a b c -> p (a b) c")
            chain.link(v, v.tensor_tensor(flat, flat, cst[:, C_WIN:C_WIN + GRID_W].unsqueeze(1).broadcast_to(
                [P, HEADS * 16, GRID_W]), ALU.add))

            def maximum(u):
                x = units[u]
                n = x["keys"][1] - x["keys"][0]
                v.wait_ge(scores_done, u + 1)
                if u >= 2:
                    v.wait_ge(exp_done, u - 1)
                src = scores(u, n)
                if x["biased"]:
                    off = 7 - 2 * x["t"]
                    chain.mark(v.scalar_tensor_tensor(
                        out=biased[:, u % 2, 0:SAMPLE], in0=src[:, 0:SAMPLE], scalar=x["scale"],
                        in1=bias[:, x["hd"], off:off + ROWS, :].rearrange("p a b -> p (a b)"), op0=ALU.mult, op1=ALU.add))
                    chain.link(v, v.tensor_scalar(biased[:, u % 2, SAMPLE:n], src[:, SAMPLE:n], x["scale"], None, ALU.mult))
                    src = biased[:, u % 2, 0:n]
                chain.link(v, v.tensor_reduce(mx[:, u % 2:u % 2 + 1], src, AXX, ALU.max))
                v.tensor_scalar(nm[:, u % 2:u % 2 + 1], mx[:, u % 2:u % 2 + 1], -1.0 if x["biased"] else -x["scale"],
                                None, ALU.mult).then_inc(neg_max_ready, 1)

            def normalise(u):
                x = units[u]
                n = x["keys"][1] - x["keys"][0]
                v.wait_ge(exp_done, u + 1)
                r = rec[:, u % 2:u % 2 + 1]
                chain.link(v, v.reciprocal(r, rowsum[:, u % 2:u % 2 + 1]))
                if x["comp"] == 1:
                    v.tensor_scalar(prob[:, u % 2, 0:n], prob[:, u % 2, 0:n], r, neglam[:, 0:1], ALU.mult, ALU.mult).then_inc(prob_ready, 1)
                else:
                    v.tensor_scalar(prob[:, u % 2, 0:n], prob[:, u % 2, 0:n], r, None, ALU.mult).then_inc(prob_ready, 1)

            def copy_out(u):
                if units[u]["last"]:
                    v.wait_ge(out_done, u + 1)
                    dst, src = out_place(u)
                    v.tensor_copy(dst, src).then_inc(out_copied, 1)

            for i in range(NU + 3):
                if i < NU:
                    maximum(i)
                if 1 <= i <= NU:
                    normalise(i - 1)
                if i >= 3:
                    copy_out(i - 3)
            v.wait_ge(df_sums_done, 1)
            v.tensor_scalar(dms[:], ps[:, 0:4].rearrange("p (a b) c -> p a (b c)", a=2)[:, :, 0:T], 1.0 / 64, EPS,
                            ALU.mult, ALU.add).then_inc(df_ms_ready, 1)
            v.wait_ge(df_root_ready, 1)
            chain.link(v, v.reciprocal(drstd[:], droot[:]))
            chain.mark(v.scalar_tensor_tensor(out=br[:, DF], in0=br[:, DF], scalar=sub[:, 0:1], in1=drstd[:],
                                              op0=ALU.mult, op1=ALU.mult))


def ssm(nc, io, g, layer):
    ps, cst, vec, sx, sz, br = g["ps"], g["cst"], g["vec"], g["sx"], g["sz"], g["br"]
    CW = T + 2
    steps = ([(0, t) for t in range(NT - 1)] + [(0, NT - 1)] + [(1, t) for t in reversed(range(NT - 1))] + [(1, NT - 1)])
    NS = len(steps)
    with stage(nc) as (block, sem, sb):
        xc = sb("conv", [P, 4, CW])
        ex = sb("conv_exp", [P, 4, CW])
        exz = sb("z_exp", [P, 2, T])
        xtok = sb("conv_tok", [P, NT, 384])
        dtu, dtn, dte, dtl, dt, a8, ac, nac = (sb(n, [P, NT, 8]) for n in (
            "dt_u", "dt_n", "dt_e", "dt_l", "dt", "dt_a", "a_cum", "neg_a_cum"))
        ea = sb("exp_a", [P, 8])
        gm = sb("bc_masked", [P, NT, 2, 2, P])
        state = sb("state", [P, 2, 2, 2, 64])
        arep = sb("a_rep", [P, 4, P])
        seg = sb("seg", [P, 4, P])
        dec = sb("dec", [P, 4, P])
        e0 = sb("exp_cum", [P, 4, P])
        mm = sb("mixing", [P, 4, P])
        cts = sb("c_scaled", [P, 2, P])
        wd = sb("w_dif", [P, 4])
        we = sb("w_exp", [P, 4])
        xw = sb("x_weighted", [P, 4, 64])
        y = sb("ssm_y", [P, 2, T])
        ysq = sb("ssm_sq", [P, 2, T])
        yms, yroot, yrstd = (sb(n, [P, T]) for n in ("ssm_ms", "ssm_root", "ssm_rstd"))
        (state_loaded, conv_ready, conv_exp, z_exp, dt_arg, dt_exp, dt_one, dt_ln, conv_silu, tok_turned, tok_copied,
         a_ready, cum_done, bc_done, bc_read, rep_ready, along_done, seg_ready, dec_ready, wd_ready, w_ready, mix_ready,
         y_done, y_added, ysq_ready, ysum_done, yms_ready, yroot_ready, gated_ready, state_out) = (
            sem(n) for n in ("state_loaded", "conv_ready", "conv_exp_done", "z_exp_done", "dt_arg", "dt_exp", "dt_one", "dt_ln",
                             "conv_silu", "tok_turned", "tok_copied", "a_ready", "cum_done", "bc_done", "bc_read",
                             "rep_ready", "along_done", "seg_ready", "dec_ready", "wd_ready", "w_ready", "mix_ready",
                             "y_done", "y_added", "ysq_ready", "ysum_done", "yms_ready", "yroot_ready", "gated_ready", "state_out"))
        chain = Count(sem("ssm_vector_chain"))

        def last_col(dr):
            return P - 1 if dr == 0 else 0

        @block.sync
        def _(sp):
            sp.dma_start(state[:, 0], layer_row(io["state"], layer)).then_inc(state_loaded, 16)
            sp.wait_ge(y_added, 2 * NS)
            sp.dma_start(layer_row(io["new_state"], layer), state[:, 1]).then_inc(state_out, 16)
            sp.wait_ge(state_out, 16)

        @block.scalar
        def _(act):
            act.activation(ea[:], vec[:, V_ALOG:V_ALOG + 8], ACT.Exp)
            act.wait_ge(dt_arg, 1)
            act.activation(dte[:], dtn[:], ACT.Exp).then_inc(dt_exp, 1)
            act.activation(exz[:], sz[:], ACT.Exp, scale=-1.0).then_inc(z_exp, 1)
            act.wait_ge(conv_ready, 1)
            act.activation(ex[:], xc[:], ACT.Exp, scale=-1.0).then_inc(conv_exp, 1)
            act.wait_ge(dt_one, 1)
            act.activation(dtl[:], dte[:], ACT.Ln).then_inc(dt_ln, 1)
            for t in range(NT):
                act.wait_ge(tok_turned, t + 1)
                act.activation(xtok[:, t, :], ps[:, t % 2, 0:384], ACT.Copy).then_inc(tok_copied, 1)
            for s, (dr, t) in enumerate(steps):
                act.wait_ge(along_done, s + 1)
                if s >= 1:
                    act.wait_ge(y_added, 2 * s)
                act.activation(e0[:], ps[:, 4, :].rearrange("p (a b) -> p a b", a=4), ACT.Exp).then_inc(dec_ready, 1)
                act.wait_ge(wd_ready, s + 1)
                act.activation(we[:], wd[:], ACT.Exp).then_inc(w_ready, 1)
                act.wait_ge(seg_ready, s + 1)
                act.activation(dec[:], seg[:], ACT.Exp).then_inc(dec_ready, 1)
            act.wait_ge(gated_ready, 1)
            act.activation(ysq[:], y[:], ACT.Square).then_inc(ysq_ready, 1)
            act.wait_ge(yms_ready, 1)
            act.activation(yroot[:], yms[:], ACT.Sqrt).then_inc(yroot_ready, 1)

        @block.tensor
        def _(pe):
            pe.wait_ge(conv_silu, 1)
            for t in range(NT):
                if t >= 2:
                    pe.wait_ge(tok_copied, t - 1)
                for c in range(3):
                    last = pe.transpose(ps[:, t % 2, c * P:(c + 1) * P], xc[:, c, pcol(t):pcol(t) + P], cst[:, C_ID:C_ID + P])
                last.then_inc(tok_turned, 1)
            pe.wait_ge(a_ready, 1)
            for dr, tri in ((0, C_LE), (1, C_GE)):
                last = pe.matmul(ps[:, 2, 20 * dr:20 * dr + 20].rearrange("p (a b) -> p a b", a=NT), cst[:, tri:tri + P],
                                 a8[:, :, 4 * dr:4 * dr + 4], start=True, stop=True)
            last.then_inc(cum_done, 1)
            for t in range(NT):
                if t >= 1:
                    pe.wait_ge(bc_read, t)
                for gr in range(2):
                    lo = 64 * gr
                    last = pe.matmul(ps[:, 3 + 4 * gr, 0:P], xc[lo:lo + 64, 2, pcol(t):pcol(t) + P],
                                     xc[lo:lo + 64, 3, pcol(t):pcol(t) + P], start=True, stop=True)
                last.then_inc(bc_done, 1)
            pe.wait_ge(tok_copied, NT)
            for s, (dr, t) in enumerate(steps):
                tri = C_LE if dr == 0 else C_GE
                pe.wait_ge(rep_ready, s + 1)
                for hd in range(4):
                    last = pe.matmul(ps[:, 4, hd * P:(hd + 1) * P], arep[:, hd, :], cst[:, tri:tri + P], start=True, stop=True)
                last.then_inc(along_done, 1)
                pe.wait_ge(mix_ready, s + 1)
                for hd in range(4):
                    lo, gl = 64 * (hd % 2), 64 * (hd // 2)
                    dst = ps[lo:lo + 64, 5 + 2 * (hd // 2), 0:P]
                    pe.matmul(dst, xtok[:, t, 64 * hd:64 * hd + 64], mm[:, hd, :], start=True, stop=False)
                    pe.matmul(dst, state[gl:gl + 64, t // 4, dr, hd % 2, :], cts[gl:gl + 64, hd % 2, :], start=False, stop=True)
                pe.matmul(ps[:, 6, 0:256], xtok[:, t, 256:384], xw[:].rearrange("p a b -> p (a b)"),
                          start=True, stop=True).then_inc(y_done, 1)
            pe.wait_ge(ysq_ready, 1)
            for a, z, bank in ((0, SAMPLE, 0), (SAMPLE, T, 1)):
                for c in range(2):
                    last = pe.matmul(ps[:, bank, 0:z - a], cst[:, C_ONE:C_ONE + P], ysq[:, c, a:z], start=(c == 0), stop=(c == 1))
            last.then_inc(ysum_done, 1)

        @block.vector
        def _(v):
            link = lambda ins: chain.link(v, ins)
            link(v.tensor_tensor(dtu[:], g["dtr"][:], vec[:, V_DTB:V_DTB + 8].unsqueeze(1).broadcast_to([P, NT, 8]), ALU.add))
            link(v.tensor_scalar(dtn[:], dtu[:], -1.0, None, ALU.mult))
            v.tensor_tensor(dtn[:], dtu[:], dtn[:], ALU.min).then_inc(dt_arg, 1)
            for c in range(4):
                w = [vec[:, V_CW + 4 * tap + c:V_CW + 4 * tap + c + 1] for tap in range(3)]
                link(v.tensor_scalar(xc[:, c], sx[:, c, 0:CW], w[0], vec[:, V_CB + c:V_CB + c + 1], ALU.mult, ALU.add))
                link(v.scalar_tensor_tensor(out=xc[:, c], in0=sx[:, c, 1:1 + CW], scalar=w[1], in1=xc[:, c], op0=ALU.mult, op1=ALU.add))
                ins = v.scalar_tensor_tensor(out=xc[:, c], in0=sx[:, c, 2:2 + CW], scalar=w[2], in1=xc[:, c], op0=ALU.mult, op1=ALU.add)
                if c == 3:
                    ins.then_inc(conv_ready, 1)
                else:
                    chain.mark(ins)
            v.wait_ge(dt_exp, 1)
            v.tensor_scalar(dte[:], dte[:], 1.0, None, ALU.add).then_inc(dt_one, 1)
            v.wait_ge(conv_exp, 1)
            link(v.tensor_scalar(ex[:], ex[:], 1.0, None, ALU.add))
            link(v.reciprocal(ex[:], ex[:]))
            v.tensor_tensor(xc[:], xc[:], ex[:], ALU.mult).then_inc(conv_silu, 1)
            v.wait_ge(dt_ln, 1)
            link(v.scalar_tensor_tensor(out=dt[:], in0=dtu[:], scalar=0.0, in1=dtl[:], op0=ALU.max, op1=ALU.add))
            v.scalar_tensor_tensor(out=a8[:], in0=dt[:], scalar=-1.0, in1=ea[:].unsqueeze(1).broadcast_to([P, NT, 8]),
                                   op0=ALU.mult, op1=ALU.mult).then_inc(a_ready, 1)
            v.wait_ge(z_exp, 1)
            link(v.tensor_scalar(exz[:], exz[:], 1.0, None, ALU.add))
            link(v.reciprocal(exz[:], exz[:]))
            link(v.tensor_tensor(sz[:], sz[:], exz[:], ALU.mult))
            v.wait_ge(conv_silu, 1)
            for c in range(2):
                for t0, t1, src in ((0, SAMPLE, 0), (SAMPLE, T, SAMPLE + 2)):
                    chain.mark(v.tensor_scalar(y[:, c, t0:t1], xc[:, c, src:src + t1 - t0],
                                               vec[:, V_SD + c:V_SD + c + 1], None, ALU.mult))
            v.wait_ge(cum_done, 1)
            cum = ps[:, 2, 0:40].rearrange("p (d a b) -> p a d b", d=2, a=NT)
            chain.mark(v.tensor_scalar(nac[:].rearrange("p a (d b) -> p a d b", d=2), cum, -1.0, None, ALU.mult))
            for t in range(NT):
                v.wait_ge(bc_done, t + 1)
                for dr, tri in ((0, C_LE), (1, C_GE)):
                    last = v.tensor_tensor(gm[:, t, dr], ps[:, 3:8:4, 0:P],
                                           cst[:, tri:tri + P].unsqueeze(1).broadcast_to([P, 2, P]), ALU.mult)
                last.then_inc(bc_read, 1)
            link(v.memset(state[:, 1], 0.0))
            v.wait_ge(state_loaded, 16)
            v.wait_ge(tok_copied, NT)
            v.wait_ge(a_ready, 1)
            v.wait_ge(bc_read, NT)
            for s, (dr, t) in enumerate(steps):
                heads = slice(4 * dr, 4 * dr + 4)
                lc = last_col(dr)
                along = ps[:, 4, :].rearrange("p (a b) -> p a b", a=4)
                v.tensor_copy(arep[:], a8[:, t, heads].unsqueeze(2).broadcast_to([P, 4, P])).then_inc(rep_ready, 1)
                v.wait_ge(dec_ready, 2 * s + 1)
                v.tensor_tensor(wd[:], along[:, :, lc], nac[:, t, heads], ALU.add).then_inc(wd_ready, 1)
                link(v.tensor_tensor(seg[:], along, nac[:, t, heads].unsqueeze(2).broadcast_to([P, 4, P]), ALU.add))
                v.tensor_scalar(seg[:], seg[:], 0.0, None, ALU.min).then_inc(seg_ready, 1)
                v.wait_ge(w_ready, s + 1)
                link(v.tensor_tensor(we[:], we[:], dt[:, t, heads], ALU.mult))
                link(v.tensor_tensor(xw[:], xtok[:, t, 0:256].rearrange("p (a b) -> p a b", a=4),
                                     we[:].unsqueeze(2).broadcast_to([P, 4, 64]), ALU.mult))
                v.wait_ge(dec_ready, 2 * s + 2)
                for gr in range(2):
                    lo = 64 * gr
                    chain.mark(v.tensor_tensor(cts[lo:lo + 64], e0[lo:lo + 64, 2 * gr:2 * gr + 2, :],
                                               xc[lo:lo + 64, 3, pcol(t):pcol(t) + P].unsqueeze(1).broadcast_to([64, 2, P]), ALU.mult))
                link(v.tensor_tensor(dec[:], dec[:], dt[:, t, heads].unsqueeze(2).broadcast_to([P, 4, P]), ALU.mult))
                v.tensor_tensor(mm[:].rearrange("p (a b) c -> p a b c", a=2), dec[:].rearrange("p (a b) c -> p a b c", a=2),
                                gm[:, t, dr].unsqueeze(2).broadcast_to([P, 2, 2, P]), ALU.mult).then_inc(mix_ready, 1)
                v.wait_ge(y_done, s + 1)
                yt = y[:, :, t * P:(t + 1) * P]
                v.tensor_tensor(yt, yt, ps[:, 5:8:2, 0:P], ALU.add).then_inc(y_added, 1)
                for gr in range(2):
                    lo = 64 * gr
                    for m in range(2):
                        hd = 2 * gr + m
                        st = state[lo:lo + 64, t // 4, dr, m, :]
                        ins = v.scalar_tensor_tensor(out=st, in0=st, scalar=e0[lo:lo + 64, hd, lc:lc + 1],
                                                     in1=ps[lo:lo + 64, 6, 64 * hd:64 * hd + 64], op0=ALU.mult, op1=ALU.add)
                        if hd == 3:
                            ins.then_inc(y_added, 1)
                        else:
                            chain.mark(ins)
                v.wait_ge(y_added, 2 * s + 2)
            v.tensor_tensor(y[:], y[:], sz[:], ALU.mult).then_inc(gated_ready, 1)
            v.wait_ge(ysum_done, 1)
            v.tensor_scalar(yms[:], ps[:, 0:2].rearrange("p a b -> p (a b)")[:, 0:T], 1.0 / 256, EPS, ALU.mult, ALU.add).then_inc(yms_ready, 1)
            v.wait_ge(yroot_ready, 1)
            link(v.reciprocal(yrstd[:], yroot[:]))
            for c in range(2):
                chain.mark(v.scalar_tensor_tensor(out=br[:, 3, c, :], in0=y[:, c, :], scalar=vec[:, V_SG + c:V_SG + c + 1],
                                                  in1=yrstd[:], op0=ALU.mult, op1=ALU.mult))


def merge(nc, io, g, layer):
    ps, x, h, br, mod = g["ps"], g["x"], g["h"], g["br"], g["mod"]
    RING = 3
    units = [(n, d) for n in range(4) for d in range(KD)]
    NU = len(units)
    chain_total = 2 * NU + (NU - KD)

    def pair(b):
        return ps[:, b:b + 2].rearrange("p a b -> p (a b)")[:, 0:T]

    with stage(nc) as (block, sem, sb):
        w = sb("merge_w", [P, RING, KD, 512])
        wb = sb("merge_wb", [P, 2, 2, D])
        eg = sb("gate_exp", [P, 2, T])
        prod = sb("gate_prod", [P, 2, T])
        mix = sb("mix", [P, KD, T])
        w_loaded = [sem(f"merge_w_loaded{i}") for i in range(RING)]
        wb_loaded = [sem(f"merge_wb_loaded{i}") for i in range(2)]
        gate_done, proj_done, exp_done, gated, out_done, x_added = (
            sem("merge_" + n) for n in ("gate_done", "proj_done", "exp_done", "gated", "out_done", "x_added"))
        chain = Count(sem("merge_vector_chain"))
        w_gate = layer_row(io["w_in"], layer)[:, O_GATE:IN_W].rearrange("(k p) n -> p k n", p=P)
        w_out = layer_row(io["w_out"], layer).rearrange("(k p) n -> p k n", p=P)
        w_branch = layer_row(io["w_branch"], layer).rearrange("n (k p) d -> n p k d", p=P)

        @block.sync
        def _(sp):
            for i in range(10):
                if i >= RING:
                    sp.wait_ge(proj_done, 4 * (i - RING + 1))
                src = w_gate[:, :, i * 512:(i + 1) * 512] if i < 8 else w_out[:, :, (i - 8) * 512:(i - 7) * 512]
                sp.dma_start(w[:, i % RING], src).then_inc(w_loaded[i % RING], 16)
                if i < 8 and i % 2 == 0:
                    n = i // 2
                    if n >= 2:
                        sp.wait_ge(proj_done, 8 * (n - 1))
                    sp.dma_start(wb[:, n % 2], w_branch[n]).then_inc(wb_loaded[n % 2], 16)

        @block.tensor
        def _(pe):
            for u, (n, d) in enumerate(units):
                i = 2 * n + d // 4
                if d % 4 == 0:
                    pe.wait_ge(w_loaded[i % RING], 16 * (i // RING + 1))
                if d == 0:
                    pe.wait_ge(wb_loaded[n % 2], 16 * (n // 2 + 1))
                if u >= 2:
                    pe.wait_ge(exp_done, u - 1)
                for a, z, o in ((0, SAMPLE, 0), (SAMPLE, T, 1)):
                    for k in range(KD):
                        last = pe.matmul(ps[:, 2 * (u % 2) + o, 0:z - a], w[:, i % RING, k, (d % 4) * P:(d % 4 + 1) * P],
                                         h[:, k, a:z], start=(k == 0), stop=(k == KD - 1))
                last.then_inc(gate_done, 1)
                if u >= 2:
                    pe.wait_ge(gated, u - 1)
                for a, z, o in ((0, SAMPLE, 0), (SAMPLE, T, 1)):
                    for k in range(2):
                        last = pe.matmul(ps[:, 4 + 2 * (u % 2) + o, 0:z - a], wb[:, n % 2, k, d * P:(d + 1) * P],
                                         br[:, n, k, a:z], start=(k == 0), stop=(k == 1))
                last.then_inc(proj_done, 1)
            pe.wait_ge(chain.sem, chain_total)
            pe.wait_ge(gated, NU)
            for d in range(KD):
                i = 8 + d // 4
                if d % 4 == 0:
                    pe.wait_ge(w_loaded[i % RING], 16 * (i // RING + 1))
                if d >= 4:
                    pe.wait_ge(x_added, d - 3)
                for a, z, o in ((0, SAMPLE, 0), (SAMPLE, T, 1)):
                    for k in range(KD):
                        last = pe.matmul(ps[:, 2 * (d % 4) + o, 0:z - a], w[:, i % RING, k, (d % 4) * P:(d % 4 + 1) * P],
                                         mix[:, k, a:z], start=(k == 0), stop=(k == KD - 1))
                last.then_inc(out_done, 1)

        @block.scalar
        def _(act):
            for u in range(NU):
                act.wait_ge(gate_done, u + 1)
                if u >= 2:
                    act.wait_ge(gated, u - 1)
                act.activation(eg[:, u % 2], pair(2 * (u % 2)), ACT.Exp, scale=-1.0).then_inc(exp_done, 1)

        @block.vector
        def _(v):
            for u, (n, d) in enumerate(units):
                v.wait_ge(exp_done, u + 1)
                chain.link(v, v.tensor_scalar(eg[:, u % 2], eg[:, u % 2], 1.0, None, ALU.add))
                chain.link(v, v.reciprocal(eg[:, u % 2], eg[:, u % 2]))
                v.wait_ge(proj_done, u + 1)
                dst = mix[:, d] if n == 0 else prod[:, u % 2]
                v.tensor_tensor(dst, pair(4 + 2 * (u % 2)), eg[:, u % 2], ALU.mult).then_inc(gated, 1)
                if n:
                    v.wait_ge(gated, u + 1)
                    chain.mark(v.tensor_tensor(mix[:, d], mix[:, d], prod[:, u % 2], ALU.add))
            assert chain.n == chain_total
            for d in range(KD):
                v.wait_ge(out_done, d + 1)
                for grp, a, z in GROUPS:
                    last = v.scalar_tensor_tensor(out=x[:, d, a:z], in0=ps[:, 2 * (d % 4) + grp, 0:z - a],
                                                  scalar=mod[:, 16 + d, grp:grp + 1], in1=x[:, d, a:z], op0=ALU.mult, op1=ALU.add)
                last.then_inc(x_added, 1)


def router(nc, io, g, layer):
    ps, cst, h, htok, pos, aff = g["ps"], g["cst"], g["h"], g["htok"], g["pos"], g["aff"]
    with stage(nc) as (block, sem, sb):
        rw = sb("router_w", [P, KD, NE])
        mx = sb("aff_max", [P, NT])
        e = sb("aff_exp", [P, NT, NE])
        su = sb("aff_sum", [P, NT])
        rc = sb("aff_rec", [P, NT])
        left = sb("aff_left", [NE, T])
        top = sb("aff_top", [NE, 8])
        chosen = sb("chosen", [NE, T])
        ones = sb("scan_ones", [NE, T])
        cum = sb("chosen_cum", [NE, T])
        slot = sb("slot", [NE, T])
        rw_loaded, logits_done, tok_turned, tok_copied, arg_ready, exp_done, aff_ready, aff_turned, slot_ready, slot_turned = (
            sem("router_" + n) for n in ("w_loaded", "logits_done", "tok_turned", "tok_copied", "arg_ready", "exp_done",
                                         "aff_ready", "aff_turned", "slot_ready", "slot_turned"))
        chain = Count(sem("router_vector_chain"))

        @block.sync
        def _(sp):
            sp.dma_start(rw[:], layer_row(io["router_w"], layer).rearrange("(k p) n -> p k n", p=P)).then_inc(rw_loaded, 16)

        @block.tensor
        def _(pe):
            pe.wait_ge(rw_loaded, 16)
            for t in range(NT):
                for k in range(KD):
                    last = pe.matmul(ps[:, 6, NE * t:NE * t + NE], h[:, k, t * P:(t + 1) * P], rw[:, k, :],
                                     start=(k == 0), stop=(k == KD - 1))
            last.then_inc(logits_done, 1)
            for t in range(NT):
                if t >= 2:
                    pe.wait_ge(tok_copied, t - 1)
                for k in range(KD):
                    last = pe.transpose(ps[:, 2 * (t % 2) + k // 4, (k % 4) * P:(k % 4 + 1) * P],
                                        h[:, k, t * P:(t + 1) * P], cst[:, C_ID:C_ID + P])
                last.then_inc(tok_turned, 1)
            pe.wait_ge(aff_ready, 1)
            for t in range(NT):
                last = pe.transpose(ps[0:NE, 4 + t // 4, (t % 4) * P:(t % 4 + 1) * P], aff[:, t, 0:NE], cst[:, C_ID:C_ID + P])
            last.then_inc(aff_turned, 1)
            pe.wait_ge(slot_ready, 1)
            for t in range(NT):
                last = pe.transpose(ps[:, 7, NE * t:NE * t + NE], slot[:, t * P:(t + 1) * P], cst[0:NE, C_ID:C_ID + NE])
            last.then_inc(slot_turned, 1)

        @block.scalar
        def _(act):
            act.wait_ge(arg_ready, 1)
            act.activation(e[:], e[:], ACT.Exp).then_inc(exp_done, 1)
            for t in range(NT):
                act.wait_ge(tok_turned, t + 1)
                act.activation(htok[:, t, :], ps[:, 2 * (t % 2):2 * (t % 2) + 2].rearrange("p a b -> p (a b)"),
                               ACT.Copy).then_inc(tok_copied, 1)

        @block.vector
        def _(v):
            link = lambda ins: chain.link(v, ins)
            logits = ps[:, 6, 0:NT * NE].rearrange("p (a b) -> p a b", a=NT)
            chain.mark(v.memset(pos[:, :, NE:NE + 1], -1.0))
            chain.mark(v.memset(aff[:, :, NE:NE + 1], 0.0))
            chain.mark(v.memset(ones[:], 1.0))
            v.wait_ge(logits_done, 1)
            link(v.tensor_reduce(mx[:], logits, AXX, ALU.max))
            v.tensor_tensor(e[:], logits, mx[:].unsqueeze(2).broadcast_to([P, NT, NE]), ALU.subtract).then_inc(arg_ready, 1)
            v.wait_ge(exp_done, 1)
            link(v.tensor_reduce(su[:], e[:], AXX, ALU.add))
            link(v.reciprocal(rc[:], su[:]))
            v.tensor_tensor(aff[:, :, 0:NE], e[:], rc[:].unsqueeze(2).broadcast_to([P, NT, NE]), ALU.mult).then_inc(aff_ready, 1)
            v.wait_ge(aff_turned, 1)
            link(v.tensor_copy(left[:], ps[0:NE, 4:6].rearrange("p a b -> p (a b)")[:, 0:T]))
            for a, z, cap, off in ((0, SAMPLE, CAP_S, 0.0), (SAMPLE, T, CAP_P, float(CAP_S))):
                for _r in range(cap // 8):
                    link(v.max(out=top[:], in_=left[:, a:z]))
                    link(v.match_replace(out=left[:, a:z], in_to_replace=top[:], in_values=left[:, a:z], imm_value=-1.0))
                link(v.tensor_scalar(chosen[:, a:z], left[:, a:z], 0.0, None, ALU.is_lt))
                link(v.tensor_tensor_scan(cum[:, a:z], ones[:, a:z], chosen[:, a:z], 0.0, ALU.mult, ALU.add))
                link(v.scalar_tensor_tensor(out=slot[:, a:z], in0=cum[:, a:z], scalar=off, in1=chosen[:, a:z],
                                            op0=ALU.add, op1=ALU.mult))
            v.tensor_scalar(slot[:], slot[:], -1.0, None, ALU.add).then_inc(slot_ready, 1)
            v.wait_ge(slot_turned, 1)
            chain.mark(v.tensor_copy(pos[:, :, 0:NE], ps[:, 7, 0:NT * NE].rearrange("p (a b) -> p a b", a=NT)))


class LoopCount:

    def __init__(self, sem, i, per, base=0):
        self.sem, self.i, self.per, self.base, self.n = sem, i, per, base, 0

    def mark(self, ins):
        self.n += 1
        ins.then_inc(self.sem, 1)

    def link(self, eng, ins):
        self.mark(ins)
        eng.wait_ge(self.sem, self.i * self.per + (self.base + self.n))


def experts(nc, io, g, layer):
    ps, cst, x, acc, htok, pos, aff, mod = (g[n] for n in ("ps", "cst", "x", "h", "htok", "pos", "aff", "mod"))

    def pair(b, rows, n):
        return ps[0:rows, b:b + 2].rearrange("p a b -> p (a b)")[:, 0:n]

    with stage(nc) as (block, sem, sb):
        wg = sb("exp_wg", [P, KD, FF])
        wu = sb("exp_wu", [P, KD, FF])
        wd = sb("exp_wd", [P, KD, D])
        pc = sb("pos_col", [P, NT])
        fc = sb("aff_col", [P, NT])
        pick = sb("pick", [P, NT, SLOTS])
        give = sb("give", [P, NT, SLOTS])
        give_t = sb("give_turned", [SLOTS, T])
        xe = sb("xe", [SLOTS, D])
        xet = sb("xe_turned", [P, KD, SLOTS])
        hid = sb("hid", [SLOTS, FF])
        hidt = sb("hid_turned", [P, KD, SLOTS])
        ye = sb("ye", [SLOTS, D])
        wg_loaded, wu_loaded, wd_loaded = sem("wg_loaded"), sem("wu_loaded"), sem("wd_loaded")
        (picks_ready, gathered, gives_turned, xe_copied, give_copied, xe_turned, xet_copied, gate_done, up_done, gate_exp,
         hid_ready, hid_turned, hidt_copied, down_done, ye_copied, chunk_scattered, chunk_added) = (
            sem("exp_" + n) for n in (
                "picks_ready", "gathered", "gives_turned", "xe_copied", "give_copied", "xe_turned", "xet_copied", "gate_done",
                "up_done", "gate_exp", "hid_ready", "hid_turned", "hidt_copied", "down_done", "ye_copied", "chunk_scattered",
                "chunk_added"))
        chain_sem = sem("exp_vector_chain")

        def expert_w(name, e):
            a = io[name][bass.ds(layer, 1), bass.ds(e, 1)] if not isinstance(e, int) else io[name][bass.ds(layer, 1), e:e + 1]
            return a.rearrange("l e (k p) n -> p (l e k) n", p=P)

        @block.sync
        def _(sp):
            def load(e, first):
                for buf, name, used, loaded in ((wg, "exp_w_gate", gate_done, wg_loaded), (wu, "exp_w_up", up_done, wu_loaded),
                                                (wd, "exp_w_down", down_done, wd_loaded)):
                    if not first:
                        sp.wait_ge(used, e)
                    sp.dma_start(buf[:], expert_w(name, e)).then_inc(loaded, 16)

            load(0, True)
            with sp.Fori(1, NE) as e:
                load(e, False)

        @block.tensor
        def _(pe):
            with pe.Fori(0, NE) as e:
                pe.wait_ge(picks_ready, e + 1)
                for half in range(2):
                    for t in range(NT):
                        last = pe.matmul(ps[0:SLOTS, half, :], pick[:, t, :], htok[:, t, half * 512:(half + 1) * 512],
                                         start=(t == 0), stop=(t == NT - 1))
                last.then_inc(gathered, 1)
                for t in range(NT):
                    last = pe.transpose(ps[0:SLOTS, 2 + t // 4, (t % 4) * P:(t % 4 + 1) * P], give[:, t, :], cst[:, C_ID:C_ID + P])
                last.then_inc(gives_turned, 1)
                pe.wait_ge(xe_copied, e + 1)
                for k in range(KD):
                    last = pe.transpose(ps[:, k // 4, (k % 4) * SLOTS:(k % 4 + 1) * SLOTS], xe[:, k * P:(k + 1) * P],
                                        cst[0:SLOTS, C_ID:C_ID + SLOTS])
                last.then_inc(xe_turned, 1)
                pe.wait_ge(xet_copied, e + 1)
                for w, loaded, done, b in ((wg, wg_loaded, gate_done, 4), (wu, wu_loaded, up_done, 6)):
                    pe.wait_ge(loaded, 16 * e + 16)
                    for half in range(2):
                        for k in range(KD):
                            last = pe.matmul(ps[0:SLOTS, b + half, :], xet[:, k, :], w[:, k, half * 512:(half + 1) * 512],
                                             start=(k == 0), stop=(k == KD - 1))
                    last.then_inc(done, 1)
                pe.wait_ge(hid_ready, e + 1)
                for k in range(KD):
                    last = pe.transpose(ps[:, k // 4, (k % 4) * SLOTS:(k % 4 + 1) * SLOTS], hid[:, k * P:(k + 1) * P],
                                        cst[0:SLOTS, C_ID:C_ID + SLOTS])
                last.then_inc(hid_turned, 1)
                pe.wait_ge(hidt_copied, e + 1)
                pe.wait_ge(give_copied, e + 1)
                pe.wait_ge(wd_loaded, 16 * e + 16)
                for half in range(2):
                    for k in range(KD):
                        last = pe.matmul(ps[0:SLOTS, 2 + half, :], hidt[:, k, :], wd[:, k, half * 512:(half + 1) * 512],
                                         start=(k == 0), stop=(k == KD - 1))
                last.then_inc(down_done, 1)
                pe.wait_ge(ye_copied, e + 1)
                for k in range(KD):
                    if k >= 2:
                        pe.wait_ge(chunk_added, e * KD + (k - 1))
                    b = 4 + 2 * (k % 2)
                    pe.matmul(ps[:, b, :], ye[:, k * P:(k + 1) * P], give_t[:, 0:SAMPLE], start=True, stop=True)
                    pe.matmul(ps[:, b + 1, 0:PROMPT], ye[:, k * P:(k + 1) * P], give_t[:, SAMPLE:T],
                              start=True, stop=True).then_inc(chunk_scattered, 1)
                pe.wait_ge(chunk_added, e * KD + KD)

        @block.scalar
        def _(act):
            with act.Fori(0, NE) as e:
                act.wait_ge(gathered, e + 1)
                act.activation(xe[:], pair(0, SLOTS, D), ACT.Copy).then_inc(xe_copied, 1)
                act.wait_ge(gives_turned, e + 1)
                act.activation(give_t[:], pair(2, SLOTS, T), ACT.Copy).then_inc(give_copied, 1)
                act.wait_ge(gate_done, e + 1)
                act.activation(hid[:], pair(4, SLOTS, FF), ACT.Exp, scale=-1.0).then_inc(gate_exp, 1)
                act.wait_ge(down_done, e + 1)
                act.activation(ye[:], pair(2, SLOTS, D), ACT.Copy).then_inc(ye_copied, 1)

        @block.vector
        def _(v):
            def picks(e, chain):
                if isinstance(e, int):
                    pcol_, acol = pos[:, :, e:e + 1], aff[:, :, e:e + 1]
                else:
                    pcol_, acol = pos[:, :, bass.ds(e, 1)], aff[:, :, bass.ds(e, 1)]
                chain.mark(v.tensor_copy(pc[:].unsqueeze(2), pcol_))
                chain.link(v, v.tensor_copy(fc[:].unsqueeze(2), acol))
                chain.link(v, v.tensor_tensor(pick[:], cst[:, C_SLOT:C_SLOT + SLOTS].unsqueeze(1).broadcast_to([P, NT, SLOTS]),
                                              pc[:].unsqueeze(2).broadcast_to([P, NT, SLOTS]), ALU.is_equal))
                v.tensor_tensor(give[:], pick[:], fc[:].unsqueeze(2).broadcast_to([P, NT, SLOTS]), ALU.mult).then_inc(picks_ready, 1)

            start = LoopCount(chain_sem, 0, 0)
            start.mark(v.memset(acc[:], 0.0))
            picks(0, start)
            with v.Fori(0, NE) as e:
                chain = LoopCount(chain_sem, e, 6, base=start.n)
                v.wait_ge(xe_turned, e + 1)
                v.tensor_copy(xet[:].rearrange("p (a b) c -> p a (b c)", a=2), ps[:, 0:2, 0:4 * SLOTS]).then_inc(xet_copied, 1)
                v.wait_ge(gives_turned, e + 1)
                picks(e + 1, chain)
                v.wait_ge(gate_exp, e + 1)
                chain.link(v, v.tensor_scalar(hid[:], hid[:], 1.0, None, ALU.add))
                chain.link(v, v.reciprocal(hid[:], hid[:]))
                chain.link(v, v.tensor_tensor(hid[:], hid[:], pair(4, SLOTS, FF), ALU.mult))
                v.wait_ge(up_done, e + 1)
                v.tensor_tensor(hid[:], hid[:], pair(6, SLOTS, FF), ALU.mult).then_inc(hid_ready, 1)
                v.wait_ge(hid_turned, e + 1)
                v.tensor_copy(hidt[:].rearrange("p (a b) c -> p a (b c)", a=2), ps[:, 0:2, 0:4 * SLOTS]).then_inc(hidt_copied, 1)
                for k in range(KD):
                    v.wait_ge(chunk_scattered, e * KD + (k + 1))
                    v.tensor_tensor(acc[:, k, :], acc[:, k, :], pair(4 + 2 * (k % 2), P, T), ALU.add).then_inc(chunk_added, 1)
                assert chain.n == chain.per
            v.wait_ge(chunk_added, KD * NE)
            for k in range(KD):
                for grp, a, z in GROUPS:
                    last = v.scalar_tensor_tensor(out=x[:, k, a:z], in0=acc[:, k, a:z], scalar=mod[:, 40 + k, grp:grp + 1],
                                                  in1=x[:, k, a:z], op0=ALU.mult, op1=ALU.add)
            last.then_inc(chain_sem, 1)


def finish(nc, io, g):
    norm(nc, g, "nf", g["fin"], None)
    with stage(nc) as (block, sem, sb):
        y_out = sem("y_out")

        @block.sync
        def _(sp):
            sp.dma_start(io["y"], g["h"][:]).then_inc(y_out, 16)
            sp.wait_ge(y_out, 16)


def constants():
    c = np.zeros((P, C_END), np.float32)
    i, j = np.arange(P)[:, None], np.arange(P)[None, :]
    c[:, C_ID:C_ID + P] = i == j
    c[:, C_LE:C_LE + P] = i <= j
    c[:, C_GE:C_GE + P] = i >= j
    c[:, C_ROT:C_ROT + P] = np.where((i == j + 1) & (j % 2 == 0), -1.0, 0.0) + np.where((i == j - 1) & (j % 2 == 1), 1.0, 0.0)
    c[:, C_BLK:C_BLK + P] = i // 64 == j // 64
    c[:, C_ONE:C_ONE + P] = 1.0
    c[:, C_SLOT:C_SLOT + SLOTS] = np.arange(SLOTS)
    col, kc = np.arange(P)[:, None] % GRID_W, np.arange(GRID_W)[None, :]
    start = np.clip(col - 8, 0, GRID_W - 16)
    c[:, C_WIN:C_WIN + GRID_W] = np.where((kc >= start) & (kc < start + 16), 0.0, -1e30)
    quarter = ROPE // 4
    inv = (10000.0 ** (-np.arange(quarter, dtype=np.float32) / quarter)).astype(np.float32)
    f = (np.arange(P) % ROPE) // 2
    tok = np.arange(SAMPLE)
    at = np.where(f[:, None] < quarter, (tok // GRID_W)[None, :], (tok % GRID_W)[None, :]).astype(np.float32)
    angle = at * inv[f % quarter][:, None]
    c[:, C_COS:C_COS + SAMPLE] = np.cos(angle)
    c[:, C_SIN:C_SIN + SAMPLE] = np.sin(angle)
    return c


def lay_out(a):
    L = DEPTH

    def feat(x, chunks):
        return x.reshape(x.shape[0], chunks, P).transpose(2, 1, 0)

    def cols(x):
        return x.reshape(L, -1, P).transpose(0, 2, 1)

    def everywhere(x):
        x = x.reshape(L, 1, -1)
        return np.broadcast_to(x, (L, P, x.shape[2]))

    o = {"cst": constants()}
    o["x"] = feat(np.concatenate([a["x_sample"][0], a["x_prompt"][0]]), KD)
    o["cond"] = feat(np.stack([a["c"][0], a["c_ctx"]]), KD)
    o["fin"] = a["final_norm_g"].reshape(KD, P).T
    lam_init = np.array([[0.8 - 0.6 * math.exp(-0.3 * i), 1.0 - (0.8 - 0.6 * math.exp(-0.3 * i))] for i in range(L)], np.float32)
    cw = a["ssm_conv_w"].reshape(L, 3, 4, P).transpose(0, 3, 1, 2).reshape(L, P, 12)
    o["vec"] = np.concatenate([
        cols(a["mod_b"]), cols(a["norm1_g"]), cols(a["norm2_g"]), cols(a["mla_q_norm_g"]), cols(a["mla_kv_norm_g"]),
        np.tile(a["df_subln_g"], (1, 2))[:, :, None], cw, cols(a["ssm_conv_b"]), everywhere(a["ssm_dt_bias"]),
        everywhere(a["ssm_a_log"]), cols(np.repeat(a["ssm_d"], 64, axis=1)), cols(a["ssm_norm_g"]),
        everywhere(a["df_lambda"]), everywhere(lam_init)], axis=2)
    w = a["w_in"]
    part = lambda first, n: w[:, :, first:first + n]
    o["w_mix"] = np.concatenate([part(O_NAQ, 256), part(O_NAK, 256), part(O_CQ, QR), part(O_CKV, KVR)]
                                + [part(O_KR, ROPE)] * 4
                                + [part(O_DFQ, 256), part(O_DFK, 256), part(O_SX, 256), part(O_SB, P), part(O_SC, P),
                                   part(O_SZ, 256), part(O_NAV, 256), part(O_DFV, 256), part(O_DT, 8)], axis=2)
    uq = a["mla_w_uq"].reshape(L, QR, HEADS, 96)
    o["w_uq"] = np.concatenate([uq[..., :64].reshape(L, QR, 256), uq[..., 64:].reshape(L, QR, 128)], axis=2)
    ukv = a["mla_w_ukv"].reshape(L, KVR, HEADS, 128)
    o["w_ukv"] = np.concatenate([ukv[..., :64].reshape(L, KVR, 256), ukv[..., 64:].reshape(L, KVR, 256)], axis=2)
    rows = []
    for i in range(L):
        rows.append(np.concatenate([
            feat(a["cache_na_k"][0, i].reshape(CTX, 256), 2), feat(a["cache_df_k"][0, i].reshape(CTX, 256), 2),
            feat(a["cache_mla_ckv"][0, i], 2), feat(np.tile(a["cache_mla_krope"][0, i], (1, 4)), 1)], axis=1))
    o["ctx_k"] = np.stack(rows)
    o["ctx_v"] = np.concatenate([a["cache_na_v"][0].reshape(L, CTX, 256), a["cache_df_v"][0].reshape(L, CTX, 256)], axis=2)
    o["state"] = a["state_ssm"][0].reshape(L, 2, 2, 2, 64, 64).transpose(0, 2, 5, 1, 3, 4).reshape(L, P, 2, 2, 64)
    rel = np.zeros((L, HEADS, 17, 2 * GRID_W), a["na_rel_bias"].dtype)
    rel[:, :, 1:16, BIAS_MID - 15:BIAS_MID + 16] = a["na_rel_bias"]
    bias = np.zeros((L, P, HEADS, 16, GRID_W), rel.dtype)
    for c in range(GRID_W):
        bias[:, c] = rel[:, :, 1:17, BIAS_MID - c:BIAS_MID - c + GRID_W]
        bias[:, GRID_W + c] = rel[:, :, 0:16, BIAS_MID - c:BIAS_MID - c + GRID_W]
    o["bias"] = bias
    for n in ("mod_w", "w_in", "w_out", "w_branch", "router_w", "exp_w_gate", "exp_w_up", "exp_w_down"):
        o[n] = a[n]
    return {n: np.ascontiguousarray(v) for n, v in o.items()}


OUTS = {"y": (P, KD, T), "new_k": (DEPTH, P, K_N, PROMPT), "new_v": (DEPTH, PROMPT, 512), "new_state": (DEPTH, P, 2, 2, 64)}


def collect(r):
    y, nk, nv, ns = (np.asarray(r[f"out_{n}"]) for n in OUTS)
    L = DEPTH
    y = y.transpose(2, 1, 0).reshape(T, D)

    def keys(first, n):
        return nk[:, :, first:first + n].transpose(0, 3, 2, 1).reshape(1, L, PROMPT, n * P)

    state = ns.reshape(L, 2, 64, 2, 2, 64).transpose(0, 3, 1, 4, 5, 2).reshape(1, L, 2, HEADS, 64, 64)
    return (y[None, SAMPLE:], y[None, :SAMPLE], keys(K_NA, 2).reshape(1, L, PROMPT, HEADS, 64),
            nv[:, :, :256].reshape(1, L, PROMPT, HEADS, 64), keys(K_CKV, 2), keys(K_KR, 1)[..., :ROPE],
            keys(K_DF, 2).reshape(1, L, PROMPT, HEADS, 2, 32), nv[:, :, 256:].reshape(1, L, PROMPT, HEADS, 64), state)


def kernel(**inputs):
    import concourse.bacc as bacc
    from concourse.bass_utils import run_bass_kernel_spmd

    arrays = lay_out({n: np.asarray(v) for n, v in inputs.items()})
    nc = bacc.Bacc("TRN2", target_bir_lowering=False, num_devices=1)
    io = {n: nc.dram_tensor(f"in_{n}", a.shape, mybir.dt.from_np(a.dtype), kind="ExternalInput").ap() for n, a in arrays.items()}
    for n, shape in OUTS.items():
        io[n] = nc.dram_tensor(f"out_{n}", shape, F32, kind="ExternalOutput").ap()
    build(nc, io)
    r = run_bass_kernel_spmd(nc, [{f"in_{n}": a for n, a in arrays.items()}], core_ids=[0])
    return tuple(np.ascontiguousarray(v) for v in collect(r.results[0]))
```

```python
import math
from contextlib import ExitStack, contextmanager

import numpy as np

import concourse.bass as bass
from concourse import mybir

F32 = mybir.dt.float32
F32R = mybir.dt.float32r
ALU = mybir.AluOpType
ACT = mybir.ActivationFunctionType
AXX = mybir.AxisListType.X

P = 128
D = 1024
KD = D // P
SAMPLE, PROMPT, CTX = 512, 128, 128
T = SAMPLE + PROMPT
NT = T // P
KEYS = SAMPLE + CTX + PROMPT
OWN_P = SAMPLE + CTX
DEPTH = 2
GRID_W = 64
ROWS = SAMPLE // GRID_W
EPS = 1e-6
HEADS = 4
NE = 16
FF = 1024
CAP_S, CAP_P = 2 * SAMPLE // NE, 2 * PROMPT // NE
SLOTS = CAP_S + CAP_P
QR, KVR, ROPE = 384, 256, 32
NA_DY, NA_DX = 15, 31
BIAS_W = 128
BIAS_MID = GRID_W - 1
O_NAQ, O_NAK, O_NAV, O_CQ, O_CKV, O_KR = 0, 256, 512, 768, 1152, 1408
O_DFQ, O_DFK, O_DFV, O_SX, O_SZ, O_SB, O_SC, O_DT, O_GATE = 1440, 1696, 1952, 2208, 2464, 2720, 2848, 2976, 2984
IN_W = O_GATE + 4 * D
GROUPS = ((0, 0, SAMPLE), (1, SAMPLE, T))


class Count:

    def __init__(self, sem):
        self.sem, self.n = sem, 0

    def mark(self, ins):
        self.n += 1
        ins.then_inc(self.sem, 1)
        return self.n

    def link(self, eng, ins):
        self.mark(ins)
        eng.wait_ge(self.sem, self.n)


class Load:

    def __init__(self, sem):
        self.sem, self.n = sem, 0

    def start(self, eng, out, in_):
        self.n += 1
        eng.dma_start(out, in_).then_inc(self.sem, 16)

    @property
    def total(self):
        return 16 * self.n


@contextmanager
def stage(nc):
    with ExitStack() as own:
        sems = []

        def sem(name):
            s = own.enter_context(nc.semaphore(name))
            sems.append(s.num)
            return s

        def sb(name, shape, dt=F32):
            return own.enter_context(nc.sbuf_tensor(name, shape, dt))

        block = ExitStack()
        b = block.enter_context(nc.Block())
        yield b, sem, sb
        block.close()
        nc.all_engine_barrier(sems_to_clear=range(min(sems), max(sems) + 1))


def layer_row(ap, layer):
    names = " ".join(f"d{i}" for i in range(len(ap.shape) - 1))
    first, rest = ("d0", names.split(" ", 1)[1] if " " in names else "")
    return ap[bass.ds(layer, 1)].rearrange(f"l {names} -> (l {first}) {rest}".strip())


def chunk_columns(vec):
    return vec.rearrange("(c p) -> p c", p=P)


C_ID, C_LE, C_GE, C_ROT, C_BLK, C_ONE, C_SLOT, C_WIN = 0, 128, 256, 384, 512, 640, 768, 768 + SLOTS
C_COS = C_WIN + GRID_W
C_SIN = C_COS + SAMPLE
C_TOK = C_SIN + SAMPLE
C_END = C_TOK + NT
V_MODB, V_N1, V_N2, V_QG, V_KVG, V_SUB, V_CW, V_CB, V_DTB, V_ALOG, V_SD, V_SG, V_LAM = (
    0, 48, 56, 64, 67, 69, 70, 82, 86, 94, 102, 104, 106)
V_LI = V_LAM + 128
V_END = V_LI + 2
FEATURE_CHUNKS = 20
M_V = FEATURE_CHUNKS * P
M_DT = M_V + 512
M_END = M_DT + 8
K_NA, K_DF, K_CKV, K_KR, K_N = 0, 2, 4, 6, 7
SXW = T + 4
SX_S, SX_P = 1, SAMPLE + 3


def pcol(t):
    return t * P if t < NT - 1 else SAMPLE + 2


def build(nc, io):
    with ExitStack() as whole:
        def sb(name, shape, dt=F32):
            return whole.enter_context(nc.sbuf_tensor(name, shape, dt))

        g = {}
        g["ps"] = whole.enter_context(nc.psum_tensor("ps", [P, 8, 512], F32))
        g["cst"] = sb("cst", [P, C_END])
        g["x"] = sb("x", [P, KD, T])
        g["h"] = sb("h", [P, KD, T])
        g["vec"] = sb("vec", [P, V_END])
        g["cond"] = sb("cond", [P, KD, 2])
        g["mod"] = sb("mod", [P, 48, 2])
        g["gs1"] = sb("gs1", [P, KD, 2])
        g["gs2"] = sb("gs2", [P, KD, 2])
        g["fin"] = sb("fin", [P, KD])
        g["xe_loaded"] = [whole.enter_context(nc.semaphore(f"xe_loaded{i}")) for i in range(2)]
        g["rows_added"] = whole.enter_context(nc.semaphore("rows_added"))
        begin(nc, io, g)
        with nc.Fori(0, DEPTH) as layer:
            modulation(nc, io, g, layer)
            norm(nc, g, "n1", g["gs1"], g["mod"][:, 0:8, :])
            with ExitStack() as mix:
                def mb(name, shape, dt=F32):
                    g[name] = mix.enter_context(nc.sbuf_tensor(name, shape, dt))

                mb("br", [P, 4, 2, T])
                with ExitStack() as heads:
                    def hb(name, shape, dt=F32):
                        g[name] = heads.enter_context(nc.sbuf_tensor(name, shape, dt))

                    hb("kt", [P, K_N, KEYS])
                    hb("qt", [P, 4, T])
                    hb("v", [P, 6, 512])
                    hb("sx", [P, 4, SXW])
                    hb("sz", [P, 2, T])
                    hb("dtr", [P, NT, 8])
                    with ExitStack() as lat:
                        for name, shape in (("cq", [P, 3, T]), ("qn", [P, 2, T]), ("qr", [P, T]),
                                            ("kn", [P, 2, KEYS]), ("mv", [P, 6, 256])):
                            g[name] = lat.enter_context(nc.sbuf_tensor(name, shape, F32))
                        projections(nc, io, g, layer)
                        latent_heads(nc, io, g, layer)
                        attention(nc, io, g, layer)
                    ssm(nc, io, g, layer)
                merge(nc, io, g, layer)
            norm(nc, g, "n2", g["gs2"], g["mod"][:, 24:32, :])
            with ExitStack() as moe:
                for name, shape, dt in (("rows", [SLOTS, NE], mybir.dt.uint32), ("weight", [SLOTS, NE], F32)):
                    g[name] = moe.enter_context(nc.sbuf_tensor(name, shape, dt))
                with ExitStack() as route:
                    for name, shape in (("htok", [P, NT, D]), ("pos", [P, NT, NE]), ("aff", [P, NT, NE])):
                        g[name] = route.enter_context(nc.sbuf_tensor(name, shape, F32))
                    router(nc, io, g, layer)
                    choose(nc, io, g)
                experts(nc, io, g, layer)
            add_experts(nc, io, g)
        finish(nc, io, g)


def begin(nc, io, g):
    with stage(nc) as (block, sem, sb):
        start_loads = Load(sem("start_loads"))

        @block.sync
        def _(sp):
            start_loads.start(sp, g["cst"][:], io["cst"])
            start_loads.start(sp, g["x"][:], io["x"])
            start_loads.start(sp, g["cond"][:], io["cond"])
            start_loads.start(sp, g["fin"][:], io["fin"])
            sp.wait_ge(start_loads.sem, start_loads.total)


def modulation(nc, io, g, layer):
    ps, vec, mod, cst = g["ps"], g["vec"], g["mod"], g["cst"]
    NCH, RING = 12, 4
    with stage(nc) as (block, sem, sb):
        w = sb("mod_w", [P, RING, KD, 512])
        th = sb("mod_tanh", [P, KD, 2])
        th2 = sb("mod_tanh_gated", [P, KD, 2])
        sc = sb("mod_sc", [P, KD, 2])
        rows = sb("mod_rows", [2, NCH * 512])
        vec_loaded = sem("vec_loaded")
        w_loaded = [sem(f"mod_w_loaded{i}") for i in range(RING)]
        chunk_done, tanh_done, rows_done, cols_done = (sem(n) for n in ("mod_chunk_done", "mod_tanh_done", "mod_rows_done", "mod_cols_done"))
        silu = Count(sem("mod_silu"))
        src = layer_row(io["mod_w"], layer).rearrange("(k p) n -> p k n", p=P)

        @block.sync
        def _(sp):
            sp.dma_start(vec[:], layer_row(io["vec"], layer)).then_inc(vec_loaded, 16)
            for n in range(NCH):
                if n >= RING:
                    sp.wait_ge(chunk_done, n - RING + 1)
                sp.dma_start(w[:, n % RING], src[:, :, n * 512:(n + 1) * 512]).then_inc(w_loaded[n % RING], 16)

        @block.scalar
        def _(act):
            act.activation(th[:], g["cond"][:], ACT.Tanh, scale=0.5).then_inc(tanh_done, 1)

        @block.tensor
        def _(pe):
            pe.wait_ge(silu.sem, 2)

            def columns(n):
                pe.wait_ge(rows_done, n + 1)
                for j in range(4 * n, 4 * n + 4):
                    last = pe.transpose(ps[:, 7, 2 * j:2 * j + 2], rows[:, j * P:(j + 1) * P], cst[0:2, C_ID:C_ID + 2])
                last.then_inc(cols_done, 1)

            for n in range(NCH):
                pe.wait_ge(w_loaded[n % RING], 16 * (n // RING + 1))
                if n >= 4:
                    pe.wait_ge(rows_done, n - 3)
                for k in range(KD):
                    last = pe.matmul(ps[0:2, n % 4, :], sc[:, k, :], w[:, n % RING, k, :],
                                     start=(k == 0), stop=(k == KD - 1))
                last.then_inc(chunk_done, 1)
                if n >= 1:
                    columns(n - 1)
            columns(NCH - 1)

        @block.vector
        def _(v):
            v.wait_ge(tanh_done, 1)
            silu.link(v, v.scalar_tensor_tensor(out=th2[:], in0=th[:], scalar=1.0, in1=g["cond"][:], op0=ALU.add, op1=ALU.mult))
            silu.link(v, v.tensor_scalar(sc[:], th2[:], 0.5, None, ALU.mult))
            for n in range(NCH):
                v.wait_ge(chunk_done, n + 1)
                v.tensor_copy(rows[:, n * 512:(n + 1) * 512], ps[0:2, n % 4, :]).then_inc(rows_done, 1)
            v.wait_ge(cols_done, NCH)
            v.wait_ge(vec_loaded, 16)
            silu.link(v, v.tensor_tensor(mod[:], ps[:, 7, 0:96].rearrange("p (a b) -> p a b", b=2),
                                         vec[:, V_MODB:V_MODB + 48].unsqueeze(2).broadcast_to([P, 48, 2]), ALU.add))
            for gs, first, gain in ((g["gs1"], 8, V_N1), (g["gs2"], 32, V_N2)):
                silu.mark(v.scalar_tensor_tensor(
                    out=gs[:], in0=mod[:, first:first + 8, :], scalar=1.0,
                    in1=vec[:, gain:gain + 8].unsqueeze(2).broadcast_to([P, KD, 2]), op0=ALU.add, op1=ALU.mult))


def norm(nc, g, name, gain, shift):
    ps, x, h, cst = g["ps"], g["x"], g["h"], g["cst"]
    with stage(nc) as (block, sem, sb):
        sq = sb(name + "_sq", [P, 2, T])
        ms = sb(name + "_ms", [P, T])
        root = sb(name + "_root", [P, T])
        rstd = sb(name + "_rstd", [P, T])
        xn = sb(name + "_xn", [P, 2, T])
        sq_ready, sq_used, ms_ready, root_ready, rstd_ready, xn_ready, h_ready = (
            sem(name + s) for s in ("_sq_ready", "_sq_used", "_ms_ready", "_root_ready", "_rstd_ready", "_xn_ready", "_h_ready"))

        @block.scalar
        def _(act):
            for k in range(KD):
                if k >= 2:
                    act.wait_ge(sq_used, k - 1)
                act.activation(sq[:, k % 2], x[:, k], ACT.Square).then_inc(sq_ready, 1)
            act.wait_ge(ms_ready, 1)
            act.activation(root[:], ms[:], ACT.Sqrt).then_inc(root_ready, 1)
            for k in range(KD):
                act.wait_ge(xn_ready, k + 1)
                for grp, a, b in GROUPS:
                    if shift is None:
                        last = act.activation(h[:, k, a:b], xn[:, k % 2, a:b], ACT.Copy)
                    else:
                        last = act.activation(h[:, k, a:b], xn[:, k % 2, a:b], ACT.Identity,
                                              bias=shift[:, k, grp:grp + 1], scale=gain[:, k, grp:grp + 1])
                last.then_inc(h_ready, 1)

        @block.tensor
        def _(pe):
            for k in range(KD):
                pe.wait_ge(sq_ready, k + 1)
                pe.matmul(ps[:, 0, :], cst[:, C_ONE:C_ONE + P], sq[:, k % 2, 0:SAMPLE], start=(k == 0), stop=(k == KD - 1))
                pe.matmul(ps[:, 1, 0:PROMPT], cst[:, C_ONE:C_ONE + P], sq[:, k % 2, SAMPLE:T],
                          start=(k == 0), stop=(k == KD - 1)).then_inc(sq_used, 1)

        @block.vector
        def _(v):
            v.wait_ge(sq_used, KD)
            v.tensor_scalar(ms[:], ps[:, 0:2].rearrange("p a b -> p (a b)")[:, 0:T], 1.0 / D, EPS, ALU.mult, ALU.add).then_inc(ms_ready, 1)
            v.wait_ge(root_ready, 1)
            v.reciprocal(rstd[:], root[:]).then_inc(rstd_ready, 1)
            v.wait_ge(rstd_ready, 1)
            for k in range(KD):
                if k >= 2:
                    v.wait_ge(h_ready, k - 1)
                if shift is None:
                    v.scalar_tensor_tensor(out=xn[:, k % 2], in0=x[:, k], scalar=gain[:, k:k + 1], in1=rstd[:],
                                           op0=ALU.mult, op1=ALU.mult).then_inc(xn_ready, 1)
                else:
                    v.tensor_tensor(xn[:, k % 2], x[:, k], rstd[:], ALU.mult).then_inc(xn_ready, 1)


def projections(nc, io, g, layer):
    ps, h = g["ps"], g["h"]
    kt, qt, v_sb, sx, sz = g["kt"], g["qt"], g["v"], g["sx"], g["sz"]
    RING, LOADS = 3, FEATURE_CHUNKS // 4 + 1

    def key(c):
        return [(kt[:, c, 0:SAMPLE], 0, SAMPLE), (kt[:, c, OWN_P:KEYS], SAMPLE, T)]

    def conv(c):
        return [(sx[:, c, SX_S:SX_S + SAMPLE], 0, SAMPLE), (sx[:, c, SX_P:SX_P + PROMPT], SAMPLE, T)]

    def plain(buf, c):
        return [(buf[:, c, :], 0, T)]

    places = ([plain(qt, 0), plain(qt, 1), key(K_NA), key(K_NA + 1)] + [plain(g["cq"], c) for c in range(3)]
              + [key(K_CKV), key(K_CKV + 1), key(K_KR), plain(qt, 2), plain(qt, 3), key(K_DF), key(K_DF + 1)]
              + [conv(c) for c in range(4)] + [plain(sz, 0), plain(sz, 1)])
    assert len(places) == FEATURE_CHUNKS
    with stage(nc) as (block, sem, sb):
        w = sb("in_w", [P, RING, KD, 512])
        wdt = sb("in_wdt", [P, KD, 8])
        w_loaded = [sem(f"in_w_loaded{i}") for i in range(RING)]
        dt_w_loaded, ctx_loaded, chunk_done, copied_v, copied_a, pads = (
            sem(n) for n in ("dt_w_loaded", "ctx_loaded", "in_chunk_done", "in_copied_vector", "in_copied_scalar", "in_pads"))
        src = layer_row(io["w_mix"], layer).rearrange("(k p) n -> p k n", p=P)
        ctx = Load(ctx_loaded)

        @block.sync
        def _(sp):
            for n in range(LOADS):
                if n >= RING:
                    sp.wait_ge(chunk_done, 4 * (n - RING + 1))
                sp.dma_start(w[:, n % RING], src[:, :, n * 512:(n + 1) * 512]).then_inc(w_loaded[n % RING], 16)
                if n == 0:
                    ctx.start(sp, kt[:, :, SAMPLE:OWN_P], layer_row(io["ctx_k"], layer))
                    ctx.start(sp, v_sb[:, 4, :], layer_row(io["ctx_v"], layer))
                    sp.dma_start(wdt[:], src[:, :, M_DT:M_END]).then_inc(dt_w_loaded, 16)
            sp.wait_ge(ctx_loaded, ctx.total)

        @block.tensor
        def _(pe):
            def free_pair(i):
                if i >= 4:
                    pe.wait_ge(copied_v if i % 2 == 0 else copied_a, (i - 4) // 2 + 1)

            for i in range(FEATURE_CHUNKS):
                n, b = i // 4, 2 * (i % 4)
                if i % 4 == 0:
                    pe.wait_ge(w_loaded[n % RING], 16 * (n // RING + 1))
                free_pair(i)
                for a, z, bank in ((0, SAMPLE, b), (SAMPLE, T, b + 1)):
                    for k in range(KD):
                        last = pe.matmul(ps[:, bank, 0:z - a], w[:, n % RING, k, (i % 4) * P:(i % 4 + 1) * P],
                                         h[:, k, a:z], start=(k == 0), stop=(k == KD - 1))
                last.then_inc(chunk_done, 1)
            pe.wait_ge(w_loaded[(LOADS - 1) % RING], 16 * ((LOADS - 1) // RING + 1))
            pe.wait_ge(dt_w_loaded, 16)
            for t in range(NT):
                i = FEATURE_CHUNKS + t
                b = 2 * (i % 4)
                free_pair(i)
                for k in range(KD):
                    pe.matmul(ps[:, b, :], h[:, k, t * P:(t + 1) * P], w[:, (LOADS - 1) % RING, k, :],
                              start=(k == 0), stop=(k == KD - 1))
                for k in range(KD):
                    last = pe.matmul(ps[:, b + 1, 0:8], h[:, k, t * P:(t + 1) * P], wdt[:, k, :],
                                     start=(k == 0), stop=(k == KD - 1))
                last.then_inc(chunk_done, 1)

        def copy_out(eng, odd, copy, done):
            for i in range(FEATURE_CHUNKS + NT):
                if i % 2 != odd:
                    continue
                eng.wait_ge(chunk_done, i + 1)
                b = 2 * (i % 4)
                if i < FEATURE_CHUNKS:
                    for dst, a, z in places[i]:
                        if a == 0 and z == T:
                            last = copy(dst, ps[:, b:b + 2].rearrange("p a b -> p (a b)")[:, 0:T])
                        else:
                            last = copy(dst, ps[:, b + (1 if a else 0), 0:z - a])
                else:
                    t = i - FEATURE_CHUNKS
                    copy(v_sb[:, t if t < NT - 1 else 5, :], ps[:, b, :])
                    last = copy(g["dtr"][:, t, :], ps[:, b + 1, 0:8])
                last.then_inc(done, 1)

        @block.vector
        def _(v):
            copy_out(v, 0, v.tensor_copy, copied_v)

        @block.scalar
        def _(act):
            copy_out(act, 1, lambda o, i: act.activation(o, i, ACT.Copy), copied_a)

        @block.gpsimd
        def _(pool):
            pool.memset(sx[:, :, 0:1], 0.0)
            pool.memset(sx[:, :, SX_S + SAMPLE:SX_P], 0.0)
            pool.memset(sx[:, :, SXW - 1:SXW], 0.0).then_inc(pads, 1)


def latent_heads(nc, io, g, layer):
    ps, cst, vec, kt, qt, cq = g["ps"], g["cst"], g["vec"], g["kt"], g["qt"], g["cq"]
    qn, qr, kn, mv = g["qn"], g["qr"], g["kn"], g["mv"]
    SPLIT = ((0, SAMPLE, 0), (SAMPLE, T, OWN_P))

    def pair(b, n=T):
        return ps[:, b:b + 2].rearrange("p a b -> p (a b)")[:, 0:n]

    with stage(nc) as (block, sem, sb):
        wuq = sb("wuq", [P, 3, 384])
        wukv = sb("wukv", [P, 2, 512])
        sq = sb("lat_sq", [P, 5, T])
        ms = sb("lat_ms", [P, 2, T])
        root = sb("lat_root", [P, 2, T])
        rstd = sb("lat_rstd", [P, 2, T])
        xc = sb("rot_cos", [P, 2, SAMPLE])
        xs = sb("rot_sin", [P, 2, SAMPLE])
        up = Load(sem("up_weights_loaded"))
        sq_ready, sums_done, ms_ready, root_ready, out_done = (
            sem(n) for n in ("lat_sq_ready", "lat_sums_done", "lat_ms_ready", "lat_root_ready", "prompt_out_done"))
        normed = Count(sem("lat_normed"))
        up_done, up_copied, turned, rotated = (
            sem(n) for n in ("up_done", "up_copied", "turned", "rotated"))
        units = []
        for c in range(3):
            dst = qn[:, c, :] if c < 2 else qr[:]
            units.append(([(dst, 0, T)], 3,
                          lambda k, c=c: wuq[:, k, c * P:(c + 1) * P], lambda k, a, z: cq[:, k, a:z], T))
        for c in range(2):
            units.append(([(kn[:, c, :], 0, KEYS)], 2,
                          lambda k, c=c: wukv[:, k, c * P:(c + 1) * P], lambda k, a, z: kt[:, K_CKV + k, a:z], KEYS))
        for t in range(6):
            units.append(([(mv[:, t, :], 0, 256)], 2,
                          lambda k, t=t: kt[:, K_CKV + k, t * P:(t + 1) * P], lambda k, a, z: wukv[:, k, 256 + a:256 + z], 256))
        NU = len(units)
        rots = [qr[:, 0:SAMPLE], kt[:, K_KR, 0:SAMPLE], qt[:, 2, 0:SAMPLE], qt[:, 3, 0:SAMPLE],
                kt[:, K_DF, 0:SAMPLE], kt[:, K_DF + 1, 0:SAMPLE]]

        @block.sync
        def _(sp):
            up.start(sp, wuq[:], layer_row(io["w_uq"], layer).rearrange("(k p) n -> p k n", p=P))
            up.start(sp, wukv[:], layer_row(io["w_ukv"], layer).rearrange("(k p) n -> p k n", p=P))
            sp.wait_ge(normed.sem, 1 + 3 + 4)
            sp.dma_start(layer_row(io["new_k"], layer), kt[:, :, OWN_P:KEYS]).then_inc(out_done, 16)
            sp.dma_start(layer_row(io["new_v"], layer), g["v"][:, 5, :]).then_inc(out_done, 16)
            sp.wait_ge(out_done, 32)

        @block.scalar
        def _(act):
            for c in range(3):
                act.activation(sq[:, c, :], cq[:, c, :], ACT.Square)
            for c in range(2):
                for a, z, ka in SPLIT:
                    last = act.activation(sq[:, 3 + c, a:z], kt[:, K_CKV + c, ka:ka + z - a], ACT.Square)
            last.then_inc(sq_ready, 1)
            act.wait_ge(ms_ready, 2)
            act.activation(root[:], ms[:], ACT.Sqrt).then_inc(root_ready, 1)
            for i in range(NU):
                act.wait_ge(up_done, i + 1)
                for dst, a, z in units[i][0]:
                    act.activation(dst, pair(2 * (i % 3), z), ACT.Copy).then_inc(up_copied, 1)

        @block.tensor
        def _(pe):
            pe.wait_ge(sq_ready, 1)
            for b, chunks in ((0, (0, 1, 2)), (2, (3, 4))):
                for a, z, bank in ((0, SAMPLE, b), (SAMPLE, T, b + 1)):
                    for c in chunks:
                        last = pe.matmul(ps[:, bank, 0:z - a], cst[:, C_ONE:C_ONE + P], sq[:, c, a:z],
                                         start=(c == chunks[0]), stop=(c == chunks[-1]))
            last.then_inc(sums_done, 1)
            pe.wait_ge(up.sem, 32)
            pe.wait_ge(normed.sem, 1 + 3 + 4)
            for i, (dsts, nk, lhs, rhs, n) in enumerate(units):
                b = 2 * (i % 3)
                if i >= 3:
                    pe.wait_ge(up_copied, i - 2)
                for a in range(0, n, 512):
                    z = min(n, a + 512)
                    for k in range(nk):
                        last = pe.matmul(ps[:, b + a // 512, 0:z - a], lhs(k), rhs(k, a, z), start=(k == 0), stop=(k == nk - 1))
                last.then_inc(up_done, 1)
            pe.wait_ge(up_copied, 3)
            for r, buf in enumerate(rots):
                if r >= 2:
                    pe.wait_ge(rotated, 3 * (r - 2) + 2)
                pe.matmul(ps[:, 6 + r % 2, :], cst[:, C_ROT:C_ROT + P], buf, start=True, stop=True).then_inc(turned, 1)

        @block.vector
        def _(v):
            v.wait_ge(sums_done, 1)
            v.tensor_scalar(ms[:, 0, :], pair(0), 1.0 / QR, EPS, ALU.mult, ALU.add).then_inc(ms_ready, 1)
            v.tensor_scalar(ms[:, 1, :], pair(2), 1.0 / KVR, EPS, ALU.mult, ALU.add).then_inc(ms_ready, 1)
            v.wait_ge(root_ready, 1)
            normed.link(v, v.reciprocal(rstd[:], root[:]))
            for c in range(3):
                normed.mark(v.scalar_tensor_tensor(out=cq[:, c, :], in0=cq[:, c, :], scalar=vec[:, V_QG + c:V_QG + c + 1],
                                                   in1=rstd[:, 0, :], op0=ALU.mult, op1=ALU.mult))
            for c in range(2):
                for a, z, ka in SPLIT:
                    dst = kt[:, K_CKV + c, ka:ka + z - a]
                    normed.mark(v.scalar_tensor_tensor(out=dst, in0=dst, scalar=vec[:, V_KVG + c:V_KVG + c + 1],
                                                       in1=rstd[:, 1, a:z], op0=ALU.mult, op1=ALU.mult))

            for r, buf in enumerate(rots):
                v.wait_ge(turned, r + 1)
                if r >= 2:
                    v.wait_ge(rotated, 3 * (r - 2) + 3)
                v.tensor_tensor(xc[:, r % 2], buf, cst[:, C_COS:C_COS + SAMPLE], ALU.mult).then_inc(rotated, 1)
                v.tensor_tensor(xs[:, r % 2], ps[:, 6 + r % 2, :], cst[:, C_SIN:C_SIN + SAMPLE], ALU.mult).then_inc(rotated, 1)
                v.wait_ge(rotated, 3 * r + 2)
                v.tensor_tensor(buf, xc[:, r % 2], xs[:, r % 2], ALU.add).then_inc(rotated, 1)



def attention(nc, io, g, layer):
    ps, cst, vec, kt, qt, br = g["ps"], g["cst"], g["vec"], g["kt"], g["qt"], g["br"]
    qn, qr, kn, mv, vv = g["qn"], g["qr"], g["kn"], g["mv"], g["v"]
    NA, MLA, DF = range(3)
    units = []
    for branch in (NA, MLA, DF):
        for hd in range(HEADS):
            lo, c = 64 * (hd % 2), hd // 2
            for t in range(NT):
                for comp in range(2 if branch == DF else 1):
                    if branch == NA:
                        parts = [(qt[lo:lo + 64, c, :], kt[lo:lo + 64, K_NA + c, :])]
                    elif branch == MLA:
                        parts = [(qn[lo:lo + 64, c, :], kn[lo:lo + 64, c, :]),
                                 (qr[32 * hd:32 * hd + 32, :], kt[32 * hd:32 * hd + 32, K_KR, :])]
                    else:
                        d0 = lo + 32 * comp
                        parts = [(qt[d0:d0 + 32, 2 + c, :], kt[d0:d0 + 32, K_DF + c, :])]
                    vals = mv[:, :, 64 * hd:64 * hd + 64] if branch == MLA else \
                        vv[:, :, (256 if branch == DF else 0) + 64 * hd:(256 if branch == DF else 0) + 64 * hd + 64]
                    units.append(dict(branch=branch, hd=hd, t=t, comp=comp, parts=parts, vals=vals,
                                      scale=(64 ** -0.5, 96 ** -0.5, 32 ** -0.5)[branch],
                                      biased=branch == NA and t < NT - 1,
                                      first=comp == 0, last=branch != DF or comp == 1,
                                      keys=(0, OWN_P) if t < NT - 1 else (OWN_P, KEYS)))
    NU = len(units)
    outs, n = [], 0
    for u in units:
        outs.append(n)
        n += u["last"]
    NO = n

    def scores(u, n):
        return ps[:, 2 * (u % 2):2 * (u % 2) + 2].rearrange("p a b -> p (a b)")[:, 0:n]

    def out_place(u):
        x = units[u]
        lo = 64 * (x["hd"] % 2)
        return (br[lo:lo + 64, x["branch"], x["hd"] // 2, x["t"] * P:(x["t"] + 1) * P],
                ps[lo:lo + 64, 6 + outs[u] % 2, 0:P])

    with stage(nc) as (block, sem, sb):
        bias = sb("na_bias", [P, HEADS, 16, GRID_W])
        biased = sb("biased_scores", [P, 2, OWN_P])
        prob = sb("prob", [P, 3, OWN_P])
        pt = sb("prob_turned", [P, 2, OWN_P])
        mx = sb("row_max", [P, 2])
        nm = sb("neg_max", [P, 2])
        rowsum = sb("row_sum", [P, 3])
        rec = sb("row_rec", [P, 3])
        lp = sb("lam_prod", [P, 2, 32])
        ls = sb("lam_sum", [P, 2])
        le = sb("lam_exp", [P, 2])
        ld = sb("lam_diff", [P, 1])
        neglam = sb("neg_lam", [P, 1])
        sub = sb("sub_gain", [P, 1])
        dsq = sb("df_sq", [P, 2, T])
        dms = sb("df_ms", [P, 2, T])
        droot = sb("df_root", [P, 2, T])
        (bias_loaded, bias_ready, lam_sum_ready, lam_exp_ready, scores_done, neg_max_ready, exp_done, prob_ready,
         turned, turned_copied, out_done, out_copied, df_sq_ready, df_sums_done, df_ms_ready, df_root_ready) = (
            sem(n) for n in ("bias_loaded", "bias_ready", "lam_sum_ready", "lam_exp_ready", "scores_done",
                             "neg_max_ready", "exp_done", "prob_ready", "prob_turned_done", "turned_copied", "out_done",
                             "out_copied", "df_sq_ready", "df_sums_done", "df_ms_ready", "df_root_ready"))
        chain = Count(sem("attention_vector_chain"))

        @block.sync
        def _(sp):
            sp.dma_start(bias[:], layer_row(io["bias"], layer)).then_inc(bias_loaded, 16)

        @block.tensor
        def _(pe):
            def score(u):
                x = units[u]
                if u >= 2:
                    pe.wait_ge(exp_done, u - 1)
                k0, k1 = x["keys"]
                for a in range(k0, k1, 512):
                    z = min(a + 512, k1)
                    dst = scores(u, z - k0)[:, a - k0:z - k0]
                    for i, (q, k) in enumerate(x["parts"]):
                        last = pe.matmul(dst, q[:, x["t"] * P:(x["t"] + 1) * P], k[:, a:z],
                                         start=(i == 0), stop=(i == len(x["parts"]) - 1))
                last.then_inc(scores_done, 1)

            def turn(u):
                x = units[u]
                pe.wait_ge(prob_ready, u + 1)
                if u >= 1:
                    pe.wait_ge(turned_copied, u)
                for b in range((x["keys"][1] - x["keys"][0]) // P):
                    last = pe.transpose(ps[:, 4:6].rearrange("p a b -> p (a b)")[:, b * P:(b + 1) * P],
                                        prob[:, u % 3, b * P:(b + 1) * P], cst[:, C_ID:C_ID + P])
                last.then_inc(turned, 1)

            def values(u):
                x = units[u]
                pe.wait_ge(turned_copied, u + 1)
                if x["first"] and outs[u] >= 2:
                    pe.wait_ge(out_copied, outs[u] - 1)
                nb = (x["keys"][1] - x["keys"][0]) // P
                for b in range(nb):
                    last = pe.matmul(out_place(u)[1], x["vals"][:, b if nb > 1 else 5, :], pt[:, u % 2, b * P:(b + 1) * P],
                                     start=(b == 0 and x["first"]), stop=(b == nb - 1 and x["last"]))
                last.then_inc(out_done, 1)

            for i in range(NU + 3):
                if i < NU:
                    score(i)
                if 2 <= i < NU + 2:
                    turn(i - 2)
                if i >= 3:
                    values(i - 3)
            pe.wait_ge(df_sq_ready, 1)
            for c in range(2):
                pe.matmul(ps[:, 2 * c, :], cst[:, C_BLK:C_BLK + P], dsq[:, c, 0:SAMPLE], start=True, stop=True)
                last = pe.matmul(ps[:, 2 * c + 1, 0:PROMPT], cst[:, C_BLK:C_BLK + P], dsq[:, c, SAMPLE:T], start=True, stop=True)
            last.then_inc(df_sums_done, 1)

        @block.scalar
        def _(act):
            act.wait_ge(lam_sum_ready, 1)
            act.activation(le[:], ls[:], ACT.Exp).then_inc(lam_exp_ready, 1)
            for i in range(NU + 2):
                if i < NU:
                    x = units[i]
                    n = x["keys"][1] - x["keys"][0]
                    act.wait_ge(neg_max_ready, i + 1)
                    if i >= 3:
                        act.wait_ge(turned, i - 2)
                    src = biased[:, i % 2, 0:n] if x["biased"] else scores(i, n)
                    act.activation(prob[:, i % 3, 0:n], src, ACT.Exp, bias=nm[:, i % 2:i % 2 + 1],
                                   scale=1.0 if x["biased"] else x["scale"],
                                   accum_out=rowsum[:, i % 3:i % 3 + 1]).then_inc(exp_done, 1)
                if i >= 2:
                    u = i - 2
                    n = units[u]["keys"][1] - units[u]["keys"][0]
                    act.wait_ge(turned, u + 1)
                    if u >= 2:
                        act.wait_ge(out_done, u - 1)
                    act.activation(pt[:, u % 2, 0:n], ps[:, 4:6].rearrange("p a b -> p (a b)")[:, 0:n],
                                   ACT.Copy).then_inc(turned_copied, 1)
            act.wait_ge(out_copied, NO)
            act.activation(dsq[:], br[:, DF], ACT.Square).then_inc(df_sq_ready, 1)
            act.wait_ge(df_ms_ready, 1)
            act.activation(droot[:], dms[:], ACT.Sqrt).then_inc(df_root_ready, 1)

        @block.vector
        def _(v):
            lam = vec[:, V_LAM:V_LAM + 128].rearrange("p (a b d) -> p a b d", a=2, b=2)
            chain.link(v, v.tensor_tensor(lp[:], lam[:, :, 0, :], lam[:, :, 1, :], ALU.mult))
            v.tensor_reduce(ls[:], lp[:], AXX, ALU.add).then_inc(lam_sum_ready, 1)
            chain.mark(v.tensor_scalar(sub[:], vec[:, V_SUB:V_SUB + 1], vec[:, V_LI + 1:V_LI + 2], None, ALU.mult))
            v.wait_ge(lam_exp_ready, 1)
            chain.link(v, v.tensor_tensor(ld[:], le[:, 1:2], le[:, 0:1], ALU.subtract))
            chain.link(v, v.tensor_tensor(neglam[:], ld[:], vec[:, V_LI:V_LI + 1], ALU.subtract))
            v.wait_ge(bias_loaded, 16)
            flat = bias[:].rearrange("p a b c -> p (a b) c")
            chain.link(v, v.tensor_tensor(flat, flat, cst[:, C_WIN:C_WIN + GRID_W].unsqueeze(1).broadcast_to(
                [P, HEADS * 16, GRID_W]), ALU.add))

            def maximum(u):
                x = units[u]
                n = x["keys"][1] - x["keys"][0]
                v.wait_ge(scores_done, u + 1)
                if u >= 2:
                    v.wait_ge(exp_done, u - 1)
                src = scores(u, n)
                if x["biased"]:
                    off = 7 - 2 * x["t"]
                    chain.mark(v.scalar_tensor_tensor(
                        out=biased[:, u % 2, 0:SAMPLE], in0=src[:, 0:SAMPLE], scalar=x["scale"],
                        in1=bias[:, x["hd"], off:off + ROWS, :].rearrange("p a b -> p (a b)"), op0=ALU.mult, op1=ALU.add))
                    chain.link(v, v.tensor_scalar(biased[:, u % 2, SAMPLE:n], src[:, SAMPLE:n], x["scale"], None, ALU.mult))
                    src = biased[:, u % 2, 0:n]
                chain.link(v, v.tensor_reduce(mx[:, u % 2:u % 2 + 1], src, AXX, ALU.max))
                v.tensor_scalar(nm[:, u % 2:u % 2 + 1], mx[:, u % 2:u % 2 + 1], -1.0 if x["biased"] else -x["scale"],
                                None, ALU.mult).then_inc(neg_max_ready, 1)

            def normalise(u):
                x = units[u]
                n = x["keys"][1] - x["keys"][0]
                v.wait_ge(exp_done, u + 1)
                r = rec[:, u % 3:u % 3 + 1]
                chain.link(v, v.reciprocal(r, rowsum[:, u % 3:u % 3 + 1]))
                if x["comp"] == 1:
                    v.tensor_scalar(prob[:, u % 3, 0:n], prob[:, u % 3, 0:n], r, neglam[:, 0:1], ALU.mult, ALU.mult).then_inc(prob_ready, 1)
                else:
                    v.tensor_scalar(prob[:, u % 3, 0:n], prob[:, u % 3, 0:n], r, None, ALU.mult).then_inc(prob_ready, 1)

            def copy_out(u):
                if units[u]["last"]:
                    v.wait_ge(out_done, u + 1)
                    dst, src = out_place(u)
                    v.tensor_copy(dst, src).then_inc(out_copied, 1)

            for i in range(NU + 4):
                if 1 <= i <= NU:
                    normalise(i - 1)
                if i >= 4:
                    copy_out(i - 4)
                if i < NU:
                    maximum(i)
            v.wait_ge(df_sums_done, 1)
            v.tensor_scalar(dms[:], ps[:, 0:4].rearrange("p (a b) c -> p a (b c)", a=2)[:, :, 0:T], 1.0 / 64, EPS,
                            ALU.mult, ALU.add).then_inc(df_ms_ready, 1)
            v.wait_ge(df_root_ready, 1)
            chain.link(v, v.reciprocal(droot[:], droot[:]))
            chain.mark(v.scalar_tensor_tensor(out=br[:, DF], in0=br[:, DF], scalar=sub[:, 0:1], in1=droot[:],
                                              op0=ALU.mult, op1=ALU.mult))


def ssm(nc, io, g, layer):
    ps, cst, vec, sx, sz, br = g["ps"], g["cst"], g["vec"], g["sx"], g["sz"], g["br"]
    CW = T + 2
    steps = ([(0, t) for t in range(NT - 1)] + [(0, NT - 1)] + [(1, t) for t in reversed(range(NT - 1))] + [(1, NT - 1)])
    NS = len(steps)
    with stage(nc) as (block, sem, sb):
        xc = sb("conv", [P, 4, CW])
        th = sb("conv_tanh", [P, 4, CW])
        thz = sb("z_tanh", [P, 2, T])
        xtok = sb("conv_tok", [P, NT, 384])
        dtu, dtn, dte, dtl, dt, a8, ac, nac = (sb(n, [P, NT, 8]) for n in (
            "dt_u", "dt_n", "dt_e", "dt_l", "dt", "dt_a", "a_cum", "neg_a_cum"))
        ea = sb("exp_a", [P, 8])
        gm = sb("bc_masked", [P, NT, 2, 2, P])
        state = sb("state", [P, 2, 2, 2, 64])
        arep = sb("a_rep", [P, 4, P])
        seg = sb("seg", [P, 4, P])
        dec = sb("dec", [P, 4, P])
        e0 = sb("exp_cum", [P, 4, P])
        mm = sb("mixing", [P, 4, P])
        cts = sb("c_scaled", [P, 2, P])
        wd = sb("w_dif", [P, 4])
        we = sb("w_exp", [P, 4])
        xw = sb("x_weighted", [P, 4, 64])
        y = sb("ssm_y", [P, 2, T])
        ysq = sb("ssm_sq", [P, 2, T])
        yms, yroot, yrstd = (sb(n, [P, T]) for n in ("ssm_ms", "ssm_root", "ssm_rstd"))
        (state_loaded, conv_ready, conv_tanh, z_tanh, dt_arg, dt_exp, dt_one, dt_ln, conv_silu, tok_turned, tok_copied,
         a_ready, cum_done, bc_done, bc_read, rep_ready, along_done, seg_ready, dec_ready, wd_ready, w_ready, mix_ready,
         y_done, y_added, ysq_ready, ysum_done, yms_ready, yroot_ready, gated_ready, state_out) = (
            sem(n) for n in ("state_loaded", "conv_ready", "conv_tanh_done", "z_tanh_done", "dt_arg", "dt_exp", "dt_one", "dt_ln",
                             "conv_silu", "tok_turned", "tok_copied", "a_ready", "cum_done", "bc_done", "bc_read",
                             "rep_ready", "along_done", "seg_ready", "dec_ready", "wd_ready", "w_ready", "mix_ready",
                             "y_done", "y_added", "ysq_ready", "ysum_done", "yms_ready", "yroot_ready", "gated_ready", "state_out"))
        chain = Count(sem("ssm_vector_chain"))

        def last_col(dr):
            return P - 1 if dr == 0 else 0

        @block.sync
        def _(sp):
            sp.dma_start(state[:, 0], layer_row(io["state"], layer)).then_inc(state_loaded, 16)
            sp.wait_ge(y_added, 2 * NS)
            sp.dma_start(layer_row(io["new_state"], layer), state[:, 1]).then_inc(state_out, 16)
            sp.wait_ge(state_out, 16)

        @block.scalar
        def _(act):
            act.activation(ea[:], vec[:, V_ALOG:V_ALOG + 8], ACT.Exp)
            act.wait_ge(dt_arg, 1)
            act.activation(dte[:], dtn[:], ACT.Exp).then_inc(dt_exp, 1)
            act.activation(thz[:], sz[:], ACT.Tanh, scale=0.5).then_inc(z_tanh, 1)
            act.wait_ge(conv_ready, 1)
            act.activation(th[:], xc[:], ACT.Tanh, scale=0.5).then_inc(conv_tanh, 1)
            act.wait_ge(dt_one, 1)
            act.activation(dtl[:], dte[:], ACT.Ln).then_inc(dt_ln, 1)
            for t in range(NT):
                act.wait_ge(tok_turned, t + 1)
                act.activation(xtok[:, t, :], ps[:, t % 2, 0:384], ACT.Copy).then_inc(tok_copied, 1)
            for s, (dr, t) in enumerate(steps):
                act.wait_ge(along_done, s + 1)
                if s >= 1:
                    act.wait_ge(y_added, 2 * s)
                act.activation(e0[:], ps[:, 4, :].rearrange("p (a b) -> p a b", a=4), ACT.Exp).then_inc(dec_ready, 1)
                act.wait_ge(wd_ready, s + 1)
                act.activation(we[:], wd[:], ACT.Exp).then_inc(w_ready, 1)
                act.wait_ge(seg_ready, s + 1)
                act.activation(dec[:], seg[:], ACT.Exp).then_inc(dec_ready, 1)
            act.wait_ge(gated_ready, 1)
            act.activation(ysq[:], y[:], ACT.Square).then_inc(ysq_ready, 1)
            act.wait_ge(yms_ready, 1)
            act.activation(yroot[:], yms[:], ACT.Sqrt).then_inc(yroot_ready, 1)

        @block.tensor
        def _(pe):
            pe.wait_ge(conv_silu, 1)
            for t in range(NT):
                if t >= 2:
                    pe.wait_ge(tok_copied, t - 1)
                for c in range(3):
                    last = pe.transpose(ps[:, t % 2, c * P:(c + 1) * P], xc[:, c, pcol(t):pcol(t) + P], cst[:, C_ID:C_ID + P])
                last.then_inc(tok_turned, 1)
            pe.wait_ge(a_ready, 1)
            for dr, tri in ((0, C_LE), (1, C_GE)):
                last = pe.matmul(ps[:, 2, 20 * dr:20 * dr + 20].rearrange("p (a b) -> p a b", a=NT), cst[:, tri:tri + P],
                                 a8[:, :, 4 * dr:4 * dr + 4], start=True, stop=True)
            last.then_inc(cum_done, 1)
            for t in range(NT):
                if t >= 1:
                    pe.wait_ge(bc_read, t)
                for gr in range(2):
                    lo = 64 * gr
                    last = pe.matmul(ps[:, 3 + 4 * gr, 0:P], xc[lo:lo + 64, 2, pcol(t):pcol(t) + P],
                                     xc[lo:lo + 64, 3, pcol(t):pcol(t) + P], start=True, stop=True)
                last.then_inc(bc_done, 1)
            pe.wait_ge(tok_copied, NT)
            for s, (dr, t) in enumerate(steps):
                tri = C_LE if dr == 0 else C_GE
                pe.wait_ge(rep_ready, s + 1)
                for hd in range(4):
                    last = pe.matmul(ps[:, 4, hd * P:(hd + 1) * P], arep[:, hd, :], cst[:, tri:tri + P], start=True, stop=True)
                last.then_inc(along_done, 1)
                pe.wait_ge(mix_ready, s + 1)
                for hd in range(4):
                    lo, gl = 64 * (hd % 2), 64 * (hd // 2)
                    dst = ps[lo:lo + 64, 5 + 2 * (hd // 2), 0:P]
                    pe.matmul(dst, xtok[:, t, 64 * hd:64 * hd + 64], mm[:, hd, :], start=True, stop=False)
                    pe.matmul(dst, state[gl:gl + 64, t // 4, dr, hd % 2, :], cts[gl:gl + 64, hd % 2, :], start=False, stop=True)
                pe.matmul(ps[:, 6, 0:256], xtok[:, t, 256:384], xw[:].rearrange("p a b -> p (a b)"),
                          start=True, stop=True).then_inc(y_done, 1)
            pe.wait_ge(ysq_ready, 1)
            for a, z, bank in ((0, SAMPLE, 0), (SAMPLE, T, 1)):
                for c in range(2):
                    last = pe.matmul(ps[:, bank, 0:z - a], cst[:, C_ONE:C_ONE + P], ysq[:, c, a:z], start=(c == 0), stop=(c == 1))
            last.then_inc(ysum_done, 1)

        @block.vector
        def _(v):
            link = lambda ins: chain.link(v, ins)
            link(v.tensor_tensor(dtu[:], g["dtr"][:], vec[:, V_DTB:V_DTB + 8].unsqueeze(1).broadcast_to([P, NT, 8]), ALU.add))
            link(v.tensor_scalar(dtn[:], dtu[:], -1.0, None, ALU.mult))
            v.tensor_tensor(dtn[:], dtu[:], dtn[:], ALU.min).then_inc(dt_arg, 1)
            for c in range(4):
                w = [vec[:, V_CW + 4 * tap + c:V_CW + 4 * tap + c + 1] for tap in range(3)]
                link(v.tensor_scalar(xc[:, c], sx[:, c, 0:CW], w[0], vec[:, V_CB + c:V_CB + c + 1], ALU.mult, ALU.add))
                link(v.scalar_tensor_tensor(out=xc[:, c], in0=sx[:, c, 1:1 + CW], scalar=w[1], in1=xc[:, c], op0=ALU.mult, op1=ALU.add))
                ins = v.scalar_tensor_tensor(out=xc[:, c], in0=sx[:, c, 2:2 + CW], scalar=w[2], in1=xc[:, c], op0=ALU.mult, op1=ALU.add)
                if c == 3:
                    ins.then_inc(conv_ready, 1)
                else:
                    chain.mark(ins)
            v.wait_ge(dt_exp, 1)
            v.tensor_scalar(dte[:], dte[:], 1.0, None, ALU.add).then_inc(dt_one, 1)
            v.wait_ge(conv_tanh, 1)
            link(v.tensor_scalar(th[:], th[:], 0.5, 0.5, ALU.mult, ALU.add))
            v.tensor_tensor(xc[:], xc[:], th[:], ALU.mult).then_inc(conv_silu, 1)
            v.wait_ge(dt_ln, 1)
            link(v.scalar_tensor_tensor(out=dt[:], in0=dtu[:], scalar=0.0, in1=dtl[:], op0=ALU.max, op1=ALU.add))
            v.scalar_tensor_tensor(out=a8[:], in0=dt[:], scalar=-1.0, in1=ea[:].unsqueeze(1).broadcast_to([P, NT, 8]),
                                   op0=ALU.mult, op1=ALU.mult).then_inc(a_ready, 1)
            v.wait_ge(z_tanh, 1)
            link(v.tensor_scalar(thz[:], thz[:], 0.5, 0.5, ALU.mult, ALU.add))
            link(v.tensor_tensor(sz[:], sz[:], thz[:], ALU.mult))
            v.wait_ge(conv_silu, 1)
            for c in range(2):
                for t0, t1, src in ((0, SAMPLE, 0), (SAMPLE, T, SAMPLE + 2)):
                    chain.mark(v.tensor_scalar(y[:, c, t0:t1], xc[:, c, src:src + t1 - t0],
                                               vec[:, V_SD + c:V_SD + c + 1], None, ALU.mult))
            v.wait_ge(cum_done, 1)
            cum = ps[:, 2, 0:40].rearrange("p (d a b) -> p a d b", d=2, a=NT)
            chain.mark(v.tensor_scalar(nac[:].rearrange("p a (d b) -> p a d b", d=2), cum, -1.0, None, ALU.mult))
            for t in range(NT):
                v.wait_ge(bc_done, t + 1)
                for dr, tri in ((0, C_LE), (1, C_GE)):
                    last = v.tensor_tensor(gm[:, t, dr], ps[:, 3:8:4, 0:P],
                                           cst[:, tri:tri + P].unsqueeze(1).broadcast_to([P, 2, P]), ALU.mult)
                last.then_inc(bc_read, 1)
            link(v.memset(state[:, 1], 0.0))
            v.wait_ge(state_loaded, 16)
            v.wait_ge(tok_copied, NT)
            v.wait_ge(a_ready, 1)
            v.wait_ge(bc_read, NT)
            for s, (dr, t) in enumerate(steps):
                heads = slice(4 * dr, 4 * dr + 4)
                lc = last_col(dr)
                along = ps[:, 4, :].rearrange("p (a b) -> p a b", a=4)
                v.tensor_copy(arep[:], a8[:, t, heads].unsqueeze(2).broadcast_to([P, 4, P])).then_inc(rep_ready, 1)
                v.wait_ge(dec_ready, 2 * s + 1)
                v.tensor_tensor(wd[:], along[:, :, lc], nac[:, t, heads], ALU.add).then_inc(wd_ready, 1)
                link(v.tensor_tensor(seg[:], along, nac[:, t, heads].unsqueeze(2).broadcast_to([P, 4, P]), ALU.add))
                v.tensor_scalar(seg[:], seg[:], 0.0, None, ALU.min).then_inc(seg_ready, 1)
                v.wait_ge(w_ready, s + 1)
                link(v.tensor_tensor(we[:], we[:], dt[:, t, heads], ALU.mult))
                link(v.tensor_tensor(xw[:], xtok[:, t, 0:256].rearrange("p (a b) -> p a b", a=4),
                                     we[:].unsqueeze(2).broadcast_to([P, 4, 64]), ALU.mult))
                v.wait_ge(dec_ready, 2 * s + 2)
                for gr in range(2):
                    lo = 64 * gr
                    chain.mark(v.tensor_tensor(cts[lo:lo + 64], e0[lo:lo + 64, 2 * gr:2 * gr + 2, :],
                                               xc[lo:lo + 64, 3, pcol(t):pcol(t) + P].unsqueeze(1).broadcast_to([64, 2, P]), ALU.mult))
                link(v.tensor_tensor(dec[:], dec[:], dt[:, t, heads].unsqueeze(2).broadcast_to([P, 4, P]), ALU.mult))
                v.tensor_tensor(mm[:].rearrange("p (a b) c -> p a b c", a=2), dec[:].rearrange("p (a b) c -> p a b c", a=2),
                                gm[:, t, dr].unsqueeze(2).broadcast_to([P, 2, 2, P]), ALU.mult).then_inc(mix_ready, 1)
                v.wait_ge(y_done, s + 1)
                yt = y[:, :, t * P:(t + 1) * P]
                v.tensor_tensor(yt, yt, ps[:, 5:8:2, 0:P], ALU.add).then_inc(y_added, 1)
                for gr in range(2):
                    lo = 64 * gr
                    for m in range(2):
                        hd = 2 * gr + m
                        st = state[lo:lo + 64, t // 4, dr, m, :]
                        ins = v.scalar_tensor_tensor(out=st, in0=st, scalar=e0[lo:lo + 64, hd, lc:lc + 1],
                                                     in1=ps[lo:lo + 64, 6, 64 * hd:64 * hd + 64], op0=ALU.mult, op1=ALU.add)
                        if hd == 3:
                            ins.then_inc(y_added, 1)
                        else:
                            chain.mark(ins)
                v.wait_ge(y_added, 2 * s + 2)
            v.tensor_tensor(y[:], y[:], sz[:], ALU.mult).then_inc(gated_ready, 1)
            v.wait_ge(ysum_done, 1)
            v.tensor_scalar(yms[:], ps[:, 0:2].rearrange("p a b -> p (a b)")[:, 0:T], 1.0 / 256, EPS, ALU.mult, ALU.add).then_inc(yms_ready, 1)
            v.wait_ge(yroot_ready, 1)
            link(v.reciprocal(yrstd[:], yroot[:]))
            for c in range(2):
                chain.mark(v.scalar_tensor_tensor(out=br[:, 3, c, :], in0=y[:, c, :], scalar=vec[:, V_SG + c:V_SG + c + 1],
                                                  in1=yrstd[:], op0=ALU.mult, op1=ALU.mult))


def merge(nc, io, g, layer):
    ps, x, h, br, mod = g["ps"], g["x"], g["h"], g["br"], g["mod"]
    RING = 3
    units = [(n, d) for n in range(4) for d in range(KD)]
    NU = len(units)
    chain_total = 1 + NU - KD

    def pair(b):
        return ps[:, b:b + 2].rearrange("p a b -> p (a b)")[:, 0:T]

    with stage(nc) as (block, sem, sb):
        w = sb("merge_w", [P, RING, KD, 512])
        wb = sb("merge_wb", [P, 2, 2, D])
        th = sb("gate_tanh", [P, 2, T])
        prod = sb("gate_prod", [P, 2, T])
        mix = sb("mix", [P, KD, T])
        half_gate = sb("half_gate", [P, KD, 2])
        w_loaded = [sem(f"merge_w_loaded{i}") for i in range(RING)]
        wb_loaded = [sem(f"merge_wb_loaded{i}") for i in range(2)]
        gate_done, proj_done, tanh_done, gated, out_done, x_added = (
            sem("merge_" + n) for n in ("gate_done", "proj_done", "tanh_done", "gated", "out_done", "x_added"))
        chain = Count(sem("merge_vector_chain"))
        w_gate = layer_row(io["w_in"], layer)[:, O_GATE:IN_W].rearrange("(k p) n -> p k n", p=P)
        w_out = layer_row(io["w_out"], layer).rearrange("(k p) n -> p k n", p=P)
        w_branch = layer_row(io["w_branch"], layer).rearrange("n (k p) d -> n p k d", p=P)

        @block.sync
        def _(sp):
            for i in range(10):
                if i >= RING:
                    sp.wait_ge(proj_done, 4 * (i - RING + 1))
                src = w_gate[:, :, i * 512:(i + 1) * 512] if i < 8 else w_out[:, :, (i - 8) * 512:(i - 7) * 512]
                sp.dma_start(w[:, i % RING], src).then_inc(w_loaded[i % RING], 16)
                if i < 8 and i % 2 == 0:
                    n = i // 2
                    if n >= 2:
                        sp.wait_ge(proj_done, 8 * (n - 1))
                    sp.dma_start(wb[:, n % 2], w_branch[n]).then_inc(wb_loaded[n % 2], 16)

        @block.tensor
        def _(pe):
            for u, (n, d) in enumerate(units):
                i = 2 * n + d // 4
                if d % 4 == 0:
                    pe.wait_ge(w_loaded[i % RING], 16 * (i // RING + 1))
                if d == 0:
                    pe.wait_ge(wb_loaded[n % 2], 16 * (n // 2 + 1))
                if u >= 2:
                    pe.wait_ge(tanh_done, u - 1)
                for a, z, o in ((0, SAMPLE, 0), (SAMPLE, T, 1)):
                    for k in range(KD):
                        last = pe.matmul(ps[:, 2 * (u % 2) + o, 0:z - a], w[:, i % RING, k, (d % 4) * P:(d % 4 + 1) * P],
                                         h[:, k, a:z], start=(k == 0), stop=(k == KD - 1))
                last.then_inc(gate_done, 1)
                if u >= 2:
                    pe.wait_ge(gated, u - 1)
                for a, z, o in ((0, SAMPLE, 0), (SAMPLE, T, 1)):
                    for k in range(2):
                        last = pe.matmul(ps[:, 4 + 2 * (u % 2) + o, 0:z - a], wb[:, n % 2, k, d * P:(d + 1) * P],
                                         br[:, n, k, a:z], start=(k == 0), stop=(k == 1))
                last.then_inc(proj_done, 1)
            pe.wait_ge(chain.sem, chain_total)
            pe.wait_ge(gated, NU)
            for d in range(KD):
                i = 8 + d // 4
                if d % 4 == 0:
                    pe.wait_ge(w_loaded[i % RING], 16 * (i // RING + 1))
                if d >= 4:
                    pe.wait_ge(x_added, d - 3)
                for a, z, o in ((0, SAMPLE, 0), (SAMPLE, T, 1)):
                    for k in range(KD):
                        last = pe.matmul(ps[:, 2 * (d % 4) + o, 0:z - a], w[:, i % RING, k, (d % 4) * P:(d % 4 + 1) * P],
                                         mix[:, k, a:z], start=(k == 0), stop=(k == KD - 1))
                last.then_inc(out_done, 1)

        @block.scalar
        def _(act):
            for u in range(NU):
                act.wait_ge(gate_done, u + 1)
                if u >= 2:
                    act.wait_ge(gated, u - 1)
                act.activation(th[:, u % 2], pair(2 * (u % 2)), ACT.Tanh, scale=0.5).then_inc(tanh_done, 1)

        @block.vector
        def _(v):
            chain.mark(v.tensor_scalar(half_gate[:], mod[:, 16:16 + KD, :], 0.5, None, ALU.mult))
            for u, (n, d) in enumerate(units):
                v.wait_ge(tanh_done, u + 1)
                v.wait_ge(proj_done, u + 1)
                dst = mix[:, d] if n == 0 else prod[:, u % 2]
                v.scalar_tensor_tensor(out=dst, in0=th[:, u % 2], scalar=1.0, in1=pair(4 + 2 * (u % 2)),
                                       op0=ALU.add, op1=ALU.mult).then_inc(gated, 1)
                if n:
                    v.wait_ge(gated, u + 1)
                    chain.mark(v.tensor_tensor(mix[:, d], mix[:, d], prod[:, u % 2], ALU.add))
            assert chain.n == chain_total
            for d in range(KD):
                v.wait_ge(out_done, d + 1)
                for grp, a, z in GROUPS:
                    last = v.scalar_tensor_tensor(out=x[:, d, a:z], in0=ps[:, 2 * (d % 4) + grp, 0:z - a],
                                                  scalar=half_gate[:, d, grp:grp + 1], in1=x[:, d, a:z], op0=ALU.mult, op1=ALU.add)
                last.then_inc(x_added, 1)


def router(nc, io, g, layer):
    ps, cst, h, htok, pos, aff = g["ps"], g["cst"], g["h"], g["htok"], g["pos"], g["aff"]
    with stage(nc) as (block, sem, sb):
        rw = sb("router_w", [P, KD, NE])
        mx = sb("aff_max", [P, NT])
        e = sb("aff_exp", [P, NT, NE])
        su = sb("aff_sum", [P, NT])
        rc = sb("aff_rec", [P, NT])
        left = sb("aff_left", [NE, T])
        top = sb("aff_top", [NE, 8])
        chosen = sb("chosen", [NE, T])
        ones = sb("scan_ones", [NE, T])
        cum = sb("chosen_cum", [NE, T])
        slot = sb("slot", [NE, T])
        rw_loaded, logits_done, tok_turned, tok_copied, arg_ready, exp_done, aff_ready, aff_turned, slot_ready, slot_turned = (
            sem("router_" + n) for n in ("w_loaded", "logits_done", "tok_turned", "tok_copied", "arg_ready", "exp_done",
                                         "aff_ready", "aff_turned", "slot_ready", "slot_turned"))
        chain = Count(sem("router_vector_chain"))

        @block.sync
        def _(sp):
            sp.dma_start(rw[:], layer_row(io["router_w"], layer).rearrange("(k p) n -> p k n", p=P)).then_inc(rw_loaded, 16)

        @block.tensor
        def _(pe):
            pe.wait_ge(rw_loaded, 16)
            for t in range(NT):
                for k in range(KD):
                    last = pe.matmul(ps[:, 6, NE * t:NE * t + NE], h[:, k, t * P:(t + 1) * P], rw[:, k, :],
                                     start=(k == 0), stop=(k == KD - 1))
            last.then_inc(logits_done, 1)
            for t in range(NT):
                if t >= 2:
                    pe.wait_ge(tok_copied, t - 1)
                for k in range(KD):
                    last = pe.transpose(ps[:, 2 * (t % 2) + k // 4, (k % 4) * P:(k % 4 + 1) * P],
                                        h[:, k, t * P:(t + 1) * P], cst[:, C_ID:C_ID + P])
                last.then_inc(tok_turned, 1)
            pe.wait_ge(aff_ready, 1)
            for t in range(NT):
                last = pe.transpose(ps[0:NE, 4 + t // 4, (t % 4) * P:(t % 4 + 1) * P], aff[:, t, 0:NE], cst[:, C_ID:C_ID + P])
            last.then_inc(aff_turned, 1)
            pe.wait_ge(slot_ready, 1)
            for t in range(NT):
                last = pe.transpose(ps[:, 7, NE * t:NE * t + NE], slot[:, t * P:(t + 1) * P], cst[0:NE, C_ID:C_ID + NE])
            last.then_inc(slot_turned, 1)

        @block.scalar
        def _(act):
            act.wait_ge(arg_ready, 1)
            act.activation(e[:], e[:], ACT.Exp).then_inc(exp_done, 1)
            for t in range(NT):
                act.wait_ge(tok_turned, t + 1)
                act.activation(htok[:, t, :], ps[:, 2 * (t % 2):2 * (t % 2) + 2].rearrange("p a b -> p (a b)"),
                               ACT.Copy).then_inc(tok_copied, 1)

        @block.vector
        def _(v):
            link = lambda ins: chain.link(v, ins)
            logits = ps[:, 6, 0:NT * NE].rearrange("p (a b) -> p a b", a=NT)
            chain.mark(v.memset(ones[:], 1.0))
            v.wait_ge(logits_done, 1)
            link(v.tensor_reduce(mx[:], logits, AXX, ALU.max))
            v.tensor_tensor(e[:], logits, mx[:].unsqueeze(2).broadcast_to([P, NT, NE]), ALU.subtract).then_inc(arg_ready, 1)
            v.wait_ge(exp_done, 1)
            link(v.tensor_reduce(su[:], e[:], AXX, ALU.add))
            link(v.reciprocal(rc[:], su[:]))
            v.tensor_tensor(aff[:, :, 0:NE], e[:], rc[:].unsqueeze(2).broadcast_to([P, NT, NE]), ALU.mult).then_inc(aff_ready, 1)
            v.wait_ge(aff_turned, 1)
            link(v.tensor_copy(left[:], ps[0:NE, 4:6].rearrange("p a b -> p (a b)")[:, 0:T]))
            for a, z, cap, off in ((0, SAMPLE, CAP_S, 0.0), (SAMPLE, T, CAP_P, float(CAP_S))):
                for _r in range(cap // 8):
                    link(v.max(out=top[:], in_=left[:, a:z]))
                    link(v.match_replace(out=left[:, a:z], in_to_replace=top[:], in_values=left[:, a:z], imm_value=-1.0))
                link(v.tensor_scalar(chosen[:, a:z], left[:, a:z], 0.0, None, ALU.is_lt))
                link(v.tensor_tensor_scan(cum[:, a:z], ones[:, a:z], chosen[:, a:z], 0.0, ALU.mult, ALU.add))
                link(v.scalar_tensor_tensor(out=slot[:, a:z], in0=cum[:, a:z], scalar=off, in1=chosen[:, a:z],
                                            op0=ALU.add, op1=ALU.mult))
            v.tensor_scalar(slot[:], slot[:], -1.0, None, ALU.add).then_inc(slot_ready, 1)
            v.wait_ge(slot_turned, 1)
            chain.mark(v.tensor_copy(pos[:, :, 0:NE], ps[:, 7, 0:NT * NE].rearrange("p (a b) -> p a b", a=NT)))


class LoopCount:

    def __init__(self, sem, i, per, base=0):
        self.sem, self.i, self.per, self.base, self.n = sem, i, per, base, 0

    def mark(self, ins):
        self.n += 1
        ins.then_inc(self.sem, 1)

    def link(self, eng, ins):
        self.mark(ins)
        eng.wait_ge(self.sem, self.i * self.per + (self.base + self.n))


def choose(nc, io, g):
    ps, cst, htok, pos, aff = g["ps"], g["cst"], g["htok"], g["pos"], g["aff"]
    rows, weight = g["rows"], g["weight"]
    with stage(nc) as (block, sem, sb):
        info = sb("tok_info", [P, NT, NE, 2])
        pick = sb("pick", [P, 2, NT, SLOTS])
        zero = sb("zero_rows", [P, D])
        zero_ready, info_ready, pick_ready, picked, slots_done, rows_out = (
            sem("choose_" + n) for n in ("zero_ready", "info_ready", "pick_ready", "picked", "slots_done", "rows_out"))

        @block.gpsimd
        def _(pool):
            pool.memset(zero[:], 0.0).then_inc(zero_ready, 1)

        @block.sync
        def _(sp):
            sp.dma_start(io["tok_rows"].rearrange("(t p) d -> p t d", p=P), htok[:]).then_inc(rows_out, 16)
            sp.wait_ge(zero_ready, 1)
            for t in range(NT):
                sp.dma_start(io["sum_rows"][t * P:(t + 1) * P, :], zero[:]).then_inc(rows_out, 16)
            sp.wait_ge(rows_out, 16 * (NT + 1))

        @block.vector
        def _(v):
            v.tensor_copy(info[:, :, :, 0], cst[:, C_TOK:C_TOK + NT].unsqueeze(2).broadcast_to([P, NT, NE]))
            v.tensor_copy(info[:, :, :, 1], aff[:, :, 0:NE]).then_inc(info_ready, 1)
            for e in range(NE):
                if e >= 2:
                    v.wait_ge(picked, e - 1)
                v.tensor_tensor(pick[:, e % 2], cst[:, C_SLOT:C_SLOT + SLOTS].unsqueeze(1).broadcast_to([P, NT, SLOTS]),
                                pos[:, :, e:e + 1].broadcast_to([P, NT, SLOTS]), ALU.is_equal).then_inc(pick_ready, 1)
            v.wait_ge(picked, NE)
            found = ps[0:SLOTS, 0, 0:2 * NE].rearrange("p (a b) -> p a b", b=2)
            v.tensor_copy(rows[:], found[:, :, 0])
            v.tensor_copy(weight[:], found[:, :, 1]).then_inc(slots_done, 1)

        @block.tensor
        def _(pe):
            pe.wait_ge(info_ready, 1)
            for e in range(NE):
                pe.wait_ge(pick_ready, e + 1)
                for t in range(NT):
                    last = pe.matmul(ps[0:SLOTS, 0, 2 * e:2 * e + 2], pick[:, e % 2, t, :], info[:, t, e, :],
                                     start=(t == 0), stop=(t == NT - 1))
                last.then_inc(picked, 1)


def experts(nc, io, g, layer):
    ps, cst, rows, weight = (g[n] for n in ("ps", "cst", "rows", "weight"))
    UNITS, RAW, SPLIT, KH = 6, 4, 4, KD // 2
    WEIGHTS = ("exp_w_gate", "exp_w_up", "exp_w_down")

    def pair(b, rows_, n):
        return ps[0:rows_, b:b + 2].rearrange("p a b -> p (a b)")[:, 0:n]

    def turned(b):
        return ps[:, b:b + 2, 0:4 * SLOTS]

    with stage(nc) as (block, sem, sb):
        raw = sb("w_raw", [P, RAW, KD, 512])
        whi = sb("w_hi", [P, SPLIT, KH, 512], F32R)
        wlo = sb("w_lo", [P, SPLIT, KH, 512], F32R)
        xe = sb("xe", [SLOTS, 2, D])
        xhi = sb("xe_hi", [P, KD, SLOTS], F32R)
        xlo = sb("xe_lo", [P, KD, SLOTS], F32R)
        hid = sb("hid", [SLOTS, FF])
        hhi = sb("hid_hi", [P, KD, SLOTS], F32R)
        hlo = sb("hid_lo", [P, KD, SLOTS], F32R)
        ye = sb("ye", [SLOTS, 2, D])
        raw_loaded = [sem(f"raw_loaded{i}") for i in range(RAW)]
        xe_loaded, rows_added = g["xe_loaded"], g["rows_added"]
        (split_free, hi_ready, lo_ready, xe_turned, xhi_ready, xlo_ready, gate_tanh, hid_ready,
         hid_turned, hhi_ready, hlo_ready, ye_free, ye_ready, down_free) = (
            sem("exp_" + n) for n in (
                "split_free", "hi_ready", "lo_ready", "xe_turned", "xhi_ready", "xlo_ready",
                "gate_tanh", "hid_ready", "hid_turned", "hhi_ready", "hlo_ready", "ye_free", "ye_ready", "down_free"))
        chain_sem = sem("exp_vector_chain")

        def each_pair(eng, body):
            with eng.Fori(0, NE // 2 - 1) as q:
                for j in range(2):
                    body(q * 2 + j, q, j, False)
            for j in range(2):
                body(NE - 2 + j, NE // 2 - 1, j, j == 1)

        @block.sync
        def _(sp):
            def load(e, j, u):
                i = UNITS * j + u
                src = io[WEIGHTS[u // 2]][bass.ds(layer, 1), bass.ds(e, 1)] if not isinstance(e, int) else \
                    io[WEIGHTS[u // 2]][bass.ds(layer, 1), e:e + 1]
                half = slice((u % 2) * 512, (u % 2 + 1) * 512)
                sp.dma_start(raw[:, i % RAW], src.rearrange("l e (k p) n -> p (l e k) n", p=P)[:, :, half]).then_inc(
                    raw_loaded[i % RAW], 16)

            def expert(e, q, j, last_one):
                for u in range(UNITS - RAW if last_one else UNITS):
                    sp.wait_ge(lo_ready, e * (2 * UNITS) + 2 * (u + 1))
                    ahead = u + RAW
                    load(e + ahead // UNITS, (j + ahead // UNITS) % 2, ahead % UNITS)

            for u in range(RAW):
                load(0, 0, u)
            each_pair(sp, expert)

        @block.gpsimd
        def _(pool):
            def gather(e):
                pool.indirect_dma_start(out=xe[:, e % 2, :], out_offset=None, in_=io["tok_rows"],
                                        in_offset=bass.IndirectOffsetOnAxis(rows[:, e:e + 1], 0)).then_inc(xe_loaded[e % 2], 16)

            pool.sem_inc(ye_free, 2)
            gather(0)
            gather(1)
            for e in range(NE):
                if e + 2 < NE:
                    pool.wait_ge(xe_turned, e + 1)
                    gather(e + 2)
                pool.wait_ge(ye_ready, e + 1)
                pool.indirect_dma_start(out=io["sum_rows"], out_offset=bass.IndirectOffsetOnAxis(rows[:, e:e + 1], 0),
                                        in_=ye[:, e % 2, :], in_offset=None, compute_op=ALU.add).then_inc(rows_added, 16)
                pool.wait_ge(rows_added, layer * (16 * NE) + 16 * (e + 1))
                pool.sem_inc(ye_free, 1)

        @block.tensor
        def _(pe):
            def turn_tokens(e, q, j):
                pe.wait_ge(xe_loaded[j], layer * (8 * NE) + (q * 16 + 16))
                for k in range(KD):
                    last = pe.transpose(ps[:, 4 + k // 4, (k % 4) * SLOTS:(k % 4 + 1) * SLOTS], xe[:, j, k * P:(k + 1) * P],
                                        cst[0:SLOTS, C_ID:C_ID + SLOTS])
                last.then_inc(xe_turned, 1)

            def unit(e, j, u, bank, hi, lo):
                for kh in range(2):
                    s = (2 * (UNITS * j + u) + kh) % SPLIT
                    pe.wait_ge(lo_ready, e * (2 * UNITS) + (2 * u + kh + 1))
                    for k in range(KH * kh, KH * kh + KH):
                        w = k % KH
                        pe.matmul(ps[0:SLOTS, bank, :], hi[:, k, :], whi[:, s, w, :], start=(k == 0), stop=False)
                        pe.matmul(ps[0:SLOTS, bank, :], hi[:, k, :], wlo[:, s, w, :], start=False, stop=False)
                        last = pe.matmul(ps[0:SLOTS, bank, :], lo[:, k, :], whi[:, s, w, :], start=False, stop=(k == KD - 1))
                    last.then_inc(split_free, 1)

            def expert(e, q, j, last_one):
                pe.wait_ge(xlo_ready, e + 1)
                for u in range(4):
                    unit(e, j, u, u, xhi, xlo)
                if not last_one:
                    turn_tokens(e + 1, q + 1 if j else q, 1 - j)
                pe.wait_ge(hid_ready, e + 1)
                pe.wait_ge(down_free, e + 1)
                for k in range(KD):
                    last = pe.transpose(ps[:, 6 + k // 4, (k % 4) * SLOTS:(k % 4 + 1) * SLOTS], hid[:, k * P:(k + 1) * P],
                                        cst[0:SLOTS, C_ID:C_ID + SLOTS])
                last.then_inc(hid_turned, 1)
                pe.wait_ge(hlo_ready, e + 1)
                for u in (4, 5):
                    unit(e, j, u, 2 + u, hhi, hlo)

            pe.sem_inc(split_free, SPLIT)
            turn_tokens(0, 0, 0)
            each_pair(pe, expert)

        @block.scalar
        def _(act):
            def split_hi(e, q, j, u):
                if u == UNITS:
                    e, q, j, u = e + 1, q + j, 1 - j, 0
                i = UNITS * j + u
                act.wait_ge(raw_loaded[i % RAW], q * (16 * 2 * UNITS // RAW) + 16 * (i // RAW + 1))
                for kh in range(2):
                    act.wait_ge(split_free, e * (2 * UNITS) + (2 * u + kh + 1))
                    act.activation(whi[:, (2 * i + kh) % SPLIT], raw[:, i % RAW, KH * kh:KH * kh + KH], ACT.Copy).then_inc(hi_ready, 1)

            def tokens_hi(e):
                act.wait_ge(xe_turned, e + 1)
                act.activation(xhi[:].rearrange("p (a b) c -> p a (b c)", a=2), turned(4), ACT.Copy).then_inc(xhi_ready, 1)

            def expert(e, q, j, last_one):
                for u in (1, 2, 3):
                    split_hi(e, q, j, u)
                act.wait_ge(split_free, e * (2 * UNITS) + (SPLIT + 4))
                act.activation(hid[:], pair(0, SLOTS, FF), ACT.Tanh, scale=0.5).then_inc(gate_tanh, 1)
                split_hi(e, q, j, 4)
                split_hi(e, q, j, 5)
                act.wait_ge(hid_turned, e + 1)
                act.activation(hhi[:].rearrange("p (a b) c -> p a (b c)", a=2), turned(6), ACT.Copy).then_inc(hhi_ready, 1)
                if not last_one:
                    tokens_hi(e + 1)
                    split_hi(e, q, j, UNITS)
                act.wait_ge(split_free, e * (2 * UNITS) + (SPLIT + 2 * UNITS))
                act.wait_ge(ye_free, e + 1)
                act.activation(ye[:, j, :], pair(6, SLOTS, D), ACT.Copy, scale=weight[:, bass.ds(e, 1)] if not isinstance(e, int)
                               else weight[:, e:e + 1]).then_inc(ye_ready, 1)
                act.sem_inc(down_free, 1)

            act.sem_inc(down_free, 1)
            tokens_hi(0)
            split_hi(0, 0, 0, 0)
            each_pair(act, expert)

        @block.vector
        def _(v):
            def split_lo(e, j, u):
                if u == UNITS:
                    e, j, u = e + 1, 1 - j, 0
                i = UNITS * j + u
                for kh in range(2):
                    s = (2 * i + kh) % SPLIT
                    v.wait_ge(hi_ready, e * (2 * UNITS) + (2 * u + kh + 1))
                    v.tensor_tensor(wlo[:, s], raw[:, i % RAW, KH * kh:KH * kh + KH], whi[:, s].bitcast(F32),
                                    ALU.subtract).then_inc(lo_ready, 1)

            def tokens_lo(e):
                v.wait_ge(xhi_ready, e + 1)
                v.tensor_tensor(xlo[:].rearrange("p (a b) c -> p a (b c)", a=2), turned(4),
                                xhi[:].bitcast(F32).rearrange("p (a b) c -> p a (b c)", a=2), ALU.subtract).then_inc(xlo_ready, 1)

            def expert(e, q, j, last_one):
                chain = LoopCount(chain_sem, e, 1)
                for u in (1, 2, 3):
                    split_lo(e, j, u)
                v.wait_ge(gate_tanh, e + 1)
                chain.link(v, v.scalar_tensor_tensor(out=hid[:], in0=hid[:], scalar=1.0, in1=pair(0, SLOTS, FF),
                                                     op0=ALU.add, op1=ALU.mult))
                split_lo(e, j, 4)
                v.wait_ge(split_free, e * (2 * UNITS) + (SPLIT + 8))
                v.scalar_tensor_tensor(out=hid[:], in0=hid[:], scalar=0.5, in1=pair(2, SLOTS, FF),
                                       op0=ALU.mult, op1=ALU.mult).then_inc(hid_ready, 1)
                v.wait_ge(hhi_ready, e + 1)
                v.tensor_tensor(hlo[:].rearrange("p (a b) c -> p a (b c)", a=2), turned(6),
                                hhi[:].bitcast(F32).rearrange("p (a b) c -> p a (b c)", a=2), ALU.subtract).then_inc(hlo_ready, 1)
                if not last_one:
                    tokens_lo(e + 1)
                split_lo(e, j, 5)
                if not last_one:
                    split_lo(e, j, UNITS)
                assert chain.n == chain.per

            tokens_lo(0)
            split_lo(0, 0, 0)
            each_pair(v, expert)


def add_experts(nc, io, g):
    ps, cst, x, mod = g["ps"], g["cst"], g["x"], g["mod"]
    with stage(nc) as (block, sem, sb):
        tok = sb("sum_tok", [P, NT, D])
        loaded = [sem(f"sum_loaded{t}") for t in range(NT)]
        tok_turned, x_added = sem("sum_turned"), sem("sum_added")

        @block.sync
        def _(sp):
            for t in range(NT):
                sp.dma_start(tok[:, t, :], io["sum_rows"][t * P:(t + 1) * P, :]).then_inc(loaded[t], 16)

        @block.tensor
        def _(pe):
            for t in range(NT):
                pe.wait_ge(loaded[t], 16)
                if t >= 4:
                    pe.wait_ge(x_added, t - 3)
                for k in range(KD):
                    last = pe.transpose(ps[:, 2 * (t % 4) + k // 4, (k % 4) * P:(k % 4 + 1) * P],
                                        tok[:, t, k * P:(k + 1) * P], cst[:, C_ID:C_ID + P])
                last.then_inc(tok_turned, 1)

        @block.vector
        def _(v):
            for t in range(NT):
                grp = int(t == NT - 1)
                v.wait_ge(tok_turned, t + 1)
                for k in range(KD):
                    dst = x[:, k, t * P:(t + 1) * P]
                    last = v.scalar_tensor_tensor(out=dst, in0=ps[:, 2 * (t % 4) + k // 4, (k % 4) * P:(k % 4 + 1) * P],
                                                  scalar=mod[:, 40 + k, grp:grp + 1], in1=dst, op0=ALU.mult, op1=ALU.add)
                last.then_inc(x_added, 1)


def finish(nc, io, g):
    norm(nc, g, "nf", g["fin"], None)
    with stage(nc) as (block, sem, sb):
        y_out = sem("y_out")

        @block.sync
        def _(sp):
            sp.dma_start(io["y"], g["h"][:]).then_inc(y_out, 16)
            sp.wait_ge(y_out, 16)


def constants():
    c = np.zeros((P, C_END), np.float32)
    i, j = np.arange(P)[:, None], np.arange(P)[None, :]
    c[:, C_ID:C_ID + P] = i == j
    c[:, C_LE:C_LE + P] = i <= j
    c[:, C_GE:C_GE + P] = i >= j
    c[:, C_ROT:C_ROT + P] = np.where((i == j + 1) & (j % 2 == 0), -1.0, 0.0) + np.where((i == j - 1) & (j % 2 == 1), 1.0, 0.0)
    c[:, C_BLK:C_BLK + P] = i // 64 == j // 64
    c[:, C_ONE:C_ONE + P] = 1.0
    c[:, C_SLOT:C_SLOT + SLOTS] = np.arange(SLOTS)
    col, kc = np.arange(P)[:, None] % GRID_W, np.arange(GRID_W)[None, :]
    start = np.clip(col - 8, 0, GRID_W - 16)
    c[:, C_WIN:C_WIN + GRID_W] = np.where((kc >= start) & (kc < start + 16), 0.0, -1e30)
    quarter = ROPE // 4
    inv = (10000.0 ** (-np.arange(quarter, dtype=np.float32) / quarter)).astype(np.float32)
    f = (np.arange(P) % ROPE) // 2
    tok = np.arange(SAMPLE)
    at = np.where(f[:, None] < quarter, (tok // GRID_W)[None, :], (tok % GRID_W)[None, :]).astype(np.float32)
    angle = at * inv[f % quarter][:, None]
    c[:, C_COS:C_COS + SAMPLE] = np.cos(angle)
    c[:, C_SIN:C_SIN + SAMPLE] = np.sin(angle)
    c[:, C_TOK:C_TOK + NT] = np.arange(NT)[None, :] * P + np.arange(P)[:, None]
    return c


def lay_out(a):
    L = DEPTH

    def feat(x, chunks):
        return x.reshape(x.shape[0], chunks, P).transpose(2, 1, 0)

    def cols(x):
        return x.reshape(L, -1, P).transpose(0, 2, 1)

    def everywhere(x):
        x = x.reshape(L, 1, -1)
        return np.broadcast_to(x, (L, P, x.shape[2]))

    o = {"cst": constants()}
    o["x"] = feat(np.concatenate([a["x_sample"][0], a["x_prompt"][0]]), KD)
    o["cond"] = feat(np.stack([a["c"][0], a["c_ctx"]]), KD)
    o["fin"] = a["final_norm_g"].reshape(KD, P).T
    lam_init = np.array([[0.8 - 0.6 * math.exp(-0.3 * i), 1.0 - (0.8 - 0.6 * math.exp(-0.3 * i))] for i in range(L)], np.float32)
    cw = a["ssm_conv_w"].reshape(L, 3, 4, P).transpose(0, 3, 1, 2).reshape(L, P, 12)
    o["vec"] = np.concatenate([
        cols(a["mod_b"]), cols(a["norm1_g"]), cols(a["norm2_g"]), cols(a["mla_q_norm_g"]), cols(a["mla_kv_norm_g"]),
        np.tile(a["df_subln_g"], (1, 2))[:, :, None], cw, cols(a["ssm_conv_b"]), everywhere(a["ssm_dt_bias"]),
        everywhere(a["ssm_a_log"]), cols(np.repeat(a["ssm_d"], 64, axis=1)), cols(a["ssm_norm_g"]),
        everywhere(a["df_lambda"]), everywhere(lam_init)], axis=2)
    w = a["w_in"]
    part = lambda first, n: w[:, :, first:first + n]
    o["w_mix"] = np.concatenate([part(O_NAQ, 256), part(O_NAK, 256), part(O_CQ, QR), part(O_CKV, KVR)]
                                + [part(O_KR, ROPE)] * 4
                                + [part(O_DFQ, 256), part(O_DFK, 256), part(O_SX, 256), part(O_SB, P), part(O_SC, P),
                                   part(O_SZ, 256), part(O_NAV, 256), part(O_DFV, 256), part(O_DT, 8)], axis=2)
    uq = a["mla_w_uq"].reshape(L, QR, HEADS, 96)
    o["w_uq"] = np.concatenate([uq[..., :64].reshape(L, QR, 256), uq[..., 64:].reshape(L, QR, 128)], axis=2)
    ukv = a["mla_w_ukv"].reshape(L, KVR, HEADS, 128)
    o["w_ukv"] = np.concatenate([ukv[..., :64].reshape(L, KVR, 256), ukv[..., 64:].reshape(L, KVR, 256)], axis=2)
    rows = []
    for i in range(L):
        rows.append(np.concatenate([
            feat(a["cache_na_k"][0, i].reshape(CTX, 256), 2), feat(a["cache_df_k"][0, i].reshape(CTX, 256), 2),
            feat(a["cache_mla_ckv"][0, i], 2), feat(np.tile(a["cache_mla_krope"][0, i], (1, 4)), 1)], axis=1))
    o["ctx_k"] = np.stack(rows)
    o["ctx_v"] = np.concatenate([a["cache_na_v"][0].reshape(L, CTX, 256), a["cache_df_v"][0].reshape(L, CTX, 256)], axis=2)
    o["state"] = a["state_ssm"][0].reshape(L, 2, 2, 2, 64, 64).transpose(0, 2, 5, 1, 3, 4).reshape(L, P, 2, 2, 64)
    rel = np.zeros((L, HEADS, 17, 2 * GRID_W), a["na_rel_bias"].dtype)
    rel[:, :, 1:16, BIAS_MID - 15:BIAS_MID + 16] = a["na_rel_bias"]
    bias = np.zeros((L, P, HEADS, 16, GRID_W), rel.dtype)
    for c in range(GRID_W):
        bias[:, c] = rel[:, :, 1:17, BIAS_MID - c:BIAS_MID - c + GRID_W]
        bias[:, GRID_W + c] = rel[:, :, 0:16, BIAS_MID - c:BIAS_MID - c + GRID_W]
    o["bias"] = bias
    for n in ("mod_w", "w_in", "w_out", "w_branch", "router_w", "exp_w_gate", "exp_w_up", "exp_w_down"):
        o[n] = a[n]
    return {n: np.ascontiguousarray(v) for n, v in o.items()}


OUTS = {"y": (P, KD, T), "new_k": (DEPTH, P, K_N, PROMPT), "new_v": (DEPTH, PROMPT, 512), "new_state": (DEPTH, P, 2, 2, 64)}


def collect(r):
    y, nk, nv, ns = (np.asarray(r[f"out_{n}"]) for n in OUTS)
    L = DEPTH
    y = y.transpose(2, 1, 0).reshape(T, D)

    def keys(first, n):
        return nk[:, :, first:first + n].transpose(0, 3, 2, 1).reshape(1, L, PROMPT, n * P)

    state = ns.reshape(L, 2, 64, 2, 2, 64).transpose(0, 3, 1, 4, 5, 2).reshape(1, L, 2, HEADS, 64, 64)
    return (y[None, SAMPLE:], y[None, :SAMPLE], keys(K_NA, 2).reshape(1, L, PROMPT, HEADS, 64),
            nv[:, :, :256].reshape(1, L, PROMPT, HEADS, 64), keys(K_CKV, 2), keys(K_KR, 1)[..., :ROPE],
            keys(K_DF, 2).reshape(1, L, PROMPT, HEADS, 2, 32), nv[:, :, 256:].reshape(1, L, PROMPT, HEADS, 64), state)


def kernel(**inputs):
    import concourse.bacc as bacc
    from concourse.bass_utils import run_bass_kernel_spmd

    arrays = lay_out({n: np.asarray(v) for n, v in inputs.items()})
    nc = bacc.Bacc("TRN2", target_bir_lowering=False, num_devices=1)
    io = {n: nc.dram_tensor(f"in_{n}", a.shape, mybir.dt.from_np(a.dtype), kind="ExternalInput").ap() for n, a in arrays.items()}
    for n, shape in OUTS.items():
        io[n] = nc.dram_tensor(f"out_{n}", shape, F32, kind="ExternalOutput").ap()
    for n in ("tok_rows", "sum_rows"):
        io[n] = nc.dram_tensor(n, (T, D), F32).ap()
    build(nc, io)
    r = run_bass_kernel_spmd(nc, [{f"in_{n}": a for n, a in arrays.items()}], core_ids=[0])
    return tuple(np.ascontiguousarray(v) for v in collect(r.results[0]))
```

```python
import math
from contextlib import ExitStack, contextmanager

import numpy as np

import concourse.bass as bass
from concourse import mybir

F32 = mybir.dt.float32
F32R = mybir.dt.float32r
ALU = mybir.AluOpType
ACT = mybir.ActivationFunctionType
AXX = mybir.AxisListType.X

P = 128
D = 1024
KD = D // P
SAMPLE, PROMPT, CTX = 512, 128, 128
T = SAMPLE + PROMPT
NT = T // P
KEYS = SAMPLE + CTX + PROMPT
OWN_P = SAMPLE + CTX
DEPTH = 2
GRID_W = 64
ROWS = SAMPLE // GRID_W
EPS = 1e-6
HEADS = 4
NE = 16
FF = 1024
CAP_S, CAP_P = 2 * SAMPLE // NE, 2 * PROMPT // NE
SLOTS = CAP_S + CAP_P
QR, KVR, ROPE = 384, 256, 32
NA_DY, NA_DX = 15, 31
BIAS_W = 128
BIAS_MID = GRID_W - 1
O_NAQ, O_NAK, O_NAV, O_CQ, O_CKV, O_KR = 0, 256, 512, 768, 1152, 1408
O_DFQ, O_DFK, O_DFV, O_SX, O_SZ, O_SB, O_SC, O_DT, O_GATE = 1440, 1696, 1952, 2208, 2464, 2720, 2848, 2976, 2984
IN_W = O_GATE + 4 * D
GROUPS = ((0, 0, SAMPLE), (1, SAMPLE, T))


class Count:

    def __init__(self, sem):
        self.sem, self.n = sem, 0

    def mark(self, ins):
        self.n += 1
        ins.then_inc(self.sem, 1)
        return self.n

    def link(self, eng, ins):
        self.mark(ins)
        eng.wait_ge(self.sem, self.n)


class Load:

    def __init__(self, sem):
        self.sem, self.n = sem, 0

    def start(self, eng, out, in_):
        self.n += 1
        eng.dma_start(out, in_).then_inc(self.sem, 16)

    @property
    def total(self):
        return 16 * self.n


@contextmanager
def stage(nc):
    with ExitStack() as own:
        sems = []

        def sem(name):
            s = own.enter_context(nc.semaphore(name))
            sems.append(s.num)
            return s

        def sb(name, shape, dt=F32):
            return own.enter_context(nc.sbuf_tensor(name, shape, dt))

        block = ExitStack()
        b = block.enter_context(nc.Block())
        yield b, sem, sb
        block.close()
        nc.all_engine_barrier(sems_to_clear=range(min(sems), max(sems) + 1))


def layer_row(ap, layer):
    names = " ".join(f"d{i}" for i in range(len(ap.shape) - 1))
    first, rest = ("d0", names.split(" ", 1)[1] if " " in names else "")
    return ap[bass.ds(layer, 1)].rearrange(f"l {names} -> (l {first}) {rest}".strip())


def chunk_columns(vec):
    return vec.rearrange("(c p) -> p c", p=P)


C_ID, C_LE, C_GE, C_ROT, C_BLK, C_ONE, C_SLOT, C_WIN = 0, 128, 256, 384, 512, 640, 768, 768 + SLOTS
C_COS = C_WIN + GRID_W
C_SIN = C_COS + SAMPLE
C_TOK = C_SIN + SAMPLE
C_PAIR = C_TOK + NT
C_END = C_PAIR + 2
V_MODB, V_N1, V_N2, V_QG, V_KVG, V_SUB, V_CW, V_CB, V_DTB, V_ALOG, V_SD, V_SG, V_LAM = (
    0, 48, 56, 64, 67, 69, 70, 82, 86, 94, 102, 104, 106)
V_LI = V_LAM + 128
V_END = V_LI + 2
FEATURE_CHUNKS = 20
M_V = FEATURE_CHUNKS * P
M_DT = M_V + 512
M_END = M_DT + 8
K_NA, K_DF, K_CKV, K_KR, K_N = 0, 2, 4, 6, 7
SXW = T + 4
SX_S, SX_P = 1, SAMPLE + 3


def pcol(t):
    return t * P if t < NT - 1 else SAMPLE + 2


def build(nc, io):
    with ExitStack() as whole:
        def sb(name, shape, dt=F32):
            return whole.enter_context(nc.sbuf_tensor(name, shape, dt))

        g = {}
        g["ps"] = whole.enter_context(nc.psum_tensor("ps", [P, 8, 512], F32))
        g["cst"] = sb("cst", [P, C_END])
        g["x"] = sb("x", [P, KD, T])
        g["h"] = sb("h", [P, KD, T])
        g["vec"] = sb("vec", [P, V_END])
        g["cond"] = sb("cond", [P, KD, 2])
        g["mod"] = sb("mod", [P, 48, 2])
        g["gs1"] = sb("gs1", [P, KD, 2])
        g["gs2"] = sb("gs2", [P, KD, 2])
        g["fin"] = sb("fin", [P, KD])
        g["xe_loaded"] = [whole.enter_context(nc.semaphore(f"xe_loaded{i}")) for i in range(2)]
        g["rows_added"] = whole.enter_context(nc.semaphore("rows_added"))
        for name, slots in (("mod_raw_loaded", 4), ("in_raw_loaded", 2), ("merge_raw_loaded", 2), ("expert_raw_loaded", 4)):
            g[name] = [whole.enter_context(nc.semaphore(f"{name}{i}")) for i in range(slots)]
        with nc.sbuf_tensor("mod_raw", MOD_RAW, F32) as place:
            g["mod_raw"] = place

        def tensor(scope, name, shape, dt=F32, side=None):
            g[name] = scope.enter_context(nc.sbuf_tensor(name, shape, dt, side=side))

        begin(nc, io, g)
        with nc.Fori(0, DEPTH) as layer:
            modulation(nc, io, g, layer)
            with ExitStack() as heads, ExitStack() as branches:
                in_weights = ExitStack()
                tensor(in_weights, "in_raw", IN_RAW, side="right")
                norm(nc, g, "n1", g["gs1"], g["mod"][:, 0:8, :], lambda sp: [load_in(sp, io, g, layer, i) for i in range(IN_RAW[1])])
                tensor(heads, "sx", [P, 4, SXW])
                tensor(heads, "sz", [P, 2, T])
                tensor(heads, "dtr", [P, NT, 8])
                with ExitStack() as attn:
                    tensor(attn, "kt", [P, K_N, KEYS])
                    tensor(attn, "qt", [P, 4, T])
                    tensor(attn, "v", [P, 6, 512])
                    tensor(attn, "cq", [P, 3, T])
                    projections(nc, io, g, layer)
                    in_weights.close()
                    tensor(branches, "br", [P, 4, 2, T], side="right")
                    for name, shape in (("qn", [P, 2, T]), ("qr", [P, T]), ("kn", [P, 2, KEYS]), ("mv", [P, 6, 256]),
                                        ("bias", [P, HEADS, 16, GRID_W])):
                        tensor(attn, name, shape)
                    latent_heads(nc, io, g, layer)
                    attention(nc, io, g, layer)
                tensor(branches, "merge_raw", MERGE_RAW, side="right")
                ssm(nc, io, g, layer)
                heads.close()
                merge(nc, io, g, layer)
            norm(nc, g, "n2", g["gs2"], g["mod"][:, 24:32, :])
            with ExitStack() as moe:
                tensor(moe, "expert_raw", EXPERT_RAW)
                tensor(moe, "rows", [SLOTS, NE], mybir.dt.uint32)
                tensor(moe, "weight", [SLOTS, NE])
                with ExitStack() as route:
                    for name, shape in (("htok", [P, NT, D]), ("pos", [P, NT, NE]), ("aff", [P, NT, NE])):
                        tensor(route, name, shape)
                    router(nc, io, g, layer)
                    choose(nc, io, g)
                experts(nc, io, g, layer)
            add_experts(nc, io, g, layer)
        with nc.sbuf_tensor("mod_raw_last", MOD_RAW, F32):
            finish(nc, io, g)


MOD_RAW = [P, 4, KD, 512]
IN_RAW, MERGE_RAW, EXPERT_RAW = [P, 2, KD, 2 * P + 4], [P, 2, KD + 2, 2 * P], [P, 4, KD, 512]
FEATURE_UNITS = FEATURE_CHUNKS // 2


def load_mod(sp, io, g, layer, n):
    src = io["mod_w"][bass.ds(layer, 1)] if not isinstance(layer, int) else io["mod_w"][layer:layer + 1]
    sp.dma_start(g["mod_raw"][:, n % 4], src.rearrange("l (k p) n -> p (l k) n", p=P)[:, :, n * 512:(n + 1) * 512]).then_inc(
        g["mod_raw_loaded"][n % 4], 16)


def in_unit(i):
    return (i * 2 * P, 2 * P) if i < FEATURE_UNITS else (M_V + (i - FEATURE_UNITS) * IN_RAW[3], IN_RAW[3])


def load_in(sp, io, g, layer, i):
    c, n = in_unit(i)
    sp.dma_start(g["in_raw"][:, i % 2, :, 0:n], layer_row(io["w_mix"], layer).rearrange("(k p) n -> p k n", p=P)[:, :, c:c + n]).then_inc(
        g["in_raw_loaded"][i % 2], 16)


GATE_UNITS, OUT_UNITS = 4 * KD // 2, KD // 2


def merge_loads(i):
    return 32 if i < GATE_UNITS else 16


def load_merge(sp, io, g, layer, i):
    raw, loaded, W = g["merge_raw"][:, i % 2], g["merge_raw_loaded"][i % 2], MERGE_RAW[3]
    if i < GATE_UNITS:
        w_gate = layer_row(io["w_in"], layer)[:, O_GATE:IN_W].rearrange("(k p) n -> p k n", p=P)
        n, c = divmod(i * W, D)
        sp.dma_start(raw[:, 0:KD], w_gate[:, :, i * W:(i + 1) * W]).then_inc(loaded, 16)
        w_branch = layer_row(io["w_branch"], layer).rearrange("n (k p) d -> n p k d", p=P)
        sp.dma_start(raw[:, KD:KD + 2], w_branch[n][:, :, c:c + W]).then_inc(loaded, 16)
    else:
        c = (i - GATE_UNITS) * W
        sp.dma_start(raw[:, 0:KD], layer_row(io["w_out"], layer).rearrange("(k p) n -> p k n", p=P)[:, :, c:c + W]).then_inc(loaded, 16)


EXPERT_UNITS = 6


def load_expert(sp, io, g, layer, e, matrix, half, slot):
    src = io[("exp_w_gate", "exp_w_up", "exp_w_down")[matrix]][bass.ds(layer, 1)]
    src = src[:, e:e + 1] if isinstance(e, int) else src[:, bass.ds(e, 1)]
    columns = slice(half * 512, (half + 1) * 512)
    sp.dma_start(g["expert_raw"][:, slot], src.rearrange("l e (k p) n -> p (l e k) n", p=P)[:, :, columns]).then_inc(
        g["expert_raw_loaded"][slot], 16)


def begin(nc, io, g):
    with stage(nc) as (block, sem, sb):
        sb("mod_raw_begin", MOD_RAW)
        start_loads = Load(sem("start_loads"))

        @block.sync
        def _(sp):
            start_loads.start(sp, g["cst"][:], io["cst"])
            start_loads.start(sp, g["x"][:], io["x"])
            start_loads.start(sp, g["cond"][:], io["cond"])
            start_loads.start(sp, g["fin"][:], io["fin"])
            for n in range(MOD_RAW[1]):
                load_mod(sp, io, g, 0, n)
            sp.wait_ge(start_loads.sem, start_loads.total)


def modulation(nc, io, g, layer):
    ps, vec, mod, cst = g["ps"], g["vec"], g["mod"], g["cst"]
    raw, raw_loaded = g["mod_raw"], g["mod_raw_loaded"]
    NCH, RAW, SPLIT, KH = 12, MOD_RAW[1], 4, KD // 2
    with stage(nc) as (block, sem, sb):
        sb("mod_raw_place", MOD_RAW)
        whi = sb("mod_w_hi", [P, SPLIT, KH, 512], F32R)
        wlo = sb("mod_w_lo", [P, SPLIT, KH, 512], F32R)
        th = sb("mod_tanh", [P, KD, 2])
        th2 = sb("mod_tanh_gated", [P, KD, 2])
        sc = sb("mod_sc", [P, KD, 2])
        scs = sb("mod_sc_split", [P, KD, 4], F32R)
        rows = sb("mod_rows", [4, NCH * 512])
        vec_loaded = sem("vec_loaded")
        w_hi_ready, w_lo_ready, half_done, tanh_done, rows_done, cols_done = (
            sem(n) for n in ("mod_w_hi_ready", "mod_w_lo_ready", "mod_half_done", "mod_tanh_done", "mod_rows_done", "mod_cols_done"))
        silu = Count(sem("mod_silu"))

        @block.sync
        def _(sp):
            sp.dma_start(vec[:], layer_row(io["vec"], layer)).then_inc(vec_loaded, 16)
            for n in range(RAW, NCH):
                sp.wait_ge(w_lo_ready, 2 * (n - RAW + 1))
                load_mod(sp, io, g, layer, n)

        @block.scalar
        def _(act):
            act.activation(th[:], g["cond"][:], ACT.Tanh, scale=0.5).then_inc(tanh_done, 1)
            for n in range(NCH):
                act.wait_ge(raw_loaded[n % RAW], layer * (16 * NCH // RAW) + 16 * (n // RAW + 1))
                for i in (2 * n, 2 * n + 1):
                    if i >= SPLIT:
                        act.wait_ge(half_done, i - SPLIT + 1)
                    act.activation(whi[:, i % SPLIT], raw[:, n % RAW, KH * (i % 2):KH * (i % 2 + 1)], ACT.Copy).then_inc(w_hi_ready, 1)

        @block.tensor
        def _(pe):
            pe.wait_ge(silu.sem, 4)

            def columns(n):
                pe.wait_ge(rows_done, n + 1)
                for j in range(4 * n, 4 * n + 4):
                    last = pe.matmul(ps[:, 7, 2 * j:2 * j + 2], rows[:, j * P:(j + 1) * P], cst[0:4, C_PAIR:C_PAIR + 2],
                                     start=True, stop=True)
                last.then_inc(cols_done, 1)

            for n in range(NCH):
                if n >= 4:
                    pe.wait_ge(rows_done, n - 3)
                for i in (2 * n, 2 * n + 1):
                    pe.wait_ge(w_lo_ready, i + 1)
                    for kk in range(KH):
                        k = KH * (i % 2) + kk
                        pe.matmul(ps[0:4, n % 4, :], scs[:, k, :], whi[:, i % SPLIT, kk, :], start=(k == 0), stop=False)
                        last = pe.matmul(ps[0:4, n % 4, :], scs[:, k, :], wlo[:, i % SPLIT, kk, :], start=False, stop=(k == KD - 1))
                    last.then_inc(half_done, 1)
                if n >= 1:
                    columns(n - 1)
            columns(NCH - 1)

        @block.vector
        def _(v):
            v.wait_ge(tanh_done, 1)
            silu.link(v, v.scalar_tensor_tensor(out=th2[:], in0=th[:], scalar=1.0, in1=g["cond"][:], op0=ALU.add, op1=ALU.mult))
            silu.link(v, v.tensor_scalar(sc[:], th2[:], 0.5, None, ALU.mult))
            silu.link(v, v.tensor_copy(scs[:, :, 0:2], sc[:]))
            silu.link(v, v.tensor_tensor(scs[:, :, 2:4], sc[:], scs[:, :, 0:2].bitcast(F32), ALU.subtract))

            def copy_rows(n):
                v.wait_ge(half_done, 2 * n + 2)
                v.tensor_copy(rows[:, n * 512:(n + 1) * 512], ps[0:4, n % 4, :]).then_inc(rows_done, 1)

            for n in range(NCH):
                for i in (2 * n, 2 * n + 1):
                    v.wait_ge(w_hi_ready, i + 1)
                    v.tensor_tensor(wlo[:, i % SPLIT], raw[:, n % RAW, KH * (i % 2):KH * (i % 2 + 1)],
                                    whi[:, i % SPLIT].bitcast(F32), ALU.subtract).then_inc(w_lo_ready, 1)
                if n >= 1:
                    copy_rows(n - 1)
            copy_rows(NCH - 1)
            v.wait_ge(cols_done, NCH)
            v.wait_ge(vec_loaded, 16)
            silu.link(v, v.tensor_tensor(mod[:], ps[:, 7, 0:96].rearrange("p (a b) -> p a b", b=2),
                                         vec[:, V_MODB:V_MODB + 48].unsqueeze(2).broadcast_to([P, 48, 2]), ALU.add))
            for gs, first, gain in ((g["gs1"], 8, V_N1), (g["gs2"], 32, V_N2)):
                silu.mark(v.scalar_tensor_tensor(
                    out=gs[:], in0=mod[:, first:first + 8, :], scalar=1.0,
                    in1=vec[:, gain:gain + 8].unsqueeze(2).broadcast_to([P, KD, 2]), op0=ALU.add, op1=ALU.mult))


def norm(nc, g, name, gain, shift, fetch=None, store=None):
    ps, x, h, cst = g["ps"], g["x"], g["h"], g["cst"]
    with stage(nc) as (block, sem, sb):
        sq = sb(name + "_sq", [P, 4, T])
        ms = sb(name + "_ms", [P, T])
        root = sb(name + "_root", [P, T])
        rstd = sb(name + "_rstd", [P, T])
        xn = sb(name + "_xn", [P, 4, T])
        sq_ready, sq_used, ms_ready, root_ready, rstd_ready, xn_ready, h_ready = (
            sem(name + s) for s in ("_sq_ready", "_sq_used", "_ms_ready", "_root_ready", "_rstd_ready", "_xn_ready", "_h_ready"))
        h_prompt_ready, stored = sem(name + "_h_prompt_ready"), sem(name + "_stored")

        @block.sync
        def _(sp):
            if fetch:
                fetch(sp)
            if store is not None:
                for k in range(KD):
                    sp.wait_ge(h_ready, k + 1)
                    sp.dma_start(store[:, k], h[:, k]).then_inc(stored, 16)
                sp.wait_ge(stored, 16 * KD)

        @block.scalar
        def _(act):
            for k in range(KD):
                if k >= 4:
                    act.wait_ge(sq_used, k - 3)
                act.activation(sq[:, k % 4], x[:, k], ACT.Square).then_inc(sq_ready, 1)
            act.wait_ge(ms_ready, 1)
            act.activation(root[:], ms[:], ACT.Sqrt).then_inc(root_ready, 1)
            if shift is not None:
                for k in range(KD):
                    act.wait_ge(xn_ready, k + 1)
                    act.activation(h[:, k, 0:SAMPLE], xn[:, k % 4, 0:SAMPLE], ACT.Identity,
                                   bias=shift[:, k, 0:1], scale=gain[:, k, 0:1]).then_inc(h_ready, 1)

        @block.gpsimd
        def _(pool):
            if shift is not None:
                for k in range(KD):
                    pool.wait_ge(xn_ready, k + 1)
                    pool.tensor_scalar(h[:, k, SAMPLE:T], xn[:, k % 4, SAMPLE:T], gain[:, k, 1:2], shift[:, k, 1:2],
                                       ALU.mult, ALU.add).then_inc(h_prompt_ready, 1)

        @block.tensor
        def _(pe):
            for k in range(KD):
                pe.wait_ge(sq_ready, k + 1)
                pe.matmul(ps[:, 0, :], cst[:, C_ONE:C_ONE + P], sq[:, k % 4, 0:SAMPLE], start=(k == 0), stop=(k == KD - 1))
                pe.matmul(ps[:, 1, 0:PROMPT], cst[:, C_ONE:C_ONE + P], sq[:, k % 4, SAMPLE:T],
                          start=(k == 0), stop=(k == KD - 1)).then_inc(sq_used, 1)

        @block.vector
        def _(v):
            v.wait_ge(sq_used, KD)
            v.tensor_scalar(ms[:], ps[:, 0:2].rearrange("p a b -> p (a b)")[:, 0:T], 1.0 / D, EPS, ALU.mult, ALU.add).then_inc(ms_ready, 1)
            v.wait_ge(root_ready, 1)
            v.reciprocal(rstd[:], root[:]).then_inc(rstd_ready, 1)
            v.wait_ge(rstd_ready, 1)
            for k in range(KD):
                if shift is None:
                    v.scalar_tensor_tensor(out=h[:, k], in0=x[:, k], scalar=gain[:, k:k + 1], in1=rstd[:],
                                           op0=ALU.mult, op1=ALU.mult).then_inc(h_ready, 1)
                else:
                    if k >= 4:
                        v.wait_ge(h_ready, k - 3)
                        v.wait_ge(h_prompt_ready, k - 3)
                    v.tensor_tensor(xn[:, k % 4], x[:, k], rstd[:], ALU.mult).then_inc(xn_ready, 1)


def projections(nc, io, g, layer):
    ps, h = g["ps"], g["h"]
    kt, qt, v_sb, sx, sz = g["kt"], g["qt"], g["v"], g["sx"], g["sz"]
    raw, raw_loaded = g["in_raw"], g["in_raw_loaded"]
    RAW, SPLIT, WV = 2, 2, IN_RAW[3]
    NU = FEATURE_UNITS + 2
    HALF = T // 2
    HALVES = ((0, HALF, 0), (HALF, T, 1))

    def key(c):
        return [(kt[:, c, 0:HALF], 0, HALF, 0), (kt[:, c, HALF:SAMPLE], HALF, SAMPLE, 1), (kt[:, c, OWN_P:KEYS], SAMPLE, T, 1)]

    def conv(c):
        return [(sx[:, c, SX_S:SX_S + HALF], 0, HALF, 0), (sx[:, c, SX_S + HALF:SX_S + SAMPLE], HALF, SAMPLE, 1),
                (sx[:, c, SX_P:SX_P + PROMPT], SAMPLE, T, 1)]

    def plain(buf, c):
        return [(buf[:, c, :], 0, T, 0)]

    places = ([plain(qt, 0), plain(qt, 1), key(K_NA), key(K_NA + 1)] + [plain(g["cq"], c) for c in range(3)]
              + [key(K_CKV), key(K_CKV + 1), key(K_KR), plain(qt, 2), plain(qt, 3), key(K_DF), key(K_DF + 1)]
              + [conv(c) for c in range(4)] + [plain(sz, 0), plain(sz, 1)])
    assert len(places) == FEATURE_CHUNKS

    def width(i):
        return in_unit(i)[1]

    with stage(nc) as (block, sem, sb):
        whi = sb("in_w_hi", [P, SPLIT, KD, WV], F32R)
        wlo = sb("in_w_lo", [P, SPLIT, KD, WV], F32R)
        h_hi = sb("in_h_hi", [P, KD, T], F32R)
        h_lo = sb("in_h_lo", [P, KD, T], F32R)
        h_hi_ready, h_lo_ready, w_hi_ready, w_lo_ready, ctx_loaded, chunk_done, copied_v, copied_a, pads = (
            sem(n) for n in ("in_h_hi_ready", "in_h_lo_ready", "in_w_hi_ready", "in_w_lo_ready", "ctx_loaded",
                             "in_chunk_done", "in_copied_vector", "in_copied_scalar", "in_pads"))
        ctx = Load(ctx_loaded)

        @block.sync
        def _(sp):
            ctx.start(sp, kt[:, :, SAMPLE:OWN_P], layer_row(io["ctx_k"], layer))
            ctx.start(sp, v_sb[:, 4, :], layer_row(io["ctx_v"], layer))
            for i in range(RAW, NU):
                sp.wait_ge(w_lo_ready, i - RAW + 1)
                load_in(sp, io, g, layer, i)
            sp.wait_ge(ctx_loaded, ctx.total)

        @block.tensor
        def _(pe):
            def free_pair(i):
                if i >= 4:
                    pe.wait_ge(copied_v if i % 2 == 0 else copied_a, (i - 4) // 2 + 1)

            for i in range(FEATURE_CHUNKS):
                s, b = (i // 2) % SPLIT, 2 * (i % 4)
                cols = slice((i % 2) * P, (i % 2 + 1) * P)
                if i % 2 == 0:
                    pe.wait_ge(w_lo_ready, i // 2 + 1)
                free_pair(i)
                for k in range(KD):
                    if i == 0:
                        pe.wait_ge(h_lo_ready, k + 1)
                    for a, z, o in HALVES:
                        dst = ps[:, b + o, 0:HALF]
                        pe.matmul(dst, whi[:, s, k, cols], h_hi[:, k, a:z], start=(k == 0), stop=False)
                        pe.matmul(dst, whi[:, s, k, cols], h_lo[:, k, a:z], start=False, stop=False)
                        last = pe.matmul(dst, wlo[:, s, k, cols], h_hi[:, k, a:z], start=False, stop=(k == KD - 1))
                last.then_inc(chunk_done, 1)
            pe.wait_ge(w_lo_ready, NU)
            for t in range(NT):
                i = FEATURE_CHUNKS + t
                b = 2 * (i % 4)
                toks = slice(t * P, (t + 1) * P)
                free_pair(i)
                for k in range(KD):
                    for o in range(2):
                        s, dst = (FEATURE_UNITS + o) % SPLIT, ps[:, b + o, 0:WV]
                        pe.matmul(dst, h_hi[:, k, toks], whi[:, s, k, :], start=(k == 0), stop=False)
                        pe.matmul(dst, h_hi[:, k, toks], wlo[:, s, k, :], start=False, stop=False)
                        last = pe.matmul(dst, h_lo[:, k, toks], whi[:, s, k, :], start=False, stop=(k == KD - 1))
                last.then_inc(chunk_done, 1)

        def copy_out(eng, odd, copy, done, split):
            for i in range(FEATURE_CHUNKS + NT):
                if i % 2 == odd:
                    eng.wait_ge(chunk_done, i + 1)
                    b = 2 * (i % 4)
                    if i < FEATURE_CHUNKS:
                        for dst, a, z, o in places[i]:
                            if a == 0 and z == T:
                                last = copy(dst.rearrange("p (a b) -> p a b", a=2), ps[:, b:b + 2, 0:HALF])
                            else:
                                last = copy(dst, ps[:, b + o, a - o * HALF:z - o * HALF])
                    else:
                        t = i - FEATURE_CHUNKS
                        row = v_sb[:, t if t < NT - 1 else 5, :]
                        copy(row[:, 0:WV], ps[:, b, 0:WV])
                        copy(row[:, WV:512], ps[:, b + 1, 0:512 - WV])
                        last = copy(g["dtr"][:, t, :], ps[:, b + 1, 512 - WV:WV])
                    last.then_inc(done, 1)
                if i % 2 == 1 and i // 2 + SPLIT < NU:
                    split(i // 2 + SPLIT)

        @block.vector
        def _(v):
            def split_lo(i):
                v.wait_ge(w_hi_ready, i + 1)
                n = width(i)
                v.tensor_tensor(wlo[:, i % SPLIT, :, 0:n], raw[:, i % RAW, :, 0:n],
                                whi[:, i % SPLIT, :, 0:n].bitcast(F32), ALU.subtract).then_inc(w_lo_ready, 1)

            split_lo(0)
            for k in range(KD):
                v.wait_ge(h_hi_ready, k + 1)
                v.tensor_tensor(h_lo[:, k], h[:, k], h_hi[:, k].bitcast(F32), ALU.subtract).then_inc(h_lo_ready, 1)
            split_lo(1)
            copy_out(v, 0, v.tensor_copy, copied_v, split_lo)

        @block.scalar
        def _(act):
            def split_hi(i):
                act.wait_ge(raw_loaded[i % RAW], layer * (16 * NU // RAW) + 16 * (i // RAW + 1))
                if i >= SPLIT:
                    act.wait_ge(chunk_done, 2 * (i - SPLIT + 1))
                n = width(i)
                act.activation(whi[:, i % SPLIT, :, 0:n], raw[:, i % RAW, :, 0:n], ACT.Copy).then_inc(w_hi_ready, 1)

            split_hi(0)
            for k in range(KD):
                act.activation(h_hi[:, k], h[:, k], ACT.Copy).then_inc(h_hi_ready, 1)
            split_hi(1)
            copy_out(act, 1, lambda o, i: act.activation(o, i, ACT.Copy), copied_a, split_hi)

        @block.gpsimd
        def _(pool):
            pool.memset(sx[:, :, 0:1], 0.0)
            pool.memset(sx[:, :, SX_S + SAMPLE:SX_P], 0.0)
            pool.memset(sx[:, :, SXW - 1:SXW], 0.0).then_inc(pads, 1)


def latent_heads(nc, io, g, layer):
    ps, cst, vec, kt, qt, cq = g["ps"], g["cst"], g["vec"], g["kt"], g["qt"], g["cq"]
    qn, qr, kn, mv = g["qn"], g["qr"], g["kn"], g["mv"]
    SPLIT = ((0, SAMPLE, 0), (SAMPLE, T, OWN_P))

    def pair(b, n=T):
        return ps[:, b:b + 2].rearrange("p a b -> p (a b)")[:, 0:n]

    with stage(nc) as (block, sem, sb):
        wuq = sb("wuq", [P, 3, 384])
        wukv = sb("wukv", [P, 2, 512])
        sq = sb("lat_sq", [P, 5, T])
        rstd = sb("lat_rstd", [P, 2, T])
        xc = sb("rot_cos", [P, 2, SAMPLE])
        xs = sb("rot_sin", [P, 2, SAMPLE])
        up = Load(sem("up_weights_loaded"))
        sq_ready, sums_done, ms_ready, root_ready, out_done = (
            sem(n) for n in ("lat_sq_ready", "lat_sums_done", "lat_ms_ready", "lat_root_ready", "prompt_out_done"))
        normed = Count(sem("lat_normed"))
        bias_loaded, bias_ready = sem("bias_loaded"), sem("bias_ready")
        up_done, up_copied, turned, rotated = (
            sem(n) for n in ("up_done", "up_copied", "turned", "rotated"))
        units = []
        for c in range(3):
            dst = qn[:, c, :] if c < 2 else qr[:]
            units.append(([(dst, 0, T)], 3,
                          lambda k, c=c: wuq[:, k, c * P:(c + 1) * P], lambda k, a, z: cq[:, k, a:z], T))
        for c in range(2):
            units.append(([(kn[:, c, :], 0, KEYS)], 2,
                          lambda k, c=c: wukv[:, k, c * P:(c + 1) * P], lambda k, a, z: kt[:, K_CKV + k, a:z], KEYS))
        for t in range(6):
            units.append(([(mv[:, t, :], 0, 256)], 2,
                          lambda k, t=t: kt[:, K_CKV + k, t * P:(t + 1) * P], lambda k, a, z: wukv[:, k, 256 + a:256 + z], 256))
        NU = len(units)
        rots = [kt[:, K_KR, 0:SAMPLE], qt[:, 2, 0:SAMPLE], qt[:, 3, 0:SAMPLE],
                kt[:, K_DF, 0:SAMPLE], kt[:, K_DF + 1, 0:SAMPLE], qr[:, 0:SAMPLE]]

        @block.sync
        def _(sp):
            sp.dma_start(g["bias"][:], layer_row(io["bias"], layer)).then_inc(bias_loaded, 16)
            up.start(sp, wuq[:], layer_row(io["w_uq"], layer).rearrange("(k p) n -> p k n", p=P))
            up.start(sp, wukv[:], layer_row(io["w_ukv"], layer).rearrange("(k p) n -> p k n", p=P))
            sp.wait_ge(normed.sem, 1 + 3 + 1 + 4)
            sp.dma_start(layer_row(io["new_k"], layer), kt[:, :, OWN_P:KEYS]).then_inc(out_done, 16)
            sp.dma_start(layer_row(io["new_v"], layer), g["v"][:, 5, :]).then_inc(out_done, 16)
            sp.wait_ge(out_done, 32)

        @block.gpsimd
        def _(pool):
            pool.wait_ge(bias_loaded, 16)
            flat = g["bias"][:].rearrange("p a b c -> p (a b) c")
            pool.tensor_tensor(flat, flat, cst[:, C_WIN:C_WIN + GRID_W].unsqueeze(1).broadcast_to([P, HEADS * 16, GRID_W]),
                               ALU.add).then_inc(bias_ready, 1)

        @block.scalar
        def _(act):
            for c in range(3):
                act.activation(sq[:, c, :], cq[:, c, :], ACT.Square)
            for c in range(2):
                for a, z, ka in SPLIT:
                    last = act.activation(sq[:, 3 + c, a:z], kt[:, K_CKV + c, ka:ka + z - a], ACT.Square)
            last.then_inc(sq_ready, 1)
            act.wait_ge(ms_ready, 2)
            act.activation(rstd[:], rstd[:], ACT.Sqrt).then_inc(root_ready, 1)
            for i in range(NU):
                act.wait_ge(up_done, i + 1)
                for dst, a, z in units[i][0]:
                    act.activation(dst, pair(2 * (i % 3), z), ACT.Copy).then_inc(up_copied, 1)

        @block.tensor
        def _(pe):
            def turn_rotary(r):
                if r >= 2:
                    pe.wait_ge(rotated, 3 * (r - 2) + 2)
                pe.matmul(ps[:, 6 + r % 2, :], cst[:, C_ROT:C_ROT + P], rots[r], start=True, stop=True).then_inc(turned, 1)

            turn_rotary(0)
            turn_rotary(1)
            pe.wait_ge(sq_ready, 1)
            for b, chunks in ((0, (0, 1, 2)), (2, (3, 4))):
                for a, z, bank in ((0, SAMPLE, b), (SAMPLE, T, b + 1)):
                    for c in chunks:
                        last = pe.matmul(ps[:, bank, 0:z - a], cst[:, C_ONE:C_ONE + P], sq[:, c, a:z],
                                         start=(c == chunks[0]), stop=(c == chunks[-1]))
            last.then_inc(sums_done, 1)
            for r in range(2, len(rots) - 1):
                turn_rotary(r)
            pe.wait_ge(up.sem, 32)
            pe.wait_ge(normed.sem, 1 + 3)
            for i, (dsts, nk, lhs, rhs, n) in enumerate(units):
                b = 2 * (i % 3)
                if i == 3:
                    pe.wait_ge(normed.sem, 1 + 3 + 1 + 4)
                if i >= 3:
                    pe.wait_ge(up_copied, i - 2)
                for a in range(0, n, 512):
                    z = min(n, a + 512)
                    for k in range(nk):
                        last = pe.matmul(ps[:, b + a // 512, 0:z - a], lhs(k), rhs(k, a, z), start=(k == 0), stop=(k == nk - 1))
                last.then_inc(up_done, 1)
                if i == 4:
                    pe.wait_ge(up_copied, 3)
                    turn_rotary(len(rots) - 1)

        @block.vector
        def _(v):
            def rotate(r):
                buf = rots[r]
                v.wait_ge(turned, r + 1)
                if r >= 2:
                    v.wait_ge(rotated, 3 * (r - 2) + 3)
                v.tensor_tensor(xc[:, r % 2], buf, cst[:, C_COS:C_COS + SAMPLE], ALU.mult).then_inc(rotated, 1)
                v.tensor_tensor(xs[:, r % 2], ps[:, 6 + r % 2, :], cst[:, C_SIN:C_SIN + SAMPLE], ALU.mult).then_inc(rotated, 1)
                v.wait_ge(rotated, 3 * r + 2)
                v.tensor_tensor(buf, xc[:, r % 2], xs[:, r % 2], ALU.add).then_inc(rotated, 1)

            rotate(0)
            rotate(1)
            v.wait_ge(sums_done, 1)
            v.tensor_scalar(rstd[:, 0, :], pair(0), 1.0 / QR, EPS, ALU.mult, ALU.add).then_inc(ms_ready, 1)
            v.tensor_scalar(rstd[:, 1, :], pair(2), 1.0 / KVR, EPS, ALU.mult, ALU.add).then_inc(ms_ready, 1)
            rotate(2)
            v.wait_ge(root_ready, 1)
            normed.link(v, v.reciprocal(rstd[:, 0], rstd[:, 0]))
            for c in range(3):
                normed.mark(v.scalar_tensor_tensor(out=cq[:, c, :], in0=cq[:, c, :], scalar=vec[:, V_QG + c:V_QG + c + 1],
                                                   in1=rstd[:, 0, :], op0=ALU.mult, op1=ALU.mult))
            normed.link(v, v.reciprocal(rstd[:, 1], rstd[:, 1]))
            for c in range(2):
                for a, z, ka in SPLIT:
                    dst = kt[:, K_CKV + c, ka:ka + z - a]
                    normed.mark(v.scalar_tensor_tensor(out=dst, in0=dst, scalar=vec[:, V_KVG + c:V_KVG + c + 1],
                                                       in1=rstd[:, 1, a:z], op0=ALU.mult, op1=ALU.mult))
            for r in range(3, len(rots)):
                rotate(r)


def attention(nc, io, g, layer):
    ps, cst, vec, kt, qt, br = g["ps"], g["cst"], g["vec"], g["kt"], g["qt"], g["br"]
    qn, qr, kn, mv, vv, bias = g["qn"], g["qr"], g["kn"], g["mv"], g["v"], g["bias"]
    NA, MLA, DF = range(3)
    units = []
    for branch in (NA, MLA, DF):
        for hd in range(HEADS):
            lo, c = 64 * (hd % 2), hd // 2
            for t in range(NT):
                for comp in range(2 if branch == DF else 1):
                    if branch == NA:
                        parts = [(qt[lo:lo + 64, c, :], kt[lo:lo + 64, K_NA + c, :])]
                    elif branch == MLA:
                        parts = [(qn[lo:lo + 64, c, :], kn[lo:lo + 64, c, :]),
                                 (qr[32 * hd:32 * hd + 32, :], kt[32 * hd:32 * hd + 32, K_KR, :])]
                    else:
                        d0 = lo + 32 * comp
                        parts = [(qt[d0:d0 + 32, 2 + c, :], kt[d0:d0 + 32, K_DF + c, :])]
                    vals = mv[:, :, 64 * hd:64 * hd + 64] if branch == MLA else \
                        vv[:, :, (256 if branch == DF else 0) + 64 * hd:(256 if branch == DF else 0) + 64 * hd + 64]
                    units.append(dict(branch=branch, hd=hd, t=t, comp=comp, parts=parts, vals=vals,
                                      scale=(64 ** -0.5, 96 ** -0.5, 32 ** -0.5)[branch],
                                      biased=branch == NA and t < NT - 1,
                                      last=branch != DF or comp == 1,
                                      keys=(0, OWN_P) if t < NT - 1 else (OWN_P, KEYS)))
    NU = len(units)
    WARM = 448
    outs, n = [], 0
    for u in units:
        outs.append(n)
        n += u["last"]
    NO = n

    reads, n = [], 0
    for u in units:
        n += u["biased"]
        reads.append(n)

    def scores(u, n):
        return ps[:, 2 * (u % 2):2 * (u % 2) + 2].rearrange("p a b -> p (a b)")[:, 0:n]

    def out_place(u):
        x = units[u]
        lo = 64 * (x["hd"] % 2)
        return (br[lo:lo + 64, x["branch"], x["hd"] // 2, x["t"] * P:(x["t"] + 1) * P],
                ps[lo:lo + 64, 6 + outs[u] % 2, 0:P])

    with stage(nc) as (block, sem, sb):
        biased = sb("biased_scores", [P, 2, OWN_P])
        prob = sb("prob", [P, 3, OWN_P])
        pt = sb("prob_turned", [P, 2, OWN_P])
        mx = sb("row_max", [P, 2])
        nm = sb("neg_max", [P, 2])
        rowsum = sb("row_sum", [P, 3])
        rec = sb("row_rec", [P, 3])
        lp = sb("lam_prod", [P, 2, 32])
        ls = sb("lam_sum", [P, 2])
        le = sb("lam_exp", [P, 2])
        ld = sb("lam_diff", [P, 1])
        neglam = sb("neg_lam", [P, 1])
        (scores_read, lam_sum_ready, lam_exp_ready, scores_done, neg_max_ready, exp_done, prob_ready,
         turned, turned_copied, out_done, out_copied) = (
            sem(n) for n in ("scores_read", "lam_sum_ready", "lam_exp_ready", "scores_done",
                             "neg_max_ready", "exp_done", "prob_ready", "prob_turned_done", "turned_copied", "out_done",
                             "out_copied"))
        chain = Count(sem("attention_vector_chain"))

        @block.tensor
        def _(pe):
            def score(u):
                x = units[u]
                if u >= 2 and units[u - 2]["biased"]:
                    pe.wait_ge(scores_read, reads[u - 2])
                elif u >= 2:
                    pe.wait_ge(exp_done, u - 1)
                k0, k1 = x["keys"]
                for a in range(k0, k1, 512):
                    z = min(a + 512, k1)
                    dst = scores(u, z - k0)[:, a - k0:z - k0]
                    for i, (q, k) in enumerate(x["parts"]):
                        last = pe.matmul(dst, q[:, x["t"] * P:(x["t"] + 1) * P], k[:, a:z],
                                         start=(i == 0), stop=(i == len(x["parts"]) - 1))
                last.then_inc(scores_done, 1)

            def turn(u):
                x = units[u]
                pe.wait_ge(prob_ready, u + 1)
                if outs[u] >= 1:
                    pe.wait_ge(turned_copied, outs[u])
                for b in range((x["keys"][1] - x["keys"][0]) // P):
                    last = pe.transpose(ps[:, 4:6].rearrange("p a b -> p (a b)")[:, b * P:(b + 1) * P],
                                        prob[:, u % 3, b * P:(b + 1) * P], cst[:, C_ID:C_ID + P])
                last.then_inc(turned, 1)

            def values(u):
                x = units[u]
                pe.wait_ge(turned_copied, outs[u] + 1)
                if outs[u] >= 2:
                    pe.wait_ge(out_copied, outs[u] - 1)
                nb = (x["keys"][1] - x["keys"][0]) // P
                for b in range(nb):
                    last = pe.matmul(out_place(u)[1], x["vals"][:, b if nb > 1 else 5, :], pt[:, outs[u] % 2, b * P:(b + 1) * P],
                                     start=(b == 0), stop=(b == nb - 1))
                last.then_inc(out_done, 1)

            def keep_warm(i):
                turned_before = sum(x["last"] for x in units[0:max(i - 2, 0)])
                if turned_before:
                    pe.wait_ge(turned_copied, turned_before)
                pe.matmul(ps[:, 4, 0:WARM], cst[:, C_ID:C_ID + P], cst[:, 0:WARM], start=True, stop=True)

            for i in range(NU + 3):
                if i < NU:
                    score(i)
                if i < NU:
                    keep_warm(i)
                if 2 <= i < NU + 2 and units[i - 2]["last"]:
                    turn(i - 2)
                if i >= 3 and units[i - 3]["last"]:
                    values(i - 3)

        @block.scalar
        def _(act):
            act.wait_ge(lam_sum_ready, 1)
            act.activation(le[:], ls[:], ACT.Exp).then_inc(lam_exp_ready, 1)
            for i in range(NU + 2):
                if i < NU:
                    x = units[i]
                    n = x["keys"][1] - x["keys"][0]
                    act.wait_ge(neg_max_ready, i + 1)
                    if i >= 3 and units[i - 3]["last"]:
                        act.wait_ge(turned, outs[i - 3] + 1)
                    elif i >= 3:
                        act.wait_ge(prob_ready, i - 1)
                    src = biased[:, i % 2, 0:n] if x["biased"] else scores(i, n)
                    act.activation(prob[:, i % 3, 0:n], src, ACT.Exp, bias=nm[:, i % 2:i % 2 + 1],
                                   scale=1.0 if x["biased"] else x["scale"],
                                   accum_out=rowsum[:, i % 3:i % 3 + 1]).then_inc(exp_done, 1)
                if i >= 2 and units[i - 2]["last"]:
                    u = i - 2
                    n = units[u]["keys"][1] - units[u]["keys"][0]
                    act.wait_ge(turned, outs[u] + 1)
                    if outs[u] >= 2:
                        act.wait_ge(out_done, outs[u] - 1)
                    act.activation(pt[:, outs[u] % 2, 0:n], ps[:, 4:6].rearrange("p a b -> p (a b)")[:, 0:n],
                                   ACT.Copy).then_inc(turned_copied, 1)

        @block.vector
        def _(v):
            lam = vec[:, V_LAM:V_LAM + 128].rearrange("p (a b d) -> p a b d", a=2, b=2)
            chain.link(v, v.tensor_tensor(lp[:], lam[:, :, 0, :], lam[:, :, 1, :], ALU.mult))
            v.tensor_reduce(ls[:], lp[:], AXX, ALU.add).then_inc(lam_sum_ready, 1)
            v.wait_ge(lam_exp_ready, 1)
            chain.link(v, v.tensor_tensor(ld[:], le[:, 1:2], le[:, 0:1], ALU.subtract))
            chain.link(v, v.tensor_tensor(neglam[:], ld[:], vec[:, V_LI:V_LI + 1], ALU.subtract))

            def maximum(u):
                x = units[u]
                n = x["keys"][1] - x["keys"][0]
                v.wait_ge(scores_done, u + 1)
                if u >= 2:
                    v.wait_ge(exp_done, u - 1)
                src = scores(u, n)
                if x["biased"]:
                    off = 7 - 2 * x["t"]
                    chain.mark(v.scalar_tensor_tensor(
                        out=biased[:, u % 2, 0:SAMPLE], in0=src[:, 0:SAMPLE], scalar=x["scale"],
                        in1=bias[:, x["hd"], off:off + ROWS, :].rearrange("p a b -> p (a b)"), op0=ALU.mult, op1=ALU.add))
                    v.tensor_scalar(biased[:, u % 2, SAMPLE:n], src[:, SAMPLE:n], x["scale"], None, ALU.mult).then_inc(scores_read, 1)
                    v.wait_ge(scores_read, reads[u])
                    src = biased[:, u % 2, 0:n]
                chain.link(v, v.tensor_reduce(mx[:, u % 2:u % 2 + 1], src, AXX, ALU.max))
                v.tensor_scalar(nm[:, u % 2:u % 2 + 1], mx[:, u % 2:u % 2 + 1], -1.0 if x["biased"] else -x["scale"],
                                None, ALU.mult).then_inc(neg_max_ready, 1)

            def normalise(u):
                x = units[u]
                n = x["keys"][1] - x["keys"][0]
                v.wait_ge(exp_done, u + 1)
                r = rec[:, u % 3:u % 3 + 1]
                chain.link(v, v.reciprocal(r, rowsum[:, u % 3:u % 3 + 1]))
                if x["comp"] == 1:
                    chain.link(v, v.tensor_tensor(r, r, neglam[:, 0:1], ALU.mult))
                    v.wait_ge(prob_ready, u)
                    v.scalar_tensor_tensor(out=prob[:, u % 3, 0:n], in0=prob[:, u % 3, 0:n], scalar=r, in1=prob[:, (u - 1) % 3, 0:n],
                                           op0=ALU.mult, op1=ALU.add).then_inc(prob_ready, 1)
                else:
                    v.tensor_scalar(prob[:, u % 3, 0:n], prob[:, u % 3, 0:n], r, None, ALU.mult).then_inc(prob_ready, 1)

            def copy_out(u):
                if units[u]["last"]:
                    v.wait_ge(out_done, outs[u] + 1)
                    dst, src = out_place(u)
                    v.tensor_copy(dst, src).then_inc(out_copied, 1)

            for i in range(NU + 4):
                if i < NU:
                    maximum(i)
                if 1 <= i <= NU:
                    normalise(i - 1)
                if i >= 4:
                    copy_out(i - 4)


def ssm(nc, io, g, layer):
    ps, cst, vec, sx, sz, br = g["ps"], g["cst"], g["vec"], g["sx"], g["sz"], g["br"]
    CW = T + 2
    steps = [step for t in range(NT - 1) for step in ((0, t), (1, NT - 2 - t))] + [(0, NT - 1), (1, NT - 1)]
    NS = len(steps)
    with stage(nc) as (block, sem, sb):
        xc = sb("conv", [P, 4, CW])
        sub = sb("sub_gain", [P, 1])
        dsq = sb("df_sq", [P, 2, T])
        drstd = sb("df_rstd", [P, 2, T])
        th = sb("conv_tanh", [P, 4, CW])
        thz = sb("z_tanh", [P, 2, T])
        xtok = sb("conv_tok", [P, NT, 384])
        dtu, dtn, dte, dtl, dt, a8, ac, nac = (sb(n, [P, NT, 8]) for n in (
            "dt_u", "dt_n", "dt_e", "dt_l", "dt", "dt_a", "a_cum", "neg_a_cum"))
        ea = sb("exp_a", [P, 8])
        gm = sb("bc_masked", [P, NT, 2, 2, P])
        state = sb("state", [P, 2, 2, 2, 64])
        arep, seg, dec, mm = (sb(n, [P, 2, 4, P]) for n in ("a_rep", "seg", "dec", "mixing"))
        e0 = sb("exp_cum", [P, 3, 4, P])
        cts = sb("c_scaled", [P, 2, 2, P])
        wd, we = sb("w_dif", [P, 2, 4]), sb("w_exp", [P, 2, 4])
        xw = sb("x_weighted", [P, 2, 4, 64])
        y = sb("ssm_y", [P, 2, T])
        ysq, yms, yroot = th[:, 0:2, 0:T], th[:, 2, 0:T], th[:, 3, 0:T]
        (state_loaded, conv_ready, conv_tanh, z_tanh, dt_arg, dt_exp, dt_one, dt_ln, conv_silu, tok_turned, tok_copied,
         a_ready, cum_done, bc_done, bc_read, rep_ready, along_done, seg_ready, dec_ready, wd_ready, w_ready, mix_ready,
         y_done, y_added, ysq_ready, ysum_done, yms_ready, yroot_ready, gated_ready, state_out) = (
            sem(n) for n in ("state_loaded", "conv_ready", "conv_tanh_done", "z_tanh_done", "dt_arg", "dt_exp", "dt_one", "dt_ln",
                             "conv_silu", "tok_turned", "tok_copied", "a_ready", "cum_done", "bc_done", "bc_read",
                             "rep_ready", "along_done", "seg_ready", "dec_ready", "wd_ready", "w_ready", "mix_ready",
                             "y_done", "y_added", "ysq_ready", "ysum_done", "yms_ready", "yroot_ready", "gated_ready", "state_out"))
        cts_ready = sem("c_scaled_ready")
        df_sq_ready, df_sums_done, df_ms_ready, df_root_ready = (
            sem(n) for n in ("df_sq_ready", "df_sums_done", "df_ms_ready", "df_root_ready"))
        df = br[:, 2]
        chain = Count(sem("ssm_vector_chain"))

        def last_col(dr):
            return P - 1 if dr == 0 else 0

        def along(s):
            return ps[:, 3 + s % 2, :].rearrange("p (a b) -> p a b", a=4)

        def bc_banks(t):
            return (3, 4) if t % 2 == 0 else (6, 7)

        def y_banks(s):
            return ((5, 7), 6) if s % 2 == 0 else ((0, 2), 1)

        @block.sync
        def _(sp):
            sp.dma_start(state[:, 0], layer_row(io["state"], layer)).then_inc(state_loaded, 16)
            for i in range(MERGE_RAW[1]):
                load_merge(sp, io, g, layer, i)
            sp.wait_ge(y_added, 2 * NS)
            sp.dma_start(layer_row(io["new_state"], layer), state[:, 1]).then_inc(state_out, 16)
            sp.wait_ge(state_out, 16)

        @block.scalar
        def _(act):
            act.activation(ea[:], vec[:, V_ALOG:V_ALOG + 8], ACT.Exp)
            act.wait_ge(dt_arg, 1)
            act.activation(dte[:], dtn[:], ACT.Exp).then_inc(dt_exp, 1)
            act.activation(thz[:], sz[:], ACT.Tanh, scale=0.5).then_inc(z_tanh, 1)
            act.activation(dsq[:], df, ACT.Square).then_inc(df_sq_ready, 1)
            act.wait_ge(df_ms_ready, 1)
            act.activation(drstd[:], drstd[:], ACT.Sqrt).then_inc(df_root_ready, 1)
            act.wait_ge(conv_ready, 1)
            act.activation(th[:], xc[:], ACT.Tanh, scale=0.5).then_inc(conv_tanh, 1)
            act.wait_ge(dt_one, 1)
            act.activation(dtl[:], dte[:], ACT.Ln).then_inc(dt_ln, 1)
            for t in range(NT):
                act.wait_ge(tok_turned, t + 1)
                act.activation(xtok[:, t, :], ps[:, t % 2, 0:384], ACT.Copy).then_inc(tok_copied, 1)

            def repeat(s):
                dr, t = steps[s]
                if s >= 2:
                    act.wait_ge(along_done, s - 1)
                act.activation(arep[:, s % 2], a8[:, t, 4 * dr:4 * dr + 4].unsqueeze(2).broadcast_to([P, 4, P]),
                               ACT.Copy).then_inc(rep_ready, 1)

            act.wait_ge(a_ready, 1)
            repeat(0)
            for s in range(NS):
                if s + 1 < NS:
                    repeat(s + 1)
                act.wait_ge(along_done, s + 1)
                if s >= 3:
                    act.wait_ge(y_added, 2 * (s - 2))
                act.activation(e0[:, s % 3], along(s), ACT.Exp).then_inc(dec_ready, 1)
                act.wait_ge(wd_ready, s + 1)
                if s >= 2:
                    act.wait_ge(mix_ready, s - 1)
                act.activation(we[:, s % 2], wd[:, s % 2], ACT.Exp).then_inc(w_ready, 1)
                act.wait_ge(seg_ready, s + 1)
                act.activation(dec[:, s % 2], seg[:, s % 2], ACT.Exp).then_inc(dec_ready, 1)
            act.wait_ge(gated_ready, 1)
            act.activation(ysq, y[:], ACT.Square).then_inc(ysq_ready, 1)
            act.wait_ge(yms_ready, 1)
            act.activation(yroot, yms, ACT.Sqrt).then_inc(yroot_ready, 1)

        @block.gpsimd
        def _(pool):
            for s, (dr, t) in enumerate(steps):
                pool.wait_ge(dec_ready, 2 * s + 1)
                if s >= 2:
                    pool.wait_ge(y_done, s - 1)
                for gr in range(2):
                    lo = 64 * gr
                    pool.tensor_tensor(cts[lo:lo + 64, s % 2], e0[lo:lo + 64, s % 3, 2 * gr:2 * gr + 2, :],
                                       xc[lo:lo + 64, 3, pcol(t):pcol(t) + P].unsqueeze(1).broadcast_to([64, 2, P]),
                                       ALU.mult).then_inc(cts_ready, 1)

        @block.tensor
        def _(pe):
            pe.wait_ge(df_sq_ready, 1)
            for c in range(2):
                pe.matmul(ps[:, 4 + 2 * c, :], cst[:, C_BLK:C_BLK + P], dsq[:, c, 0:SAMPLE], start=True, stop=True)
                last = pe.matmul(ps[:, 5, c * PROMPT:(c + 1) * PROMPT], cst[:, C_BLK:C_BLK + P], dsq[:, c, SAMPLE:T], start=True, stop=True)
            last.then_inc(df_sums_done, 1)
            pe.wait_ge(conv_silu, 1)
            for t in range(NT):
                if t >= 2:
                    pe.wait_ge(tok_copied, t - 1)
                for c in range(3):
                    last = pe.transpose(ps[:, t % 2, c * P:(c + 1) * P], xc[:, c, pcol(t):pcol(t) + P], cst[:, C_ID:C_ID + P])
                last.then_inc(tok_turned, 1)
            pe.wait_ge(a_ready, 1)
            for dr, tri in ((0, C_LE), (1, C_GE)):
                last = pe.matmul(ps[:, 2, 20 * dr:20 * dr + 20].rearrange("p (a b) -> p a b", a=NT), cst[:, tri:tri + P],
                                 a8[:, :, 4 * dr:4 * dr + 4], start=True, stop=True)
            last.then_inc(cum_done, 1)
            for t in range(NT):
                if t >= 2:
                    pe.wait_ge(bc_read, t - 1)
                for gr in range(2):
                    lo = 64 * gr
                    last = pe.matmul(ps[:, bc_banks(t)[gr], 0:P], xc[lo:lo + 64, 2, pcol(t):pcol(t) + P],
                                     xc[lo:lo + 64, 3, pcol(t):pcol(t) + P], start=True, stop=True)
                last.then_inc(bc_done, 1)
            pe.wait_ge(tok_copied, NT)
            pe.wait_ge(bc_read, NT)

            def decays(s):
                tri = (C_LE, C_GE)[steps[s][0]]
                pe.wait_ge(rep_ready, s + 1)
                if s >= 2:
                    pe.wait_ge(seg_ready, s - 1)
                for hd in range(4):
                    last = pe.matmul(along(s)[:, hd, :], arep[:, s % 2, hd, :], cst[:, tri:tri + P], start=True, stop=True)
                last.then_inc(along_done, 1)

            def outputs(s):
                (dr, t), (banks, state_bank) = steps[s], y_banks(s)
                pe.wait_ge(mix_ready, s + 1)
                pe.wait_ge(cts_ready, 2 * (s + 1))
                if s >= 2:
                    pe.wait_ge(y_added, 2 * (s - 1))
                for hd in range(4):
                    lo, gl = 64 * (hd % 2), 64 * (hd // 2)
                    dst = ps[lo:lo + 64, banks[hd // 2], 0:P]
                    pe.matmul(dst, xtok[:, t, 64 * hd:64 * hd + 64], mm[:, s % 2, hd, :], start=True, stop=False)
                    pe.matmul(dst, state[gl:gl + 64, t // 4, dr, hd % 2, :], cts[gl:gl + 64, s % 2, hd % 2, :], start=False, stop=True)
                pe.matmul(ps[:, state_bank, 0:256], xtok[:, t, 256:384], xw[:, s % 2].rearrange("p a b -> p (a b)"),
                          start=True, stop=True).then_inc(y_done, 1)

            for s in range(NS + 2):
                if s < NS:
                    decays(s)
                if s >= 2:
                    outputs(s - 2)
            pe.wait_ge(ysq_ready, 1)
            for a, z, bank in ((0, SAMPLE, 0), (SAMPLE, T, 1)):
                for c in range(2):
                    last = pe.matmul(ps[:, bank, 0:z - a], cst[:, C_ONE:C_ONE + P], ysq[:, c, a:z], start=(c == 0), stop=(c == 1))
            last.then_inc(ysum_done, 1)

        @block.vector
        def _(v):
            link = lambda ins: chain.link(v, ins)
            link(v.tensor_tensor(dtu[:], g["dtr"][:], vec[:, V_DTB:V_DTB + 8].unsqueeze(1).broadcast_to([P, NT, 8]), ALU.add))
            link(v.tensor_scalar(dtn[:], dtu[:], -1.0, None, ALU.mult))
            v.tensor_tensor(dtn[:], dtu[:], dtn[:], ALU.min).then_inc(dt_arg, 1)
            for c in range(4):
                if c == 3:
                    v.wait_ge(df_sums_done, 1)
                    v.tensor_scalar(drstd[:, :, 0:SAMPLE], ps[:, 4:7:2, :], 1.0 / 64, EPS, ALU.mult, ALU.add)
                    v.tensor_scalar(drstd[:, :, SAMPLE:T], ps[:, 5, 0:2 * PROMPT].rearrange("p (a b) -> p a b", a=2), 1.0 / 64, EPS,
                                    ALU.mult, ALU.add).then_inc(df_ms_ready, 1)
                w = [vec[:, V_CW + 4 * tap + c:V_CW + 4 * tap + c + 1] for tap in range(3)]
                link(v.tensor_scalar(xc[:, c], sx[:, c, 0:CW], w[0], vec[:, V_CB + c:V_CB + c + 1], ALU.mult, ALU.add))
                link(v.scalar_tensor_tensor(out=xc[:, c], in0=sx[:, c, 1:1 + CW], scalar=w[1], in1=xc[:, c], op0=ALU.mult, op1=ALU.add))
                ins = v.scalar_tensor_tensor(out=xc[:, c], in0=sx[:, c, 2:2 + CW], scalar=w[2], in1=xc[:, c], op0=ALU.mult, op1=ALU.add)
                if c == 3:
                    ins.then_inc(conv_ready, 1)
                else:
                    chain.mark(ins)
            v.wait_ge(dt_exp, 1)
            v.tensor_scalar(dte[:], dte[:], 1.0, None, ALU.add).then_inc(dt_one, 1)
            def scale_df(c):
                link(v.reciprocal(drstd[:, c], drstd[:, c]))
                chain.mark(v.scalar_tensor_tensor(out=df[:, c], in0=df[:, c], scalar=sub[:, 0:1], in1=drstd[:, c],
                                                  op0=ALU.mult, op1=ALU.mult))

            v.wait_ge(df_root_ready, 1)
            link(v.tensor_scalar(sub[:], vec[:, V_SUB:V_SUB + 1], vec[:, V_LI + 1:V_LI + 2], None, ALU.mult))
            scale_df(0)
            v.wait_ge(conv_tanh, 1)
            link(v.tensor_scalar(th[:], th[:], 0.5, 0.5, ALU.mult, ALU.add))
            v.tensor_tensor(xc[:], xc[:], th[:], ALU.mult).then_inc(conv_silu, 1)
            v.wait_ge(dt_ln, 1)
            link(v.scalar_tensor_tensor(out=dt[:], in0=dtu[:], scalar=0.0, in1=dtl[:], op0=ALU.max, op1=ALU.add))
            v.scalar_tensor_tensor(out=a8[:], in0=dt[:], scalar=-1.0, in1=ea[:].unsqueeze(1).broadcast_to([P, NT, 8]),
                                   op0=ALU.mult, op1=ALU.mult).then_inc(a_ready, 1)
            v.wait_ge(z_tanh, 1)
            link(v.tensor_scalar(thz[:], thz[:], 0.5, 0.5, ALU.mult, ALU.add))
            link(v.tensor_tensor(sz[:], sz[:], thz[:], ALU.mult))
            v.wait_ge(conv_silu, 1)
            for c in range(2):
                for t0, t1, src in ((0, SAMPLE, 0), (SAMPLE, T, SAMPLE + 2)):
                    chain.mark(v.tensor_scalar(y[:, c, t0:t1], xc[:, c, src:src + t1 - t0],
                                               vec[:, V_SD + c:V_SD + c + 1], None, ALU.mult))
            v.wait_ge(cum_done, 1)
            cum = ps[:, 2, 0:40].rearrange("p (d a b) -> p a d b", d=2, a=NT)
            chain.mark(v.tensor_scalar(nac[:].rearrange("p a (d b) -> p a d b", d=2), cum, -1.0, None, ALU.mult))
            scale_df(1)
            for t in range(NT):
                v.wait_ge(bc_done, t + 1)
                for dr, tri in ((0, C_LE), (1, C_GE)):
                    last = v.tensor_tensor(gm[:, t, dr], ps[:, bc_banks(t)[0]:bc_banks(t)[1] + 1, 0:P],
                                           cst[:, tri:tri + P].unsqueeze(1).broadcast_to([P, 2, P]), ALU.mult)
                last.then_inc(bc_read, 1)
            link(v.memset(state[:, 1], 0.0))
            v.wait_ge(state_loaded, 16)
            v.wait_ge(tok_copied, NT)
            v.wait_ge(a_ready, 1)
            v.wait_ge(bc_read, NT)

            def decays(s):
                dr, t = steps[s]
                v.wait_ge(dec_ready, 2 * s + 1)
                v.tensor_tensor(wd[:, s % 2], along(s)[:, :, last_col(dr)], nac[:, t, 4 * dr:4 * dr + 4], ALU.add).then_inc(wd_ready, 1)
                for hd in range(4):
                    last = v.tensor_scalar(seg[:, s % 2, hd, :], along(s)[:, hd, :], nac[:, t, 4 * dr + hd:4 * dr + hd + 1], 0.0,
                                           ALU.add, ALU.min)
                last.then_inc(seg_ready, 1)

            def mixing(s):
                dr, t = steps[s]
                h = s % 2
                v.wait_ge(w_ready, s + 1)
                link(v.tensor_tensor(we[:, h], we[:, h], dt[:, t, 4 * dr:4 * dr + 4], ALU.mult))
                chain.mark(v.tensor_tensor(xw[:, h], xtok[:, t, 0:256].rearrange("p (a b) -> p a b", a=4),
                                           we[:, h].unsqueeze(2).broadcast_to([P, 4, 64]), ALU.mult))
                v.wait_ge(dec_ready, 2 * s + 2)
                for hd in range(4):
                    last = v.scalar_tensor_tensor(out=mm[:, h, hd, :], in0=dec[:, h, hd, :], scalar=dt[:, t, 4 * dr + hd:4 * dr + hd + 1],
                                                  in1=gm[:, t, dr, hd // 2, :], op0=ALU.mult, op1=ALU.mult)
                last.then_inc(mix_ready, 1)

            def update(s):
                (dr, t), (banks, state_bank) = steps[s], y_banks(s)
                lc = last_col(dr)
                v.wait_ge(y_done, s + 1)
                if s:
                    v.wait_ge(y_added, 2 * s)
                yt = y[:, :, t * P:(t + 1) * P]
                v.tensor_tensor(yt, yt, ps[:, banks[0]:banks[1] + 1:2, 0:P], ALU.add).then_inc(y_added, 1)
                for gr in range(2):
                    lo = 64 * gr
                    for m in range(2):
                        hd = 2 * gr + m
                        st = state[lo:lo + 64, t // 4, dr, m, :]
                        ins = v.scalar_tensor_tensor(out=st, in0=st, scalar=e0[lo:lo + 64, s % 3, hd, lc:lc + 1],
                                                     in1=ps[lo:lo + 64, state_bank, 64 * hd:64 * hd + 64], op0=ALU.mult, op1=ALU.add)
                        if hd == 3:
                            ins.then_inc(y_added, 1)
                        else:
                            chain.mark(ins)

            for s in range(NS + 2):
                if s < NS:
                    decays(s)
                if 1 <= s <= NS:
                    mixing(s - 1)
                if s >= 2:
                    update(s - 2)
            v.wait_ge(y_added, 2 * NS)
            v.tensor_tensor(y[:], y[:], sz[:], ALU.mult).then_inc(gated_ready, 1)
            v.wait_ge(ysum_done, 1)
            v.tensor_scalar(yms, ps[:, 0:2].rearrange("p a b -> p (a b)")[:, 0:T], 1.0 / 256, EPS, ALU.mult, ALU.add).then_inc(yms_ready, 1)
            v.wait_ge(yroot_ready, 1)
            link(v.reciprocal(yroot, yroot))
            for c in range(2):
                chain.mark(v.scalar_tensor_tensor(out=br[:, 3, c, :], in0=y[:, c, :], scalar=vec[:, V_SG + c:V_SG + c + 1],
                                                  in1=yroot, op0=ALU.mult, op1=ALU.mult))


def merge(nc, io, g, layer):
    ps, x, h, br, mod = g["ps"], g["x"], g["h"], g["br"], g["mod"]
    raw, raw_loaded = g["merge_raw"], g["merge_raw_loaded"]
    RAW, SPLIT, PER = 2, 2, 2
    NU = GATE_UNITS + OUT_UNITS
    chunks = [(n, d) for n in range(4) for d in range(KD)]
    NC = len(chunks)

    HALF = T // 2
    HALVES = ((0, HALF, 0), (HALF, T, 1))
    PIECES = ((0, 0, HALF, 0), (0, HALF, SAMPLE, 1), (1, SAMPLE, T, 1))

    def pair(b):
        return ps[:, b:b + 2, 0:HALF]

    def halves(a):
        return a.rearrange("p (a b) -> p a b", a=2)

    with stage(nc) as (block, sem, sb):
        whi = sb("merge_w_hi", [P, SPLIT, KD + 2, P], F32R)
        wlo = sb("merge_w_lo", [P, SPLIT, KD + 2, P], F32R)
        h_hi = sb("merge_h_hi", [P, KD, T], F32R)
        h_lo = sb("merge_h_lo", [P, KD, T], F32R)
        bm_hi = sb("branch_mix_hi", [P, KD + 2, T], F32R)
        bm_lo = sb("branch_mix_lo", [P, KD + 2, T], F32R)
        th = sb("gate_tanh", [P, 3, T])
        mix = h
        half_gate = sb("half_gate", [P, KD, 2])
        flat_br = br[:].rearrange("p n k t -> p (n k) t")
        (h_hi_ready, h_lo_ready, br_hi_ready, br_lo_ready, w_hi_ready, w_lo_ready, added, mix_hi_ready, mix_lo_ready,
         gate_done, proj_done, tanh_done, gated, out_done, x_added) = (
            sem("merge_" + n) for n in (
                "h_hi_ready", "h_lo_ready", "br_hi_ready", "br_lo_ready", "w_hi_ready", "w_lo_ready", "added", "mix_hi_ready",
                "mix_lo_ready", "gate_done", "proj_done", "tanh_done", "gated", "out_done", "x_added"))
        chain = Count(sem("merge_vector_chain"))
        total = sum(merge_loads(i) for i in range(0, NU, RAW))
        loaded = [sum(merge_loads(b) for b in range(i % RAW, i + 1, RAW)) for i in range(NU)]
        assert total == loaded[-1] == loaded[-2]

        def chunk_weights(split, c):
            rows = KD + 2 if c < NC else KD
            return split[:, c % SPLIT, 0:rows], raw[:, c // PER % RAW, 0:rows, (c % PER) * P:(c % PER + 1) * P]

        def mix_slot(d):
            return d if d < 6 else d + 2

        @block.sync
        def _(sp):
            for i in range(RAW, NU):
                sp.wait_ge(w_lo_ready, PER * (i - RAW + 1))
                load_merge(sp, io, g, layer, i)

        @block.tensor
        def _(pe):
            def product(dst, hi, lo, whi_, wlo_, first, last):
                pe.matmul(dst, whi_, hi, start=first, stop=False)
                pe.matmul(dst, whi_, lo, start=False, stop=False)
                return pe.matmul(dst, wlo_, hi, start=False, stop=last)

            for u, (n, d) in enumerate(chunks):
                s = u % SPLIT
                pe.wait_ge(w_lo_ready, u + 1)
                if u >= 2:
                    pe.wait_ge(tanh_done, u - 1)
                for k in range(KD):
                    if u == 0:
                        pe.wait_ge(h_lo_ready, k + 1)
                    for a, z, o in HALVES:
                        last = product(ps[:, 2 * (u % 2) + o, 0:z - a], h_hi[:, k, a:z], h_lo[:, k, a:z],
                                       whi[:, s, k, :], wlo[:, s, k, :], k == 0, k == KD - 1)
                last.then_inc(gate_done, 1)
                if d == 0:
                    pe.wait_ge(br_lo_ready, 2 * n + 2)
                if u >= 2:
                    pe.wait_ge(gated, u - 1)
                for k in range(2):
                    for a, z, o in HALVES:
                        last = product(ps[:, 4 + 2 * (u % 2) + o, 0:z - a], bm_hi[:, 2 * n + k, a:z], bm_lo[:, 2 * n + k, a:z],
                                       whi[:, s, KD + k, :], wlo[:, s, KD + k, :], k == 0, k == 1)
                last.then_inc(proj_done, 1)
            for d in range(KD):
                s = (NC + d) % SPLIT
                pe.wait_ge(w_lo_ready, NC + d + 1)
                if d >= 4:
                    pe.wait_ge(x_added, d - 3)
                elif d >= 2:
                    pe.wait_ge(gated, NC - 3 + d)
                else:
                    pe.wait_ge(tanh_done, NC - 1 + d)
                for k in range(KD):
                    if d == 0:
                        pe.wait_ge(mix_lo_ready, k + 1)
                    for a, z, o in HALVES:
                        last = product(ps[:, 2 * (d % 4) + o, 0:z - a], bm_hi[:, mix_slot(k), a:z], bm_lo[:, mix_slot(k), a:z],
                                       whi[:, s, k, :], wlo[:, s, k, :], k == 0, k == KD - 1)
                last.then_inc(out_done, 1)

        @block.scalar
        def _(act):
            def split_hi(c):
                act.wait_ge(raw_loaded[c // PER % RAW], layer * total + loaded[c // PER])
                last = c - SPLIT
                if last >= NC:
                    act.wait_ge(out_done, last - NC + 1)
                elif last >= 0:
                    act.wait_ge(proj_done, last + 1)
                hi, src = chunk_weights(whi, c)
                act.activation(hi, src, ACT.Copy).then_inc(w_hi_ready, 1)

            def mix_split_hi(d):
                act.wait_ge(added, 2 * KD + d + 1)
                if d == 0:
                    act.wait_ge(proj_done, 3 * KD)
                act.activation(bm_hi[:, mix_slot(d)], mix[:, d], ACT.Copy).then_inc(mix_hi_ready, 1)

            split_hi(0)
            for k in range(KD):
                act.activation(h_hi[:, k], h[:, k], ACT.Copy).then_inc(h_hi_ready, 1)
            for k in range(KD):
                act.activation(bm_hi[:, k], flat_br[:, k], ACT.Copy).then_inc(br_hi_ready, 1)
            split_hi(1)
            for u, (n, d) in enumerate(chunks):
                act.wait_ge(gate_done, u + 1)
                if u >= 3 + KD:
                    act.wait_ge(added, u - 2 - KD)
                elif u >= 3:
                    act.wait_ge(gated, u - 2)
                act.activation(halves(th[:, u % 3]), pair(2 * (u % 2)), ACT.Tanh, scale=0.5).then_inc(tanh_done, 1)
                if n == 3 and d:
                    mix_split_hi(d - 1)
                split_hi(u + SPLIT)
            mix_split_hi(KD - 1)
            for c in range(NC + SPLIT, NC + KD):
                split_hi(c)

        @block.vector
        def _(v):
            def split_lo(c):
                v.wait_ge(w_hi_ready, c + 1)
                (lo, src), (hi, _) = chunk_weights(wlo, c), chunk_weights(whi, c)
                v.tensor_tensor(lo, src, hi.bitcast(F32), ALU.subtract).then_inc(w_lo_ready, 1)

            def mix_split_lo(d):
                v.wait_ge(mix_hi_ready, d + 1)
                v.tensor_tensor(bm_lo[:, mix_slot(d)], mix[:, d], bm_hi[:, mix_slot(d)].bitcast(F32), ALU.subtract).then_inc(mix_lo_ready, 1)

            chain.mark(v.tensor_scalar(half_gate[:], mod[:, 16:16 + KD, :], 0.5, None, ALU.mult))
            split_lo(0)
            for k in range(KD):
                v.wait_ge(h_hi_ready, k + 1)
                v.tensor_tensor(h_lo[:, k], h[:, k], h_hi[:, k].bitcast(F32), ALU.subtract).then_inc(h_lo_ready, 1)
            for k in range(KD):
                v.wait_ge(br_hi_ready, k + 1)
                v.tensor_tensor(bm_lo[:, k], flat_br[:, k], bm_hi[:, k].bitcast(F32), ALU.subtract).then_inc(br_lo_ready, 1)
            split_lo(1)
            for u, (n, d) in enumerate(chunks):
                v.wait_ge(tanh_done, u + 1)
                v.wait_ge(proj_done, u + 1)
                dst = mix[:, d] if n == 0 else th[:, u % 3]
                v.scalar_tensor_tensor(out=halves(dst), in0=halves(th[:, u % 3]), scalar=1.0, in1=pair(4 + 2 * (u % 2)),
                                       op0=ALU.add, op1=ALU.mult).then_inc(gated, 1)
                if n:
                    v.wait_ge(gated, u + 1)
                    v.tensor_tensor(mix[:, d], mix[:, d], th[:, u % 3], ALU.add).then_inc(added, 1)
                if n == 3 and d:
                    mix_split_lo(d - 1)
                split_lo(u + SPLIT)
            mix_split_lo(KD - 1)
            for d in range(KD):
                v.wait_ge(out_done, d + 1)
                for grp, a, z, o in PIECES:
                    last = v.scalar_tensor_tensor(out=x[:, d, a:z], in0=ps[:, 2 * (d % 4) + o, a - o * HALF:z - o * HALF],
                                                  scalar=half_gate[:, d, grp:grp + 1], in1=x[:, d, a:z], op0=ALU.mult, op1=ALU.add)
                last.then_inc(x_added, 1)
                if d + SPLIT < KD:
                    split_lo(NC + d + SPLIT)


def router(nc, io, g, layer):
    ps, cst, h, htok, pos, aff = g["ps"], g["cst"], g["h"], g["htok"], g["pos"], g["aff"]
    with stage(nc) as (block, sem, sb):
        rw = sb("router_w", [P, KD, NE])
        logit_rows = sb("logit_rows", [NE, T])
        zero = sb("zero_rows", [P, D])
        mx = sb("aff_max", [P, NT])
        e = sb("aff_exp", [P, NT, NE])
        su = sb("aff_sum", [P, NT])
        rc = sb("aff_rec", [P, NT])
        left = sb("aff_left", [NE, T])
        top = sb("aff_top", [NE, 8])
        chosen = sb("chosen", [NE, T])
        ones = sb("scan_ones", [NE, T])
        cum = sb("chosen_cum", [NE, T])
        slot = sb("slot", [NE, T])
        rw_loaded, rows_done, rows_copied, logits_done, tok_turned, tok_copied, arg_ready, exp_done, aff_ready, aff_turned, slot_ready, slot_turned = (
            sem("router_" + n) for n in ("w_loaded", "rows_done", "rows_copied", "logits_done", "tok_turned", "tok_copied", "arg_ready", "exp_done",
                                         "aff_ready", "aff_turned", "slot_ready", "slot_turned"))
        zero_ready, rows_out = sem("zero_ready"), sem("rows_out")
        chain = Count(sem("router_vector_chain"))

        @block.sync
        def _(sp):
            sp.dma_start(rw[:], layer_row(io["router_w"], layer).rearrange("(k p) n -> p k n", p=P)).then_inc(rw_loaded, 16)
            for u in range(2):
                load_expert(sp, io, g, layer, 0, u // 2, u % 2, u)
            sp.wait_ge(zero_ready, 1)
            for t in range(NT):
                sp.dma_start(io["sum_rows"][t * P:(t + 1) * P, :], zero[:]).then_inc(rows_out, 16)
            for t in range(NT):
                sp.wait_ge(tok_copied, t + 1)
                sp.dma_start(io["tok_rows"][t * P:(t + 1) * P, :], htok[:, t, :]).then_inc(rows_out, 16)
            for u in range(2, EXPERT_RAW[1]):
                load_expert(sp, io, g, layer, 0, u // 2, u % 2, u)
            sp.wait_ge(rows_out, 16 * 2 * NT)

        @block.gpsimd
        def _(pool):
            pool.memset(zero[:], 0.0).then_inc(zero_ready, 1)

        @block.tensor
        def _(pe):
            pe.wait_ge(rw_loaded, 16)
            for a, z, bank in ((0, SAMPLE, 4), (SAMPLE, T, 5)):
                for k in range(KD):
                    last = pe.matmul(ps[0:NE, bank, 0:z - a], rw[:, k, :], h[:, k, a:z], start=(k == 0), stop=(k == KD - 1))
            last.then_inc(rows_done, 1)
            for t in range(NT):
                if t == 1:
                    pe.wait_ge(rows_copied, 1)
                    for tt in range(NT):
                        last = pe.transpose(ps[:, 6, NE * tt:NE * tt + NE], logit_rows[:, tt * P:(tt + 1) * P], cst[0:NE, C_ID:C_ID + NE])
                    last.then_inc(logits_done, 1)
                if t >= 2:
                    pe.wait_ge(tok_copied, t - 1)
                for k in range(KD):
                    last = pe.transpose(ps[:, 2 * (t % 2) + k // 4, (k % 4) * P:(k % 4 + 1) * P],
                                        h[:, k, t * P:(t + 1) * P], cst[:, C_ID:C_ID + P])
                last.then_inc(tok_turned, 1)
                if t == 1:
                    pe.wait_ge(aff_ready, 1)
                    for tt in range(NT):
                        last = pe.transpose(ps[0:NE, 4 + tt // 4, (tt % 4) * P:(tt % 4 + 1) * P], aff[:, tt, 0:NE], cst[:, C_ID:C_ID + P])
                    last.then_inc(aff_turned, 1)
            pe.wait_ge(slot_ready, 1)
            for t in range(NT):
                last = pe.transpose(ps[:, 7, NE * t:NE * t + NE], slot[:, t * P:(t + 1) * P], cst[0:NE, C_ID:C_ID + NE])
            last.then_inc(slot_turned, 1)

        @block.scalar
        def _(act):
            act.wait_ge(arg_ready, 1)
            act.activation(e[:], e[:], ACT.Exp).then_inc(exp_done, 1)
            for t in range(NT):
                act.wait_ge(tok_turned, t + 1)
                act.activation(htok[:, t, :], ps[:, 2 * (t % 2):2 * (t % 2) + 2].rearrange("p a b -> p (a b)"),
                               ACT.Copy).then_inc(tok_copied, 1)

        @block.vector
        def _(v):
            link = lambda ins: chain.link(v, ins)
            logits = ps[:, 6, 0:NT * NE].rearrange("p (a b) -> p a b", a=NT)
            chain.mark(v.memset(ones[:], 1.0))
            v.wait_ge(rows_done, 1)
            v.tensor_copy(logit_rows[:], ps[0:NE, 4:6].rearrange("p a b -> p (a b)")[:, 0:T]).then_inc(rows_copied, 1)
            v.wait_ge(logits_done, 1)
            link(v.tensor_reduce(mx[:], logits, AXX, ALU.max))
            v.tensor_tensor(e[:], logits, mx[:].unsqueeze(2).broadcast_to([P, NT, NE]), ALU.subtract).then_inc(arg_ready, 1)
            v.wait_ge(exp_done, 1)
            link(v.tensor_reduce(su[:], e[:], AXX, ALU.add))
            link(v.reciprocal(rc[:], su[:]))
            v.tensor_tensor(aff[:, :, 0:NE], e[:], rc[:].unsqueeze(2).broadcast_to([P, NT, NE]), ALU.mult).then_inc(aff_ready, 1)
            v.wait_ge(aff_turned, 1)
            link(v.tensor_copy(left[:], ps[0:NE, 4:6].rearrange("p a b -> p (a b)")[:, 0:T]))
            for a, z, cap, off in ((0, SAMPLE, CAP_S, 0.0), (SAMPLE, T, CAP_P, float(CAP_S))):
                for _r in range(cap // 8):
                    link(v.max(out=top[:], in_=left[:, a:z]))
                    link(v.match_replace(out=left[:, a:z], in_to_replace=top[:], in_values=left[:, a:z], imm_value=-1.0))
                link(v.tensor_scalar(chosen[:, a:z], left[:, a:z], 0.0, None, ALU.is_lt))
                link(v.tensor_tensor_scan(cum[:, a:z], ones[:, a:z], chosen[:, a:z], 0.0, ALU.mult, ALU.add))
                link(v.scalar_tensor_tensor(out=slot[:, a:z], in0=cum[:, a:z], scalar=off, in1=chosen[:, a:z],
                                            op0=ALU.add, op1=ALU.mult))
            v.tensor_scalar(slot[:], slot[:], -1.0, None, ALU.add).then_inc(slot_ready, 1)
            v.wait_ge(slot_turned, 1)
            chain.mark(v.tensor_copy(pos[:, :, 0:NE], ps[:, 7, 0:NT * NE].rearrange("p (a b) -> p a b", a=NT)))


class LoopCount:

    def __init__(self, sem, i, per, base=0):
        self.sem, self.i, self.per, self.base, self.n = sem, i, per, base, 0

    def mark(self, ins):
        self.n += 1
        ins.then_inc(self.sem, 1)

    def link(self, eng, ins):
        self.mark(ins)
        eng.wait_ge(self.sem, self.i * self.per + (self.base + self.n))


def choose(nc, io, g):
    ps, cst, htok, pos, aff = g["ps"], g["cst"], g["htok"], g["pos"], g["aff"]
    rows, weight = g["rows"], g["weight"]
    with stage(nc) as (block, sem, sb):
        info = sb("tok_info", [P, NT, NE, 4], F32R)
        pick = sb("pick", [P, 4, NT, SLOTS], F32R)
        info_ready, pick_ready, picked, slots_done = (
            sem("choose_" + n) for n in ("info_ready", "pick_ready", "picked", "slots_done"))

        @block.vector
        def _(v):
            v.tensor_copy(info[:, :, :, 0], cst[:, C_TOK:C_TOK + NT].unsqueeze(2).broadcast_to([P, NT, NE]))
            v.tensor_copy(info[:, :, :, 3], cst[:, C_TOK:C_TOK + NT].unsqueeze(2).broadcast_to([P, NT, NE]))
            v.tensor_copy(info[:, :, :, 1], aff[:, :, 0:NE]).then_inc(info_ready, 1)
            v.wait_ge(info_ready, 1)
            v.tensor_tensor(info[:, :, :, 2], aff[:, :, 0:NE], info[:, :, :, 1].bitcast(F32), ALU.subtract).then_inc(info_ready, 1)
            for e in range(NE):
                if e >= 4:
                    v.wait_ge(picked, e - 3)
                v.tensor_tensor(pick[:, e % 4], cst[:, C_SLOT:C_SLOT + SLOTS].unsqueeze(1).broadcast_to([P, NT, SLOTS]),
                                pos[:, :, e:e + 1].broadcast_to([P, NT, SLOTS]), ALU.is_equal).then_inc(pick_ready, 1)
            v.wait_ge(picked, NE)
            found = ps[0:SLOTS, 0, 0:4 * NE].rearrange("p (a b) -> p a b", b=4)
            v.tensor_copy(rows[:], found[:, :, 0])
            v.tensor_reduce(weight[:], found[:, :, 1:3], AXX, ALU.add).then_inc(slots_done, 1)

        @block.tensor
        def _(pe):
            pe.wait_ge(info_ready, 2)
            for e in range(NE):
                pe.wait_ge(pick_ready, e + 1)
                for t in range(NT):
                    last = pe.matmul(ps[0:SLOTS, 0, 4 * e:4 * e + 4], pick[:, e % 4, t, :], info[:, t, e, :],
                                     start=(t == 0), stop=(t == NT - 1))
                last.then_inc(picked, 1)


def experts(nc, io, g, layer):
    ps, cst, rows, weight = (g[n] for n in ("ps", "cst", "rows", "weight"))
    RAW, SPLIT, KH = EXPERT_RAW[1], 4, KD // 2
    GATE, UP, DOWN = range(3)
    UNITS, LEAD = EXPERT_UNITS, 2
    UP0, NEXT0, DOWN0 = 0, 2, 4
    raw, raw_loaded = g["expert_raw"], g["expert_raw_loaded"]

    def pair(b, rows_, n):
        return ps[0:rows_, b:b + 2].rearrange("p a b -> p (a b)")[:, 0:n]

    def turned(b):
        return ps[:, b:b + 2, 0:4 * SLOTS]

    def part(j, u):
        return UNITS * j + LEAD + u

    def halves(e, u):
        return e * (2 * UNITS) + 2 * (LEAD + u)

    with stage(nc) as (block, sem, sb):
        whi = sb("w_hi", [P, SPLIT, KH, 512], F32R)
        wlo = sb("w_lo", [P, SPLIT, KH, 512], F32R)
        xhi = sb("xe_hi", [P, 2, KD, SLOTS], F32R)
        xlo = sb("xe_lo", [P, 2, KD, SLOTS], F32R)
        hhi = sb("hid_hi", [P, KD, SLOTS], F32R)
        hlo = sb("hid_lo", [P, KD, SLOTS], F32R)
        place = g["h"][0:SLOTS].rearrange("p a b -> p (a b)")
        xe = place[:, 0:2 * D].rearrange("p (a b) -> p a b", a=2)
        ye = place[:, 2 * D:4 * D].rearrange("p (a b) -> p a b", a=2)
        hid = place[:, 4 * D:4 * D + FF]
        xe_loaded, rows_added = g["xe_loaded"], g["rows_added"]
        (split_free, hi_ready, lo_ready, xe_turned, xhi_ready, xlo_ready, gate_tanh, gated, hid_ready,
         hid_turned, hhi_ready, hlo_ready, ye_free, ye_ready) = (
            sem("exp_" + n) for n in (
                "split_free", "hi_ready", "lo_ready", "xe_turned", "xhi_ready", "xlo_ready", "gate_tanh", "gated",
                "hid_ready", "hid_turned", "hhi_ready", "hlo_ready", "ye_free", "ye_ready"))

        def each_pair(eng, body):
            with eng.Fori(0, NE // 2 - 1) as q:
                for j in range(2):
                    body(q * 2 + j, q, j, False, False)
            for j in range(2):
                body(NE - 2 + j, NE // 2 - 1, j, j == 0, j == 1)

        @block.sync
        def _(sp):
            def load(e, matrix, half, slot):
                load_expert(sp, io, g, layer, e, matrix, half, slot)

            def expert(e, q, j, before_last, last_one):
                if last_one:
                    return
                for u in range(UNITS):
                    sp.wait_ge(lo_ready, halves(e, u + 1))
                    slot = part(j, u) % RAW
                    if u < NEXT0:
                        load(e, DOWN, u, slot)
                    elif u < DOWN0:
                        load(e + 1, UP, u - NEXT0, slot)
                    elif before_last:
                        load(e + 1, DOWN, u - DOWN0, slot)
                    else:
                        load(e + 2, GATE, u - DOWN0, slot)

            for u in range(LEAD):
                sp.wait_ge(lo_ready, 2 * (u + 1))
                load(1, GATE, u, u)
            each_pair(sp, expert)

        @block.gpsimd
        def _(pool):
            def gather(e):
                pool.indirect_dma_start(out=xe[:, e % 2, :], out_offset=None, in_=io["tok_rows"],
                                        in_offset=bass.IndirectOffsetOnAxis(rows[:, e:e + 1], 0)).then_inc(xe_loaded[e % 2], 16)

            pool.sem_inc(ye_free, 2)
            gather(0)
            gather(1)
            for e in range(NE):
                if e + 2 < NE:
                    pool.wait_ge(xe_turned, e + 1)
                    gather(e + 2)
                pool.wait_ge(ye_ready, e + 2)
                pool.indirect_dma_start(out=io["sum_rows"], out_offset=bass.IndirectOffsetOnAxis(rows[:, e:e + 1], 0),
                                        in_=ye[:, e % 2, :], in_offset=None, compute_op=ALU.add).then_inc(rows_added, 16)
                pool.wait_ge(rows_added, layer * (16 * NE) + 16 * (e + 1))
                pool.sem_inc(ye_free, 1)

        @block.tensor
        def _(pe):
            def turn_tokens(q, j):
                pe.wait_ge(xe_loaded[j], layer * (8 * NE) + (q * 16 + 16))
                for k in range(KD):
                    last = pe.transpose(ps[:, 4 + k // 4, (k % 4) * SLOTS:(k % 4 + 1) * SLOTS], xe[:, j, k * P:(k + 1) * P],
                                        cst[0:SLOTS, C_ID:C_ID + SLOTS])
                last.then_inc(xe_turned, 1)

            def unit(e, j, u, bank, hi, lo):
                for kh in range(2):
                    s = (2 * part(j, u) + kh) % SPLIT
                    pe.wait_ge(lo_ready, halves(e, u) + (kh + 1))
                    for k in range(KH * kh, KH * kh + KH):
                        w = k % KH
                        pe.matmul(ps[0:SLOTS, bank, :], hi[:, k, :], whi[:, s, w, :], start=(k == 0), stop=False)
                        pe.matmul(ps[0:SLOTS, bank, :], hi[:, k, :], wlo[:, s, w, :], start=False, stop=False)
                        last = pe.matmul(ps[0:SLOTS, bank, :], lo[:, k, :], whi[:, s, w, :], start=False, stop=(k == KD - 1))
                    last.then_inc(split_free, 1)

            def turn_hidden(e):
                pe.wait_ge(hid_ready, e + 1)
                pe.wait_ge(ye_ready, e + 1)
                for k in range(KD):
                    last = pe.transpose(ps[:, 6 + k // 4, (k % 4) * SLOTS:(k % 4 + 1) * SLOTS], hid[:, k * P:(k + 1) * P],
                                        cst[0:SLOTS, C_ID:C_ID + SLOTS])
                last.then_inc(hid_turned, 1)

            def expert(e, q, j, before_last, last_one):
                for i in range(2):
                    unit(e, j, UP0 + i, 2 + i, xhi[:, j], xlo[:, j])
                if last_one:
                    turn_hidden(e)
                else:
                    pe.wait_ge(xlo_ready, e + 2)
                    pe.wait_ge(gated, e + 1)
                    unit(e, j, NEXT0, 0, xhi[:, 1 - j], xlo[:, 1 - j])
                    turn_hidden(e)
                    unit(e, j, NEXT0 + 1, 1, xhi[:, 1 - j], xlo[:, 1 - j])
                pe.wait_ge(hlo_ready, e + 1)
                for i in range(2):
                    unit(e, j, (NEXT0 if last_one else DOWN0) + i, 6 + i, hhi, hlo)
                if not (before_last or last_one):
                    turn_tokens(q + 1, j)

            pe.sem_inc(split_free, SPLIT)
            turn_tokens(0, 0)
            pe.wait_ge(xlo_ready, 1)
            for i in range(LEAD):
                unit(0, 0, i - LEAD, i, xhi[:, 0], xlo[:, 0])
            turn_tokens(0, 1)
            each_pair(pe, expert)

        @block.scalar
        def _(act):
            def split_hi(e, q, j, u):
                i = part(j, u)
                act.wait_ge(raw_loaded[i % RAW], layer * (16 * NE * UNITS // RAW) + (q * (16 * 2 * UNITS // RAW) + 16 * (i // RAW + 1)))
                for kh in range(2):
                    act.wait_ge(split_free, halves(e, u) + (kh + 1))
                    act.activation(whi[:, (2 * i + kh) % SPLIT], raw[:, i % RAW, KH * kh:KH * kh + KH], ACT.Copy).then_inc(hi_ready, 1)

            def tokens_hi(nth, j):
                act.wait_ge(xe_turned, nth)
                act.activation(xhi[:, j].rearrange("p (a b) c -> p a (b c)", a=2), turned(4), ACT.Copy).then_inc(xhi_ready, 1)

            def gate(multiplied):
                act.wait_ge(split_free, multiplied + SPLIT)
                act.activation(hid, pair(0, SLOTS, FF), ACT.Tanh, scale=0.5).then_inc(gate_tanh, 1)

            def expert(e, q, j, before_last, last_one):
                if not last_one:
                    split_hi(e, q, j, NEXT0)
                    split_hi(e, q, j, NEXT0 + 1)
                    split_hi(e, q, j, DOWN0)
                act.wait_ge(hid_turned, e + 1)
                act.activation(hhi[:].rearrange("p (a b) c -> p a (b c)", a=2), turned(6), ACT.Copy).then_inc(hhi_ready, 1)
                if not last_one:
                    split_hi(e, q, j, DOWN0 + 1)
                    gate(halves(e, DOWN0))
                    split_hi(e, q, j, UNITS)
                    split_hi(e, q, j, UNITS + 1)
                    if before_last:
                        split_hi(e, q, j, UNITS + 2)
                        split_hi(e, q, j, UNITS + 3)
                act.wait_ge(split_free, halves(e, DOWN0 if last_one else UNITS) + SPLIT)
                act.wait_ge(ye_free, e + 1)
                act.activation(ye[:, j, :], pair(6, SLOTS, D), ACT.Copy, scale=weight[:, bass.ds(e, 1)] if not isinstance(e, int)
                               else weight[:, e:e + 1]).then_inc(ye_ready, 1)
                if not (before_last or last_one):
                    tokens_hi(e + 3, j)

            act.sem_inc(ye_ready, 1)
            for u in range(-LEAD, 0):
                split_hi(0, 0, 0, u)
            tokens_hi(1, 0)
            split_hi(0, 0, 0, UP0)
            split_hi(0, 0, 0, UP0 + 1)
            gate(2 * LEAD)
            tokens_hi(2, 1)
            each_pair(act, expert)

        @block.vector
        def _(v):
            def split_lo(e, j, u):
                i = part(j, u)
                for kh in range(2):
                    s = (2 * i + kh) % SPLIT
                    v.wait_ge(hi_ready, halves(e, u) + (kh + 1))
                    v.tensor_tensor(wlo[:, s], raw[:, i % RAW, KH * kh:KH * kh + KH], whi[:, s].bitcast(F32),
                                    ALU.subtract).then_inc(lo_ready, 1)

            def tokens_lo(nth, j):
                v.wait_ge(xhi_ready, nth)
                v.tensor_tensor(xlo[:, j].rearrange("p (a b) c -> p a (b c)", a=2), turned(4),
                                xhi[:, j].bitcast(F32).rearrange("p (a b) c -> p a (b c)", a=2), ALU.subtract).then_inc(xlo_ready, 1)

            def gate(nth):
                v.wait_ge(gate_tanh, nth)
                v.scalar_tensor_tensor(out=hid, in0=hid, scalar=1.0, in1=pair(0, SLOTS, FF), op0=ALU.add, op1=ALU.mult).then_inc(gated, 1)

            def expert(e, q, j, before_last, last_one):
                if not last_one:
                    split_lo(e, j, NEXT0)
                v.wait_ge(split_free, halves(e, NEXT0) + SPLIT)
                v.wait_ge(gated, e + 1)
                v.scalar_tensor_tensor(out=hid, in0=hid, scalar=0.5, in1=pair(2, SLOTS, FF),
                                       op0=ALU.mult, op1=ALU.mult).then_inc(hid_ready, 1)
                if not last_one:
                    split_lo(e, j, NEXT0 + 1)
                    split_lo(e, j, DOWN0)
                v.wait_ge(hhi_ready, e + 1)
                v.tensor_tensor(hlo[:].rearrange("p (a b) c -> p a (b c)", a=2), turned(6),
                                hhi[:].bitcast(F32).rearrange("p (a b) c -> p a (b c)", a=2), ALU.subtract).then_inc(hlo_ready, 1)
                if not last_one:
                    split_lo(e, j, DOWN0 + 1)
                    gate(e + 2)
                    split_lo(e, j, UNITS)
                    split_lo(e, j, UNITS + 1)
                    if before_last:
                        split_lo(e, j, UNITS + 2)
                        split_lo(e, j, UNITS + 3)
                    else:
                        tokens_lo(e + 3, j)

            for u in range(-LEAD, 0):
                split_lo(0, 0, u)
            tokens_lo(1, 0)
            split_lo(0, 0, UP0)
            split_lo(0, 0, UP0 + 1)
            gate(1)
            tokens_lo(2, 1)
            each_pair(v, expert)


def add_experts(nc, io, g, layer):
    ps, cst, x, mod = g["ps"], g["cst"], g["x"], g["mod"]
    with stage(nc) as (block, sem, sb):
        sb("mod_raw_end", MOD_RAW)
        tok = sb("sum_tok", [P, NT, D])
        loaded = [sem(f"sum_loaded{t}") for t in range(NT)]
        tok_turned, x_added = sem("sum_turned"), sem("sum_added")

        @block.sync
        def _(sp):
            for t in range(NT):
                sp.dma_start(tok[:, t, :], io["sum_rows"][t * P:(t + 1) * P, :]).then_inc(loaded[t], 16)
            for n in range(MOD_RAW[1]):
                load_mod(sp, io, g, (layer + 1) % DEPTH, n)

        @block.tensor
        def _(pe):
            for t in range(NT):
                pe.wait_ge(loaded[t], 16)
                if t >= 4:
                    pe.wait_ge(x_added, t - 3)
                for k in range(KD):
                    last = pe.transpose(ps[:, 2 * (t % 4) + k // 4, (k % 4) * P:(k % 4 + 1) * P],
                                        tok[:, t, k * P:(k + 1) * P], cst[:, C_ID:C_ID + P])
                last.then_inc(tok_turned, 1)

        @block.vector
        def _(v):
            for t in range(NT):
                grp = int(t == NT - 1)
                v.wait_ge(tok_turned, t + 1)
                for k in range(KD):
                    dst = x[:, k, t * P:(t + 1) * P]
                    last = v.scalar_tensor_tensor(out=dst, in0=ps[:, 2 * (t % 4) + k // 4, (k % 4) * P:(k % 4 + 1) * P],
                                                  scalar=mod[:, 40 + k, grp:grp + 1], in1=dst, op0=ALU.mult, op1=ALU.add)
                last.then_inc(x_added, 1)


def finish(nc, io, g):
    def wait_mod(sp):
        for n in range(MOD_RAW[1]):
            sp.wait_ge(g["mod_raw_loaded"][n], 16 * (DEPTH * 3 + 1))

    norm(nc, g, "nf", g["fin"], None, fetch=wait_mod, store=io["y"])


def constants():
    c = np.zeros((P, C_END), np.float32)
    i, j = np.arange(P)[:, None], np.arange(P)[None, :]
    c[:, C_ID:C_ID + P] = i == j
    c[:, C_LE:C_LE + P] = i <= j
    c[:, C_GE:C_GE + P] = i >= j
    c[:, C_ROT:C_ROT + P] = np.where((i == j + 1) & (j % 2 == 0), -1.0, 0.0) + np.where((i == j - 1) & (j % 2 == 1), 1.0, 0.0)
    c[:, C_BLK:C_BLK + P] = i // 64 == j // 64
    c[:, C_ONE:C_ONE + P] = 1.0
    c[:, C_SLOT:C_SLOT + SLOTS] = np.arange(SLOTS)
    col, kc = np.arange(P)[:, None] % GRID_W, np.arange(GRID_W)[None, :]
    start = np.clip(col - 8, 0, GRID_W - 16)
    c[:, C_WIN:C_WIN + GRID_W] = np.where((kc >= start) & (kc < start + 16), 0.0, -1e30)
    quarter = ROPE // 4
    inv = (10000.0 ** (-np.arange(quarter, dtype=np.float32) / quarter)).astype(np.float32)
    f = (np.arange(P) % ROPE) // 2
    tok = np.arange(SAMPLE)
    at = np.where(f[:, None] < quarter, (tok // GRID_W)[None, :], (tok % GRID_W)[None, :]).astype(np.float32)
    angle = at * inv[f % quarter][:, None]
    c[:, C_COS:C_COS + SAMPLE] = np.cos(angle)
    c[:, C_SIN:C_SIN + SAMPLE] = np.sin(angle)
    c[:, C_PAIR:C_PAIR + 2] = i % 2 == j[:, 0:2]
    c[:, C_TOK:C_TOK + NT] = np.arange(NT)[None, :] * P + np.arange(P)[:, None]
    return c


def lay_out(a):
    L = DEPTH

    def feat(x, chunks):
        return x.reshape(x.shape[0], chunks, P).transpose(2, 1, 0)

    def cols(x):
        return x.reshape(L, -1, P).transpose(0, 2, 1)

    def everywhere(x):
        x = x.reshape(L, 1, -1)
        return np.broadcast_to(x, (L, P, x.shape[2]))

    o = {"cst": constants()}
    o["x"] = feat(np.concatenate([a["x_sample"][0], a["x_prompt"][0]]), KD)
    o["cond"] = feat(np.stack([a["c"][0], a["c_ctx"]]), KD)
    o["fin"] = a["final_norm_g"].reshape(KD, P).T
    lam_init = np.array([[0.8 - 0.6 * math.exp(-0.3 * i), 1.0 - (0.8 - 0.6 * math.exp(-0.3 * i))] for i in range(L)], np.float32)
    cw = a["ssm_conv_w"].reshape(L, 3, 4, P).transpose(0, 3, 1, 2).reshape(L, P, 12)
    o["vec"] = np.concatenate([
        cols(a["mod_b"]), cols(a["norm1_g"]), cols(a["norm2_g"]), cols(a["mla_q_norm_g"]), cols(a["mla_kv_norm_g"]),
        np.tile(a["df_subln_g"], (1, 2))[:, :, None], cw, cols(a["ssm_conv_b"]), everywhere(a["ssm_dt_bias"]),
        everywhere(a["ssm_a_log"]), cols(np.repeat(a["ssm_d"], 64, axis=1)), cols(a["ssm_norm_g"]),
        everywhere(a["df_lambda"]), everywhere(lam_init)], axis=2)
    w = a["w_in"]
    part = lambda first, n: w[:, :, first:first + n]
    o["w_mix"] = np.concatenate([part(O_NAQ, 256), part(O_NAK, 256), part(O_CQ, QR), part(O_CKV, KVR)]
                                + [part(O_KR, ROPE)] * 4
                                + [part(O_DFQ, 256), part(O_DFK, 256), part(O_SX, 256), part(O_SB, P), part(O_SC, P),
                                   part(O_SZ, 256), part(O_NAV, 256), part(O_DFV, 256), part(O_DT, 8)], axis=2)
    uq = a["mla_w_uq"].reshape(L, QR, HEADS, 96)
    o["w_uq"] = np.concatenate([uq[..., :64].reshape(L, QR, 256), uq[..., 64:].reshape(L, QR, 128)], axis=2)
    ukv = a["mla_w_ukv"].reshape(L, KVR, HEADS, 128)
    o["w_ukv"] = np.concatenate([ukv[..., :64].reshape(L, KVR, 256), ukv[..., 64:].reshape(L, KVR, 256)], axis=2)
    rows = []
    for i in range(L):
        rows.append(np.concatenate([
            feat(a["cache_na_k"][0, i].reshape(CTX, 256), 2), feat(a["cache_df_k"][0, i].reshape(CTX, 256), 2),
            feat(a["cache_mla_ckv"][0, i], 2), feat(np.tile(a["cache_mla_krope"][0, i], (1, 4)), 1)], axis=1))
    o["ctx_k"] = np.stack(rows)
    o["ctx_v"] = np.concatenate([a["cache_na_v"][0].reshape(L, CTX, 256), a["cache_df_v"][0].reshape(L, CTX, 256)], axis=2)
    o["state"] = a["state_ssm"][0].reshape(L, 2, 2, 2, 64, 64).transpose(0, 2, 5, 1, 3, 4).reshape(L, P, 2, 2, 64)
    rel = np.zeros((L, HEADS, 17, 2 * GRID_W), a["na_rel_bias"].dtype)
    rel[:, :, 1:16, BIAS_MID - 15:BIAS_MID + 16] = a["na_rel_bias"]
    bias = np.zeros((L, P, HEADS, 16, GRID_W), rel.dtype)
    for c in range(GRID_W):
        bias[:, c] = rel[:, :, 1:17, BIAS_MID - c:BIAS_MID - c + GRID_W]
        bias[:, GRID_W + c] = rel[:, :, 0:16, BIAS_MID - c:BIAS_MID - c + GRID_W]
    o["bias"] = bias
    for n in ("mod_w", "w_in", "w_out", "w_branch", "router_w", "exp_w_gate", "exp_w_up", "exp_w_down"):
        o[n] = a[n]
    return {n: np.ascontiguousarray(v) for n, v in o.items()}


OUTS = {"y": (P, KD, T), "new_k": (DEPTH, P, K_N, PROMPT), "new_v": (DEPTH, PROMPT, 512), "new_state": (DEPTH, P, 2, 2, 64)}


def collect(r):
    y, nk, nv, ns = (np.asarray(r[f"out_{n}"]) for n in OUTS)
    L = DEPTH
    y = y.transpose(2, 1, 0).reshape(T, D)

    def keys(first, n):
        return nk[:, :, first:first + n].transpose(0, 3, 2, 1).reshape(1, L, PROMPT, n * P)

    state = ns.reshape(L, 2, 64, 2, 2, 64).transpose(0, 3, 1, 4, 5, 2).reshape(1, L, 2, HEADS, 64, 64)
    return (y[None, SAMPLE:], y[None, :SAMPLE], keys(K_NA, 2).reshape(1, L, PROMPT, HEADS, 64),
            nv[:, :, :256].reshape(1, L, PROMPT, HEADS, 64), keys(K_CKV, 2), keys(K_KR, 1)[..., :ROPE],
            keys(K_DF, 2).reshape(1, L, PROMPT, HEADS, 2, 32), nv[:, :, 256:].reshape(1, L, PROMPT, HEADS, 64), state)


def kernel(**inputs):
    import concourse.bacc as bacc
    from concourse.bass_utils import run_bass_kernel_spmd

    arrays = lay_out({n: np.asarray(v) for n, v in inputs.items()})
    nc = bacc.Bacc("TRN2", target_bir_lowering=False, num_devices=1)
    io = {n: nc.dram_tensor(f"in_{n}", a.shape, mybir.dt.from_np(a.dtype), kind="ExternalInput").ap() for n, a in arrays.items()}
    for n, shape in OUTS.items():
        io[n] = nc.dram_tensor(f"out_{n}", shape, F32, kind="ExternalOutput").ap()
    for n in ("tok_rows", "sum_rows"):
        io[n] = nc.dram_tensor(n, (T, D), F32).ap()
    build(nc, io)
    r = run_bass_kernel_spmd(nc, [{f"in_{n}": a for n, a in arrays.items()}], core_ids=[0])
    return tuple(np.ascontiguousarray(v) for v in collect(r.results[0]))
```
